# Optimizing a Trainium2 kernel written in Bass

```python
import jax, jax.numpy as jnp
from jax import lax
import numpy as np

D_MODEL = 1024
BATCH = 1
SEQ = 256
DEPTH = 2

N_A_LAYERS = DEPTH // 2
N_B_LAYERS = DEPTH - N_A_LAYERS
N_DENSE = (DEPTH + 1) // 2
N_MOE = DEPTH // 2

HG_HEADS = 8
HG_KEY_DIM = 128
HG_VAL_DIM = D_MODEL // HG_HEADS
HG_Q = HG_HEADS * HG_KEY_DIM
HG_V = HG_HEADS * HG_VAL_DIM
HG_CHUNK = 64
LB_FLOOR = 1e-30

FOX_HEADS = 16
FOX_HEAD_DIM = 64
FOX_DIM = FOX_HEADS * FOX_HEAD_DIM
Q_BLOCK = 128
FGATE_BIAS_MEAN = 3.0
MASK_VALUE = -1e30

FFN_DIM = 2816
N_EXPERTS = 8
TOP_K = 2
EXPERT_DIM = 3584

ALPHA = (2 * DEPTH) ** 0.25
BETA = (8 * DEPTH) ** -0.25
LN_EPS = 1e-5
RMS_EPS = 1e-6

kernel_name = "yoco_hgrn2_fox_moe_deepnorm"

def layer_norm(x, g, b):
    xf = x.astype(jnp.float32)
    mu = jnp.mean(xf, axis=-1, keepdims=True)
    var = jnp.mean(jnp.square(xf - mu), axis=-1, keepdims=True)
    y = (xf - mu) * lax.rsqrt(var + LN_EPS) * g.astype(jnp.float32) + b.astype(jnp.float32)
    return y.astype(x.dtype)

def deepnorm_residual(x, y, g, b):
    return layer_norm(ALPHA * x + y, g, b)

def hgrn2_lower_bounds(lb_logits):
    p = jax.nn.softmax(lb_logits.astype(jnp.float32), axis=0)
    return jnp.cumsum(p, axis=0) - p[0]

def hgrn2_mixer(x, w_in, lb, norm_w, w_out):
    bsz, s, _ = x.shape
    proj = x @ w_in
    q, f, i, g = jnp.split(proj, [HG_Q, 2 * HG_Q, 2 * HG_Q + HG_V], axis=-1)
    z = f.astype(jnp.float32)
    log_lb = jnp.log(jnp.maximum(lb, LB_FLOOR))
    log_f = jnp.logaddexp(jax.nn.log_sigmoid(z), log_lb + jax.nn.log_sigmoid(-z))
    k = (1.0 - lb) * jax.nn.sigmoid(-z)
    q = jax.nn.silu(q.astype(jnp.float32))
    v = i.astype(jnp.float32)
    n_chunks = s // HG_CHUNK

    def to_chunks(t, d):
        return t.reshape(bsz, n_chunks, HG_CHUNK, HG_HEADS, d).transpose(1, 0, 3, 2, 4)

    qc, kc, vc, gc = (to_chunks(q, HG_KEY_DIM), to_chunks(k, HG_KEY_DIM),
                      to_chunks(v, HG_VAL_DIM), to_chunks(log_f, HG_KEY_DIM))
    causal = jnp.tril(jnp.ones((HG_CHUNK, HG_CHUNK), dtype=bool))[:, :, None]

    def chunk_step(state, inp):
        q_c, k_c, v_c, g_c = inp
        b = jnp.cumsum(g_c, axis=2)
        o_inter = jnp.einsum('bhtd,bhde->bhte', q_c * jnp.exp(b), state)
        diff = b[:, :, :, None, :] - b[:, :, None, :, :]
        decay = jnp.where(causal, jnp.exp(jnp.where(causal, diff, 0.0)), 0.0)
        scores = jnp.einsum('bhtsd,bhsd->bhts', q_c[:, :, :, None, :] * decay, k_c)
        o_intra = jnp.einsum('bhts,bhse->bhte', scores, v_c)
        b_last = b[:, :, -1:, :]
        new_state = (jnp.exp(b_last[:, :, 0, :])[..., None] * state
                     + jnp.einsum('bhsd,bhse->bhde', k_c * jnp.exp(b_last - b), v_c))
        return new_state, o_inter + o_intra

    state0 = jnp.zeros((bsz, HG_HEADS, HG_KEY_DIM, HG_VAL_DIM), jnp.float32)
    _, o = lax.scan(chunk_step, state0, (qc, kc, vc, gc))
    o = o.transpose(1, 0, 3, 2, 4).reshape(bsz, s, HG_HEADS, HG_VAL_DIM)
    o = o * lax.rsqrt(jnp.mean(jnp.square(o), axis=-1, keepdims=True) + RMS_EPS)
    o = o * norm_w.astype(jnp.float32) * jax.nn.silu(g.astype(jnp.float32)).reshape(bsz, s, HG_HEADS, HG_VAL_DIM)
    return o.reshape(bsz, s, HG_V).astype(x.dtype) @ w_out

def shared_kv(x, w_kv, b_f):
    bsz, s, _ = x.shape
    kv = x @ w_kv
    k, v, f = jnp.split(kv, [FOX_DIM, 2 * FOX_DIM], axis=-1)
    k = k.reshape(bsz, s, FOX_HEADS, FOX_HEAD_DIM).transpose(0, 2, 1, 3)
    v = v.reshape(bsz, s, FOX_HEADS, FOX_HEAD_DIM).transpose(0, 2, 1, 3)
    log_f = jax.nn.log_sigmoid(f.astype(jnp.float32) + b_f.astype(jnp.float32))
    cum_log_f = jnp.cumsum(log_f, axis=1).transpose(0, 2, 1)
    return k, v, cum_log_f

def fox_mixer(x, w_qg, k, v, cum_log_f, w_out):
    bsz, s, _ = x.shape
    q, gate = jnp.split(x @ w_qg, [FOX_DIM], axis=-1)
    q = q.reshape(bsz, s, FOX_HEADS, FOX_HEAD_DIM).transpose(0, 2, 1, 3)
    scale = FOX_HEAD_DIM ** -0.5
    outs = []
    for blk in range(s // Q_BLOCK):
        qs, qe = blk * Q_BLOCK, (blk + 1) * Q_BLOCK
        logits = jnp.einsum('bhqd,bhkd->bhqk', q[:, :, qs:qe], k[:, :, :qe]).astype(jnp.float32) * scale
        logits = logits + cum_log_f[:, :, qs:qe, None] - cum_log_f[:, :, None, :qe]
        mask = jnp.arange(qe)[None, :] <= (qs + jnp.arange(Q_BLOCK))[:, None]
        probs = jax.nn.softmax(jnp.where(mask, logits, MASK_VALUE), axis=-1)
        outs.append(jnp.einsum('bhqk,bhkd->bhqd', probs.astype(v.dtype), v[:, :, :qe]))
    o = jnp.concatenate(outs, axis=2).transpose(0, 2, 1, 3).reshape(bsz, s, FOX_DIM)
    return (o * jax.nn.sigmoid(gate)) @ w_out

def swiglu(x, w_gu, w_down):
    a, b = jnp.split(x @ w_gu, 2, axis=-1)
    return (jax.nn.silu(a) * b) @ w_down

def moe_swiglu(x, w_router, w_gu, w_down):
    bsz, s, d = x.shape
    xf = x.reshape(-1, d)
    logits = (xf @ w_router).astype(jnp.float32)
    top_vals, top_idx = lax.top_k(logits, TOP_K)
    top_w = jax.nn.softmax(top_vals, axis=-1)
    combine = jnp.sum(jax.nn.one_hot(top_idx, N_EXPERTS, dtype=jnp.float32) * top_w[..., None], axis=1)
    y = jnp.zeros(xf.shape, jnp.float32)
    for e in range(N_EXPERTS):
        y = y + combine[:, e:e + 1] * swiglu(xf, w_gu[e], w_down[e]).astype(jnp.float32)
    return y.astype(x.dtype).reshape(bsz, s, d)

def setup_inputs(seed: int = 0) -> dict:
    key = jax.random.key(seed)
    ks = jax.random.split(key, 20)

    def nrm(k, shape, scale):
        return jax.random.normal(k, shape, jnp.float32) * scale

    hg_col_scale = jnp.concatenate([jnp.ones((2 * HG_Q,), jnp.float32), jnp.full((HG_V,), BETA, jnp.float32),
                                    jnp.ones((HG_V,), jnp.float32)])
    kv_col_scale = jnp.concatenate([jnp.ones((FOX_DIM,), jnp.float32), jnp.full((FOX_DIM,), BETA, jnp.float32),
                                    jnp.ones((FOX_HEADS,), jnp.float32)])
    return {
        "x": nrm(ks[0], (BATCH, SEQ, D_MODEL), 1.0),
        "hg_w_in": nrm(ks[1], (N_A_LAYERS, D_MODEL, 2 * HG_Q + 2 * HG_V), D_MODEL ** -0.5) * hg_col_scale,
        "hg_lb_logits": 1.0 + nrm(ks[2], (N_A_LAYERS, HG_Q), 0.1),
        "hg_norm_w": 1.0 + nrm(ks[3], (N_A_LAYERS, HG_VAL_DIM), 0.1),
        "hg_w_out": nrm(ks[4], (N_A_LAYERS, HG_V, D_MODEL), HG_V ** -0.5 * BETA),
        "kv_w": nrm(ks[5], (D_MODEL, 2 * FOX_DIM + FOX_HEADS), D_MODEL ** -0.5) * kv_col_scale,
        "kv_fgate_b": FGATE_BIAS_MEAN + nrm(ks[6], (FOX_HEADS,), 0.5),
        "fox_w_qg": nrm(ks[7], (N_B_LAYERS, D_MODEL, 2 * FOX_DIM), D_MODEL ** -0.5),
        "fox_w_out": nrm(ks[8], (N_B_LAYERS, FOX_DIM, D_MODEL), FOX_DIM ** -0.5 * BETA),
        "ln_mix_g": 1.0 + nrm(ks[9], (DEPTH, D_MODEL), 0.05),
        "ln_mix_b": nrm(ks[10], (DEPTH, D_MODEL), 0.02),
        "ln_ffn_g": 1.0 + nrm(ks[11], (DEPTH, D_MODEL), 0.05),
        "ln_ffn_b": nrm(ks[12], (DEPTH, D_MODEL), 0.02),
        "ffn_w_gu": nrm(ks[13], (N_DENSE, D_MODEL, 2 * FFN_DIM), D_MODEL ** -0.5),
        "ffn_w_down": nrm(ks[14], (N_DENSE, FFN_DIM, D_MODEL), FFN_DIM ** -0.5 * BETA),
        "moe_w_router": nrm(ks[15], (N_MOE, D_MODEL, N_EXPERTS), D_MODEL ** -0.5),
        "moe_w_gu": nrm(ks[16], (N_MOE, N_EXPERTS, D_MODEL, 2 * EXPERT_DIM), D_MODEL ** -0.5),
        "moe_w_down": nrm(ks[17], (N_MOE, N_EXPERTS, EXPERT_DIM, D_MODEL), EXPERT_DIM ** -0.5 * BETA),
    }

def reference(x, hg_w_in, hg_lb_logits, hg_norm_w, hg_w_out, kv_w, kv_fgate_b, fox_w_qg, fox_w_out,
              ln_mix_g, ln_mix_b, ln_ffn_g, ln_ffn_b, ffn_w_gu, ffn_w_down,
              moe_w_router, moe_w_gu, moe_w_down):
    lbs = hgrn2_lower_bounds(hg_lb_logits)
    k_sh = v_sh = c_sh = None
    for layer in range(DEPTH):
        if layer < N_A_LAYERS:
            a = layer
            y = hgrn2_mixer(x, hg_w_in[a], lbs[a], hg_norm_w[a], hg_w_out[a])
        else:
            bi = layer - N_A_LAYERS
            y = fox_mixer(x, fox_w_qg[bi], k_sh, v_sh, c_sh, fox_w_out[bi])
        x = deepnorm_residual(x, y, ln_mix_g[layer], ln_mix_b[layer])
        if layer % 2 == 0:
            y = swiglu(x, ffn_w_gu[layer // 2], ffn_w_down[layer // 2])
        else:
            y = moe_swiglu(x, moe_w_router[layer // 2], moe_w_gu[layer // 2], moe_w_down[layer // 2])
        x = deepnorm_residual(x, y, ln_ffn_g[layer], ln_ffn_b[layer])
        if layer == N_A_LAYERS - 1:
            k_sh, v_sh, c_sh = shared_kv(x, kv_w, kv_fgate_b)
    return x


_drawn_inputs = setup_inputs


def setup_inputs(seed=0):
    import zlib

    import numpy as np

    out = dict(_drawn_inputs(seed))
    spreads = {}
    factors = {'kv_fgate_b': 36.552, 'fox_w_qg': 2.963}
    for name, (base, spread) in spreads.items():
        noise = np.random.default_rng([zlib.crc32(name.encode()), seed]).standard_normal(out[name].shape)
        drawn = base * np.exp(spread * noise) if base else spread * noise
        out[name] = __import__('jax').numpy.asarray(drawn.astype(out[name].dtype))
    for name, factor in factors.items():
        out[name] = (out[name] * factor).astype(out[name].dtype)
    return out
```

```python
from contextlib import ExitStack

import concourse.bass as bass
from concourse import mybir

F32 = mybir.dt.float32
I32 = mybir.dt.int32
U8 = mybir.dt.uint8
ALU = mybir.AluOpType
ACT = mybir.ActivationFunctionType
AX_X = mybir.AxisListType.X

P = 128
D = 1024
T = 256
TB = T // P
KT = D // P
N = 512
HG_HEADS = 8
FOX_HEADS = 16
FOX_DIM = 64
FFN = 2816
FFN_TILES = FFN // P
E = 8
F = 3584
CH = F // N
FT = N // P
ALPHA = 4 ** 0.25
LN_EPS = 1e-5
RMS_EPS = 1e-6
LB_FLOOR = 1e-30
LN_SHIFT = 50
LN2 = 0.6931471805599453
MASKED = -1e30
NOT_CHOSEN = 1e6

RING = 7
SLOT = KT * N
HG_SLOTS = 8
S_HG_OUT = HG_SLOTS
S_GU = S_HG_OUT + 2
FFN_CH = 11
S_DOWN = S_GU + FFN_CH
DOWN_SLOTS = 6
S_KVQG = S_DOWN + DOWN_SLOTS
S_FOX_OUT = S_KVQG + 8
S_MOE = S_FOX_OUT + 2
MOE_SLOTS = 3 * CH
assert MOE_SLOTS % RING == 0
MOE_ORDER = [("a", 0), ("b", 0)]
for _c in range(1, CH):
    MOE_ORDER += [("a", _c), ("b", _c), ("d", _c - 1)]
MOE_ORDER += [("d", CH - 1)]

HALVES = [64, 32, 16, 8, 4, 2, 1]
LEVELS = len(HALVES) + 1
BUF_LEVELS = len(HALVES) + 1


class Steps:

    def __init__(self, eng, sem, start=0):
        self.eng, self.sem, self.n = eng, sem, start

    def __call__(self, ins):
        ins.then_inc(self.sem, 1)
        self.n += 1
        self.eng.wait_ge(self.sem, self.n)

    def note(self, ins):
        ins.then_inc(self.sem, 1)
        self.n += 1


def build(nc, x, w_in, lb_logits, norm_w, w_out, kv_w, fgate_b, fox_qg, fox_out, ln_mix_g, ln_mix_b,
          ln_ffn_g, ln_ffn_b, ffn_gu, ffn_down, router_w, moe_gu, moe_down,
          c_square, c_levels, c_negsel, c_causal, c_route, out):
    with ExitStack() as ctx:
        def sb(name, shape, dt=F32):
            return ctx.enter_context(nc.sbuf_tensor(name, shape, dt))

        def sem(name):
            return ctx.enter_context(nc.semaphore(name))

        ring = sb("ring", [P, RING, SLOT])
        xres = sb("xres", [P, TB, D])
        xT = sb("xT", [P, KT, T])
        gb = sb("gb", [P, 2, D])
        sq = sb("sq", [P, 2 * P])
        level_mask = sb("level_mask", [P, LEVELS, P], U8)
        A = sb("A", [P, 17408])
        sm = sb("sm", [P, 96])
        fgb = sb("fgb", [FOX_HEADS, 1])
        itf = sb("itf", [1, 40])
        items = sb("items", [1, 17], I32)

        ident = sq[:, 0:P]
        ones = sq[:, P:2 * P]
        ps = ctx.enter_context(nc.psum_tensor("ps", [P, 8, N], F32))

        def bank(n, cols=N):
            return ps[:, n, 0:cols]

        zb = A[:, 0:2048]
        hq = A[:, 2048:4096]
        hk = A[:, 4096:6144]
        hv = A[:, 6144:8192].rearrange("p (t n) -> p t n", t=TB)
        hg = A[:, 8192:10240].rearrange("p (t n) -> p t n", t=TB)
        ph_l, ph_a = A[:, 8192:9216], A[:, 9216:10240]
        lev_e = [A[:, 10240:11264], A[:, 11264:12288]]
        lev_q = [A[:, 12288:13312], A[:, 13312:14336]]
        lev_k = [A[:, 14336:15360], A[:, 15360:16384]]
        scT = A[:, 16384:17408]
        khatT = lev_k[0][:, 0:N]
        state = lev_q[0][:, 0:N]
        ho = gb
        lbt = sm[:, 0:8]
        one_m_lb = sm[:, 8:16]
        loglb = sm[:, 16:24]
        nloglb = sm[:, 24:32]
        ssq = sm[:, 32:48].rearrange("p (t h) -> p t h", t=TB)
        stats = sm[:, 48:72].rearrange("p (t n s) -> p t n s", t=TB, n=2)
        mv = sm[:, 72:76].rearrange("p (t s) -> p t s", t=TB)
        std = sm[:, 76:78]
        normw = A[:, 10240:10368]

        hT = A[:, 0:FFN_TILES * T].rearrange("p (f t) -> p f t", f=FFN_TILES)
        ffn_s = [A[:, 5632:5888], A[:, 5888:6144]]

        fk = A[:, 0:2048].rearrange("p (c t) -> p c t", t=T)
        fq = A[:, 2048:4096].rearrange("p (c t) -> p c t", t=T)
        fv = A[:, 4096:6144].rearrange("p (t n) -> p t n", t=TB)
        fg = A[:, 6144:8192].rearrange("p (t n) -> p t n", t=TB)
        fo = A[:, 8192:10240].rearrange("p (t n) -> p t n", t=TB)
        KW = 3 * P
        flog = [A[:, 10240:10240 + KW], A[:, 10624:10624 + KW]]
        fprob = [A[:, 11008:11008 + KW], A[:, 11392:11392 + KW]]
        fprobT = [A[:, 11776:11776 + KW], A[:, 12160:12160 + KW]]
        negsel = A[0:FOX_HEADS, 12544:14592].rearrange("p (h m) -> p h m", h=FOX_HEADS)
        causal = A[:, 14592:14592 + KW]
        fz = A[0:FOX_HEADS, 14976:15232]
        fl = A[0:FOX_HEADS, 15232:15488]
        fc = A[0:FOX_HEADS, 15488:15744]
        nmax = A[:, 15744:15776]
        rsum = A[:, 15776:15808]
        rinv = A[:, 15808:15840]
        cT = A[:, 16000:16032].rearrange("p (t h) -> p t h", t=TB)

        iota = A[:, 16032:16160]
        before = A[:, 16160:16288]
        w8 = A[:, 16288:16296]
        w_router = A[:, 16296:16360].rearrange("p (k n) -> p k n", k=KT)
        w_f = A[:, 16360:16488].rearrange("p (k n) -> p k n", k=KT)
        xe = A[:, 0:1024].rearrange("p (k t) -> p k t", k=KT)
        pick = A[:, 1024:1280].rearrange("p (t n) -> p t n", t=TB)
        pickw = A[:, 1280:1536].rearrange("p (t n) -> p t n", t=TB)
        spread = A[:, 1536:1792].rearrange("p (t n) -> p t n", t=TB)
        gate_s = [A[:, 1792:2304], A[:, 2304:2816]]
        eh = A[:, 2816:3328]
        ehT = A[:, 3328:3840]
        ye = A[:, 3840:4864].rearrange("p (n c) -> p n c", n=2)
        yacc = A[:, 4864:6912].rearrange("p (t n) -> p t n", t=TB)
        rt = [A[:, 6912 + 16 * n:6928 + 16 * n] for n in range(12)]
        rank2 = A[:, 7200:7232].rearrange("p (t c) -> p t c", t=TB)
        comb2 = A[:, 7232:7264].rearrange("p (t c) -> p t c", t=TB)
        cur = A[:, 7264:7268]

        w_ready = [sem(f"w_ready{r}") for r in range(RING)]
        levels_loaded, mask_ready = sem("levels_loaded"), sem("mask_ready")
        consts_loaded, x_loaded, small_loaded = sem("consts_loaded"), sem("x_loaded"), sem("small_loaded")
        normw_loaded, gb_loaded, fox_loaded, route_loaded = (sem("normw_loaded"), sem("gb_loaded"),
                                                             sem("fox_loaded"), sem("route_loaded"))
        tp_done, tp_dve, tp_act = sem("tp_done"), sem("tp_copied_dve"), sem("tp_copied_act")
        pj_done, pj_out = sem("proj_done"), sem("proj_copied")
        lb_ready, loglb_ready, lb_exp = sem("lb_ready"), sem("loglb_ready"), sem("lb_exp")
        act_steps, dve_steps = sem("act_steps"), sem("dve_steps")
        sp_log, sp_sum, rlog_ready, kexp_ready, b_ready = (sem("softplus_log"), sem("softplus_sum"),
                                                          sem("floor_log"), sem("k_exp"), sem("b_ready"))
        q_ready, floor_max = sem("q_ready"), sem("floor_max")
        diff_ready, exp_ready, qt_ready, kt_ready = (sem("diff_ready"), sem("exp_ready"), sem("qt_ready"),
                                                     sem("kt_ready"))
        sc_done, sc_sel = sem("scores_done"), sem("scores_selected")
        at_done, at_out = sem("attn_done"), sem("attn_copied")
        sq_ready, ms_ready, rms_ready, gn_ready, on_ready = (sem("squares"), sem("mean_squares"), sem("rms"),
                                                             sem("gate_norm"), sem("hgrn_out"))
        hg_silu = sem("hgrn_gate_silu")
        y_done = sem("y_done")
        ln_var, ln_std, ln_scaled, x_ready = sem("ln_var"), sem("ln_std"), sem("ln_scaled"), sem("x_ready")
        ffn_done, ffn_silu, ffn_h, ffn_down_used = (sem("ffn_done"), sem("ffn_silu"), sem("ffn_h"),
                                                    sem("ffn_down_used"))
        f_log, c_ready, cT_done, cT_ready = sem("f_log"), sem("c_ready"), sem("cT_done"), sem("cT_ready")
        fx_qk, fx_max, fx_exp, fx_pt, fx_ptc, fx_pv, fx_out = (sem("fox_qk"), sem("fox_max"), sem("fox_exp"),
                                                              sem("fox_pT"), sem("fox_pT_copied"),
                                                              sem("fox_pv"), sem("fox_out"))
        fg_sig, og_ready = sem("fox_gate_sigmoid"), sem("fox_gated")
        lg_done, e2_in, e2_out, sel_ready, rk_done, pick_ready = (
            sem("router_logits"), sem("top2_difference"), sem("top2_exp"), sem("chosen_ready"),
            sem("ranks_done"), sem("pick_ready"))
        items_ready = sem("items_ready")
        ga_done, gaA_copied = sem("gather_done"), sem("xe_copied")
        a_done, b_done, d_done, silu_done, h_ready = (sem("a_done"), sem("b_done"), sem("down_done"),
                                                      sem("silu_done"), sem("h_ready"))
        htr_done, hT_ready = sem("hT_done"), sem("hT_copied")
        spr_done, spr_ready, ye_ready = sem("spread_done"), sem("spread_copied"), sem("ye_copied")
        sc2_done, yacc_up = sem("scatter_done"), sem("yacc_updates")
        dve_item = sem("dve_item_steps")
        dve_tail, out_done = sem("dve_tail_steps"), sem("out_done")

        w_in_v = w_in[0].rearrange("(k p) n -> p k n", p=P)
        w_out_v = w_out[0].rearrange("(k p) n -> p k n", p=P)
        gu_v = ffn_gu[0].rearrange("(k p) n -> p k n", p=P)
        down_v = ffn_down[0].rearrange("(f p) n -> p f n", p=P)
        kv_v = kv_w.rearrange("(k p) n -> p k n", p=P)
        qg_v = fox_qg[0].rearrange("(k p) n -> p k n", p=P)
        fo_v = fox_out[0].rearrange("(k p) n -> p k n", p=P)

        def slot(s):
            return ring[:, s % RING, :]

        def slot_k(s):
            return slot(s).rearrange("p (k n) -> p k n", k=KT)

        def loads_of(s):
            if s < S_HG_OUT:
                col = [1, 0, 2, 1, 0, 2, 3, 3][s] * D + [0, 0, 0, 1, 1, 1, 0, 1][s] * N
                return [(slot_k(s), w_in_v[:, :, col:col + N])]
            if s < S_GU:
                n = s - S_HG_OUT
                return [(slot_k(s), w_out_v[:, :, n * N:(n + 1) * N])]
            if s < S_DOWN:
                c = s - S_GU
                half = slot(s).rearrange("p (h k n) -> p h k n", h=2, k=KT)
                return [(half[:, h], gu_v[:, :, h * FFN + c * T:h * FFN + (c + 1) * T]) for h in range(2)]
            if s < S_KVQG:
                f0 = (s - S_DOWN) * FT
                f1 = min(f0 + FT, FFN_TILES)
                return [(slot(s)[:, 0:(f1 - f0) * D].rearrange("p (f n) -> p f n", n=D), down_v[:, f0:f1, :])]
            if s < S_FOX_OUT:
                n = s - S_KVQG
                src = [kv_v, kv_v, qg_v, qg_v, kv_v, kv_v, qg_v, qg_v][n]
                col = [0, N, 0, N, D, D + N, D, D + N][n]
                return [(slot_k(s), src[:, :, col:col + N])]
            n = s - S_FOX_OUT
            return [(slot_k(s), fo_v[:, :, n * N:(n + 1) * N])]

        filled = [0] * RING
        ready_at = []
        for s in range(S_MOE):
            filled[s % RING] += 16 * len(loads_of(s))
            ready_at.append(filled[s % RING])

        def slot_landed(pe, s):
            pe.wait_ge(w_ready[s % RING], ready_at[s])

        FOX_TILE0 = 24

        def slot_read(s):
            if s < S_HG_OUT:
                return pj_done, [4, 8, 10, 14, 18, 20, 22, 24][s]
            if s < S_GU:
                return y_done, 2 * (s - S_HG_OUT) + 2
            if s < S_DOWN:
                return ffn_done, 2 * (s - S_GU) + 2
            if s < S_KVQG - 1:
                return ffn_down_used, s - S_DOWN + 1
            if s == S_KVQG - 1:
                return y_done, 8
            if s < S_FOX_OUT:
                return pj_done, FOX_TILE0 + 1 + [4, 8, 12, 16, 18, 20, 22, 24][s - S_KVQG]
            return y_done, 8 + 2 * (s - S_FOX_OUT) + 2

        def moe_slot_read(i, j):
            kind, c = MOE_ORDER[j]
            return {"a": a_done, "b": b_done, "d": d_done}[kind], i * CH + c + 1

        def moe_ready(i, j):
            s = S_MOE + j
            return w_ready[s % RING], i * (16 * MOE_SLOTS // RING) + filled[s % RING] + 16 * (j // RING + 1)

        def moe_load(sp, e, j):
            kind, c = MOE_ORDER[j]
            s = S_MOE + j
            if kind == "d":
                src = moe_down[0, e, c * N:(c + 1) * N, :].rearrange("(f p) n -> p f n", p=P)
                dst = slot(s).rearrange("p (f n) -> p f n", n=D)
            else:
                col = c * N + (F if kind == "b" else 0)
                src = moe_gu[0, e, :, col:col + N].rearrange("(k p) n -> p k n", p=P)
                dst = slot_k(s)
            sp.dma_start(dst, src).then_inc(w_ready[s % RING], 16)

        block = ctx.enter_context(nc.Block())

        @block.sync
        def _(sp):
            sp.dma_start(xres[:, :, :], x[0].rearrange("(t p) n -> p t n", p=P)).then_inc(x_loaded, 16)
            for s in range(S_MOE):
                if s >= RING:
                    sp.wait_ge(*slot_read(s - RING))
                for dst, src in loads_of(s):
                    sp.dma_start(dst, src).then_inc(w_ready[s % RING], 16)
            for j in range(RING):
                sp.wait_ge(*slot_read(S_MOE + j - RING))
                moe_load(sp, 0, j)

            def rest_of(i, e):
                for j in range(RING, MOE_SLOTS):
                    sp.wait_ge(*moe_slot_read(i, j - RING))
                    moe_load(sp, e, j)

            def first_of(i, e):
                for j in range(RING):
                    sp.wait_ge(*moe_slot_read(i - 1, j + MOE_SLOTS - RING))
                    moe_load(sp, e, j)

            with sp.Fori(0, E - 1) as i:
                rest_of(i, i)
                first_of(i + 1, i + 1)
            rest_of(E - 1, E - 1)
            sp.wait_ge(items_ready, 2)
            more = sp.value_load(items[0:1, 16:17], min_val=0, max_val=3)
            with sp.If(more > 0):
                with sp.Fori(0, more) as n:
                    col = sp.value_load(items[0:1, bass.ds(n + E, 1)], min_val=E, max_val=2 * E - 1)
                    first_of(n + E, col - E)
                    rest_of(n + E, col - E)
            for t in range(TB):
                sp.wait_ge(x_ready, 6 + t + 1)
                sp.dma_start(out[0, t * P:(t + 1) * P, :], yacc[:, t, :]).then_inc(out_done, 16)
            sp.wait_ge(out_done, 16 * TB)

        @block.tensor
        def _(pe):
            def transpose_rows(stage, src, ready):
                for g in range(2 * TB):
                    t, half = divmod(g, 2)
                    if half == 0:
                        pe.wait_ge(*ready(t))
                    if t:
                        pe.wait_ge((tp_dve, tp_act)[half], 2 * stage + 1)
                    for j in range(4):
                        k = 4 * half + j
                        mm = pe.transpose(ps[:, 6 + half, j * P:(j + 1) * P], src[:, t, k * P:(k + 1) * P], ident)
                    mm.then_inc(tp_done, 1)

            def xT_ready(stage):
                pe.wait_ge(tp_dve, 2 * stage + 2)
                pe.wait_ge(tp_act, 2 * stage + 2)

            def proj_bank(n):
                if n >= 2:
                    pe.wait_ge(pj_out, n - 1)
                return n % 2

            def feature_tile(n, s, col, width=P):
                b = proj_bank(n)
                w = slot_k(s)
                for k in range(KT):
                    mm = pe.matmul(ps[0:width, b, 0:T], w[:, k, col:col + width], xT[:, k, :],
                                   start=(k == 0), stop=(k == KT - 1))
                mm.then_inc(pj_done, 1)

            def token_tile(n, s, t):
                b = proj_bank(n)
                w = slot_k(s)
                for k in range(KT):
                    mm = pe.matmul(bank(b), xT[:, k, t * P:(t + 1) * P], w[:, k, :],
                                   start=(k == 0), stop=(k == KT - 1))
                mm.then_inc(pj_done, 1)

            def hg_tile(n):
                s, j = [(0, 0), (0, 1), (0, 2), (0, 3), (1, 0), (1, 1), (1, 2), (1, 3), (2, 0), (2, 1),
                        (3, 0), (3, 1), (3, 2), (3, 3), (4, 0), (4, 1), (4, 2), (4, 3), (5, 0), (5, 1),
                        (6, 0), (6, 1), (7, 0), (7, 1)][n]
                if j == 0:
                    slot_landed(pe, s)
                if s in (0, 1, 3, 4):
                    feature_tile(n, s, j * P)
                else:
                    token_tile(n, s, j)

            def level(g, l):
                m, c = BUF_LEVELS * g + l, LEVELS * g + l
                if l < len(HALVES):
                    pe.wait_ge(qt_ready, m + 1)
                    pe.wait_ge(kt_ready, m + 1)
                    kk, qq = lev_k[m % 2], lev_q[m % 2]
                else:
                    kk, qq = hk[:, g * 1024:(g + 1) * 1024], hq[:, g * 1024:(g + 1) * 1024]
                if c >= 2:
                    pe.wait_ge(sc_sel, 2 * (c - 1))
                for h in range(2):
                    b = 2 + 2 * (c % 2) + h
                    for u in range(4):
                        cols = slice((4 * h + u) * P, (4 * h + u + 1) * P)
                        mm = pe.matmul(ps[:, b, u * P:(u + 1) * P], kk[:, cols], qq[:, cols],
                                       start=True, stop=True)
                    mm.then_inc(sc_done, 1)

            def attend_state(g):
                if g:
                    pe.wait_ge(at_out, 4 * g)
                pe.wait_ge(kt_ready, BUF_LEVELS * (g + 1))
                kk = lev_k[1]
                for h in range(4):
                    mm = pe.transpose(ps[:, 6, h * P:(h + 1) * P], kk[:, 2 * h * P:(2 * h + 1) * P], ident)
                mm.then_inc(at_done, 1)

            def attend(g):
                pe.wait_ge(at_out, 4 * g + 1)
                pe.wait_ge(pj_out, 10 + 10 * g)
                for h in range(4):
                    mm = pe.matmul(ps[:, 7, h * P:(h + 1) * P], khatT[:, h * P:(h + 1) * P],
                                   hv[:, 0, (4 * g + h) * P:(4 * g + h + 1) * P], start=True, stop=True)
                mm.then_inc(at_done, 1)
                pe.wait_ge(sc_sel, 2 * LEVELS * (g + 1))
                for h in range(4):
                    mm = pe.matmul(ps[:, 6, h * P:(h + 1) * P], scT[:, 2 * h * P:(2 * h + 1) * P],
                                   hv[:, 0, (4 * g + h) * P:(4 * g + h + 1) * P], start=True, stop=True)
                mm.then_inc(at_done, 1)
                pe.wait_ge(at_out, 4 * g + 2)
                pe.wait_ge(qt_ready, BUF_LEVELS * (g + 1))
                qq = lev_q[1]
                for h in range(4):
                    pe.matmul(ps[:, 7, h * P:(h + 1) * P], scT[:, (2 * h + 1) * P:(2 * h + 2) * P],
                              hv[:, 1, (4 * g + h) * P:(4 * g + h + 1) * P], start=True, stop=False)
                    mm = pe.matmul(ps[:, 7, h * P:(h + 1) * P], qq[:, (2 * h + 1) * P:(2 * h + 2) * P],
                                   state[:, h * P:(h + 1) * P], start=False, stop=True)
                mm.then_inc(at_done, 1)

            def out_projection(s0):
                for n in range(2):
                    slot_landed(pe, s0 + n)
                    w = slot_k(s0 + n)
                    for t in range(TB):
                        for k in range(KT):
                            mm = pe.matmul(bank(2 + 2 * n + t), xT[:, k, t * P:(t + 1) * P], w[:, k, :],
                                           start=(k == 0), stop=(k == KT - 1))
                        mm.then_inc(y_done, 1)

            pe.wait_ge(consts_loaded, 16)
            transpose_rows(0, xres, lambda t: (x_loaded, 16))
            xT_ready(0)
            for n in range(10):
                hg_tile(n)
            for l in range(LEVELS):
                hg_tile(10 + l)
                if l == LEVELS - 1:
                    pe.wait_ge(q_ready, 1)
                    pe.wait_ge(b_ready, 1)
                level(0, l)
            attend_state(0)
            hg_tile(18)
            attend(0)
            hg_tile(19)
            hg_tile(20)
            for n, levels in ((21, (0,)), (22, (1, 2)), (23, (3, 4, 5, 6, 7))):
                hg_tile(n)
                for l in levels:
                    if l == LEVELS - 1:
                        pe.wait_ge(q_ready, 2)
                        pe.wait_ge(b_ready, 2)
                    level(1, l)
            attend_state(1)
            attend(1)
            transpose_rows(1, ho, lambda t: (on_ready, t + 1))
            xT_ready(1)
            out_projection(S_HG_OUT)

            transpose_rows(2, xres, lambda t: (x_ready, t + 1))
            xT_ready(2)
            for c in range(FFN_CH):
                s = S_GU + c
                slot_landed(pe, s)
                w = slot(s).rearrange("p (h k n) -> p h k n", h=2, k=KT)
                for j in range(2):
                    f = 2 * c + j
                    if f >= 2:
                        pe.wait_ge(ffn_h, f - 1)
                    for h in range(2):
                        for k in range(KT):
                            mm = pe.matmul(ps[:, f % 2, h * T:(h + 1) * T], w[:, h, k, j * P:(j + 1) * P],
                                           xT[:, k, :], start=(k == 0), stop=(k == KT - 1))
                    mm.then_inc(ffn_done, 1)
            for f in range(FFN_TILES):
                s = S_DOWN + f // FT
                if f % FT == 0:
                    slot_landed(pe, s)
                pe.wait_ge(ffn_h, f + 1)
                w = slot(s).rearrange("p (f n) -> p f n", n=D)
                for t in range(TB):
                    for n in range(2):
                        mm = pe.matmul(bank(2 + 2 * n + t), hT[:, f, t * P:(t + 1) * P],
                                       w[:, f % FT, n * N:(n + 1) * N],
                                       start=(f == 0), stop=(f == FFN_TILES - 1))
                        if f == FFN_TILES - 1:
                            mm.then_inc(y_done, 1)
                if f % FT == FT - 1:
                    mm.then_inc(ffn_down_used, 1)

            transpose_rows(3, xres, lambda t: (x_ready, 2 + t + 1))
            xT_ready(3)
            pe.wait_ge(route_loaded, 80)
            for k in range(KT):
                mm = pe.matmul(ps[0:FOX_HEADS, 0, 0:T], w_f[:, k, :], xT[:, k, :],
                               start=(k == 0), stop=(k == KT - 1))
            mm.then_inc(pj_done, 1)
            for n in range(16):
                s = S_KVQG + n // 4
                if n % 4 == 0:
                    slot_landed(pe, s)
                feature_tile(FOX_TILE0 + 1 + n, s, (n % 4) * P)

            def fox_token_tile(n):
                s = S_KVQG + 4 + n // 2
                if n % 2 == 0:
                    slot_landed(pe, s)
                token_tile(FOX_TILE0 + 17 + n, s, n % 2)

            fox_token_tile(0)
            fox_token_tile(1)
            pe.wait_ge(c_ready, 1)
            for t in range(TB):
                mm = pe.transpose(ps[:, 6, t * FOX_HEADS:(t + 1) * FOX_HEADS], fc[:, t * P:(t + 1) * P],
                                  sq[0:FOX_HEADS, 0:FOX_HEADS])
            mm.then_inc(cT_done, 1)
            pe.wait_ge(fox_loaded, 32)

            def fox_scores(h):
                if h >= 2:
                    pe.wait_ge(fx_max, h - 1)
                if h == 0:
                    pe.wait_ge(pj_out, FOX_TILE0 + 17)
                rows = slice((h % 2) * 64, (h % 2) * 64 + 64)
                for t in range(TB):
                    dst = ps[:, 2 + h % 2, t * P:t * P + (t + 1) * P]
                    pe.matmul(dst, negsel[:, h, :], fc[:, 0:(t + 1) * P], start=True, stop=False)
                    mm = pe.matmul(dst, fq[rows, h // 2, t * P:(t + 1) * P], fk[rows, h // 2, 0:(t + 1) * P],
                                   start=False, stop=True)
                mm.then_inc(fx_qk, 1)

            def fox_turn(h):
                pe.wait_ge(fx_exp, h + 1)
                if h >= 2:
                    pe.wait_ge(fx_ptc, h - 1)
                for j in range(3):
                    mm = pe.transpose(ps[:, 4 + h % 2, j * P:(j + 1) * P], fprob[h % 2][:, j * P:(j + 1) * P], ident)
                mm.then_inc(fx_pt, 1)

            def fox_values(h):
                pe.wait_ge(fx_ptc, h + 1)
                if h == 0:
                    pe.wait_ge(cT_ready, 1)
                    pe.wait_ge(pj_out, FOX_TILE0 + 19)
                if h == 8:
                    pe.wait_ge(pj_out, FOX_TILE0 + 21)
                if h >= 2:
                    pe.wait_ge(fx_out, h - 1)
                cols = slice(h * FOX_DIM, (h + 1) * FOX_DIM)
                pT = fprobT[h % 2]
                pe.matmul(ps[:, 6 + h % 2, 0:64], pT[:, 0:P], fv[:, 0, cols], start=True, stop=True)
                pe.matmul(ps[:, 6 + h % 2, 64:128], pT[:, P:2 * P], fv[:, 0, cols], start=True, stop=False)
                pe.matmul(ps[:, 6 + h % 2, 64:128], pT[:, 2 * P:3 * P], fv[:, 1, cols], start=False,
                          stop=True).then_inc(fx_pv, 1)

            for h in range(FOX_HEADS + 2):
                if h < FOX_HEADS:
                    fox_scores(h)
                if 1 <= h <= FOX_HEADS:
                    fox_turn(h - 1)
                if h >= 2:
                    fox_values(h - 2)
                if h % 2 == 1 and h < 12:
                    fox_token_tile(2 + h // 2)
            transpose_rows(4, fo, lambda t: (og_ready, t + 1))
            xT_ready(4)
            out_projection(S_FOX_OUT)

            transpose_rows(5, xres, lambda t: (x_ready, 4 + t + 1))
            xT_ready(5)
            for t in range(TB):
                for k in range(KT):
                    mm = pe.matmul(ps[:, 0, t * E:(t + 1) * E], xT[:, k, t * P:(t + 1) * P], w_router[:, k, :],
                                   start=(k == 0), stop=(k == KT - 1))
            mm.then_inc(lg_done, 1)
            pe.wait_ge(sel_ready, 1)
            sel = rt[8]
            pe.matmul(ps[:, 1, 0:E], before, sel[:, 0:E], start=True, stop=True)
            pe.matmul(ps[:, 1, E:2 * E], ones, sel[:, 0:E], start=True, stop=False)
            pe.matmul(ps[:, 1, E:2 * E], before, sel[:, E:2 * E], start=False, stop=True)
            pe.matmul(ps[0:1, 1, 2 * E:3 * E], ones[:, 0:1], sel[:, 0:E], start=True, stop=False)
            pe.matmul(ps[0:1, 1, 2 * E:3 * E], ones[:, 0:1], sel[:, E:2 * E], start=False,
                      stop=True).then_inc(rk_done, 1)

            def gather(i, half):
                if half == 0:
                    pe.wait_ge(pick_ready, i + 1)
                for j in range(4):
                    k = 4 * half + j
                    for t in range(TB):
                        mm = pe.matmul(ps[:, 7 - half, j * P:(j + 1) * P], xres[:, t, k * P:(k + 1) * P],
                                       pick[:, t, :], start=(t == 0), stop=(t == TB - 1))
                mm.then_inc(ga_done, 1)

            def gate_or_up(i, c, kind):
                j = MOE_ORDER.index((kind, c))
                pe.wait_ge(*moe_ready(i, j))
                w = slot_k(S_MOE + j)
                b = 2 * (c % 2) + (kind == "b")
                for k in range(KT):
                    mm = pe.matmul(bank(b), xe[:, k, :], w[:, k, :], start=(k == 0), stop=(k == KT - 1))
                mm.then_inc(b_done if kind == "b" else a_done, 1)

            def turn_h(i, c):
                pe.wait_ge(h_ready, i * CH + c + 1)
                for f in range(FT):
                    mm = pe.transpose(ps[:, 6, f * P:(f + 1) * P], eh[:, f * P:(f + 1) * P], ident)
                mm.then_inc(htr_done, 1)

            def down(i, c):
                j = MOE_ORDER.index(("d", c))
                pe.wait_ge(*moe_ready(i, j))
                pe.wait_ge(hT_ready, i * CH + c + 1)
                w = slot(S_MOE + j).rearrange("p (f n) -> p f n", n=D)
                for f in range(FT):
                    for n in range(2):
                        mm = pe.matmul(bank(4 + n), ehT[:, f * P:(f + 1) * P], w[:, f, n * N:(n + 1) * N],
                                       start=(c == 0 and f == 0), stop=(c == CH - 1 and f == FT - 1))
                mm.then_inc(d_done, 1)

            def item(i):
                pe.wait_ge(gaA_copied, 2 * i + 2)
                gate_or_up(i, 0, "a")
                gate_or_up(i, 0, "b")
                pe.wait_ge(yacc_up, 4 * i + 2)
                for t in range(TB):
                    mm = pe.transpose(ps[:, 6, t * P:(t + 1) * P], pickw[:, t, :], ident)
                mm.then_inc(spr_done, 1)
                for c in range(1, CH):
                    gate_or_up(i, c, "a")
                    if c == 1:
                        pe.wait_ge(spr_ready, i + 1)
                    turn_h(i, c - 1)
                    gate_or_up(i, c, "b")
                    down(i, c - 1)
                turn_h(i, CH - 1)
                gather(i + 1, 0)
                down(i, CH - 1)
                gather(i + 1, 1)
                pe.wait_ge(ye_ready, 2 * i + 2)
                for n in range(2):
                    for t in range(TB):
                        if n == 0:
                            pe.wait_ge(gaA_copied, 2 * i + 3 + t)
                        else:
                            pe.wait_ge(yacc_up, 4 * i + 3 + t)
                        pe.matmul(bank(7 - t), spread[:, t, :], ye[:, n, :], start=True,
                                  stop=True).then_inc(sc2_done, 1)

            gather(0, 0)
            gather(0, 1)
            with pe.Fori(0, E) as i:
                item(i)
            more = pe.value_load(items[0:1, 16:17], min_val=0, max_val=3)
            with pe.If(more > 0):
                with pe.Fori(0, more) as n:
                    item(n + E)

        @block.scalar
        def _(act):
            step = Steps(act, act_steps)

            def turned(stage):
                for t in range(TB):
                    act.wait_ge(tp_done, 4 * stage + 2 * t + 2)
                    act.activation(xT[:, 4:8, t * P:(t + 1) * P],
                                   bank(7).rearrange("p (k t) -> p k t", k=4), ACT.Copy).then_inc(tp_act, 1)

            def copy_tile(n, dst, scale=1.0, cols=N):
                act.wait_ge(pj_done, n + 1)
                act.activation(dst, bank(n % 2, cols), ACT.Copy, scale=scale).then_inc(pj_out, 1)

            act.dma_start(sq[:, :], c_square).then_inc(consts_loaded, 16)
            act.dma_start(lev_k[0], c_levels).then_inc(levels_loaded, 16)
            act.wait_ge(lb_ready, 1)
            act.activation(lbt, sm[:, 32:40], ACT.Exp).then_inc(lb_exp, 1)
            act.wait_ge(lb_ready, 2)
            step(act.activation(loglb, sm[:, 40:48], ACT.Ln, scale=2.0 ** LN_SHIFT))
            act.activation(loglb, loglb, ACT.Copy, bias=-LN_SHIFT * LN2).then_inc(loglb_ready, 1)
            turned(0)

            def hg_copy(n):
                if n in (0, 1, 2, 3, 10, 11, 12, 13):
                    h = n if n < 4 else n - 6
                    copy_tile(n, zb[:, h * T:(h + 1) * T], cols=T)
                elif n in (4, 5, 6, 7, 14, 15, 16, 17):
                    h = n - 4 if n < 8 else n - 10
                    copy_tile(n, hq[:, h * T:(h + 1) * T], cols=T)
                elif n < 20:
                    t, g = n % 2, n // 18
                    copy_tile(n, hv[:, t, g * N:(g + 1) * N])
                else:
                    t, g = n % 2, (n - 20) // 2
                    copy_tile(n, hg[:, t, g * N:(g + 1) * N])

            def log_gates_a(g):
                z = zb[:, g * 1024:(g + 1) * 1024]
                act.wait_ge(pj_out, 4 + 10 * g)
                if g:
                    act.wait_ge(b_ready, 1)
                step(act.activation(ph_l, z, ACT.Abs))
                step(act.activation(ph_l, ph_l, ACT.Exp, scale=-1.0))
                act.activation(ph_l, ph_l, ACT.Ln, bias=1.0).then_inc(sp_log, 1)

            def log_gates_b(g):
                k = hk[:, g * 1024:(g + 1) * 1024]
                act.wait_ge(sp_sum, g + 1)
                for h in range(4):
                    ins = act.activation(ph_l[:, h * T:(h + 1) * T], zb[:, (4 * g + h) * T:(4 * g + h + 1) * T],
                                         ACT.Abs, bias=nloglb[:, 4 * g + h:4 * g + h + 1])
                step(ins)
                step(act.activation(ph_l, ph_l, ACT.Exp, scale=-1.0))
                act.activation(ph_l, ph_l, ACT.Ln, bias=1.0).then_inc(rlog_ready, 1)
                act.wait_ge(floor_max, g + 1)
                act.activation(k, k, ACT.Exp, scale=-1.0).then_inc(kexp_ready, 1)

            def silu_q(g):
                act.wait_ge(pj_out, 8 + 10 * g)
                q = hq[:, g * 1024:(g + 1) * 1024]
                act.activation(q, q, ACT.Silu).then_inc(q_ready, 1)

            def level_exp(g, l):
                m = BUF_LEVELS * g + l
                e = lev_e[m % 2]
                if l < len(HALVES):
                    act.wait_ge(diff_ready, len(HALVES) * g + l + 1)
                    act.activation(e, e, ACT.Exp).then_inc(exp_ready, 1)
                    return
                act.wait_ge(kt_ready, m - 1)
                act.wait_ge(qt_ready, m - 1)
                for h in range(4):
                    b = zb[:, (4 * g + h) * T:(4 * g + h + 1) * T]
                    act.activation(e[:, h * T:h * T + P], b[:, 0:P], ACT.Exp, scale=-1.0, bias=b[:, P - 1:P])
                    ins = act.activation(e[:, h * T + P:(h + 1) * T], b[:, P:T], ACT.Exp)
                ins.then_inc(exp_ready, 1)

            def attn_copies(g, first, last):
                for n in range(first, last):
                    act.wait_ge(at_done, 4 * g + n + 1)
                    dst = [khatT, state, ho[:, 0, g * N:(g + 1) * N], ho[:, 1, g * N:(g + 1) * N]][n]
                    act.activation(dst, bank(6 + n % 2), ACT.Copy).then_inc(at_out, 1)

            for n in range(4):
                hg_copy(n)
            act.wait_ge(lb_ready, 3)
            log_gates_a(0)
            hg_copy(4)
            hg_copy(5)
            log_gates_b(0)
            for n in range(6, 10):
                hg_copy(n)
            silu_q(0)
            for l in range(len(HALVES)):
                level_exp(0, l)
                hg_copy(10 + l)
            level_exp(0, len(HALVES))
            hg_copy(17)
            attn_copies(0, 0, 1)
            hg_copy(18)
            attn_copies(0, 1, 4)
            hg_copy(19)
            log_gates_a(1)
            log_gates_b(1)
            silu_q(1)
            act.wait_ge(b_ready, 2)
            hg_copy(20)
            level_exp(1, 0)
            level_exp(1, 1)
            hg_copy(21)
            level_exp(1, 2)
            level_exp(1, 3)
            hg_copy(22)
            for l in range(4, len(HALVES) + 1):
                level_exp(1, l)
                if l == 4:
                    hg_copy(23)
            act.wait_ge(pj_out, 24)
            act.activation(A[:, 8192:10240], A[:, 8192:10240], ACT.Silu).then_inc(hg_silu, 1)
            attn_copies(1, 0, 4)
            act.wait_ge(at_out, 8)
            act.wait_ge(at_done, 8)
            for t in range(TB):
                act.activation(lev_q[t], ho[:, t, :], ACT.Square).then_inc(sq_ready, 1)
            act.wait_ge(ms_ready, 1)
            act.activation(sm[:, 32:48], sm[:, 32:48], ACT.Sqrt).then_inc(rms_ready, 1)
            turned(1)

            def ln_sqrt(k):
                act.wait_ge(ln_var, k + 1)
                act.activation(std, mv[:, :, 1], ACT.Sqrt).then_inc(ln_std, 1)

            ln_sqrt(0)
            turned(2)
            for f in range(FFN_TILES):
                act.wait_ge(ffn_done, f + 1)
                if f >= 2:
                    act.wait_ge(ffn_h, f - 1)
                act.activation(ffn_s[f % 2], ps[:, f % 2, 0:T], ACT.Silu).then_inc(ffn_silu, 1)
            ln_sqrt(1)
            turned(3)

            act.wait_ge(pj_done, FOX_TILE0 + 1)
            act.wait_ge(small_loaded, 32)
            act.activation(fz, ps[0:FOX_HEADS, 0, 0:T], ACT.Identity, bias=fgb[:, 0:1]).then_inc(pj_out, 1)
            act.wait_ge(pj_out, FOX_TILE0 + 1)
            step(act.activation(fl, fz, ACT.Abs))
            step(act.activation(fl, fl, ACT.Exp, scale=-1.0))
            act.activation(fl, fl, ACT.Ln, bias=1.0).then_inc(f_log, 1)
            for n in range(8):
                copy_tile(FOX_TILE0 + 1 + n, fk[:, n, :], cols=T)
            for n in range(8):
                copy_tile(FOX_TILE0 + 9 + n, fq[:, n, :], scale=FOX_DIM ** -0.5, cols=T)

            def fox_copy(n):
                dst = fv if n < 4 else fg
                c = (n % 4) // 2
                copy_tile(FOX_TILE0 + 17 + n, dst[:, n % 2, c * N:(c + 1) * N])

            fox_copy(0)
            fox_copy(1)
            for h in range(FOX_HEADS + 1):
                if h < FOX_HEADS:
                    act.wait_ge(fx_max, h + 1)
                    if h >= 2:
                        act.wait_ge(fx_pt, h - 1)
                    for t in range(TB):
                        cols = slice(0, P) if t == 0 else slice(P, KW)
                        c = 2 * h + t
                        ins = act.activation(fprob[h % 2][:, cols], flog[h % 2][:, cols], ACT.Exp,
                                             bias=nmax[:, c:c + 1], accum_out=rsum[:, c:c + 1])
                    ins.then_inc(fx_exp, 1)
                if h >= 1:
                    act.wait_ge(fx_pt, h)
                    if h >= 3:
                        act.wait_ge(fx_pv, h - 2)
                    act.activation(fprobT[(h - 1) % 2], bank(4 + (h - 1) % 2, KW), ACT.Copy).then_inc(fx_ptc, 1)
                if h % 2 == 1 and h < 12:
                    fox_copy(2 + h // 2)
            act.wait_ge(pj_out, FOX_TILE0 + 25)
            for t in range(TB):
                act.activation(fg[:, t, :], fg[:, t, :], ACT.Sigmoid).then_inc(fg_sig, 1)
            turned(4)
            ln_sqrt(2)
            turned(5)
            act.wait_ge(e2_in, 1)
            act.activation(rt[9][:, 0:2], rt[9][:, 2:4], ACT.Exp).then_inc(e2_out, 1)

            def copy_rows(i, half):
                act.wait_ge(ga_done, 2 * i + half + 1)
                act.activation(xe[:, 4 * half:4 * half + 4, :],
                               bank(7 - half).rearrange("p (k t) -> p k t", k=4), ACT.Copy).then_inc(gaA_copied, 1)

            def copy_hT(i, c):
                act.wait_ge(htr_done, i * CH + c + 1)
                act.activation(ehT, bank(6), ACT.Copy).then_inc(hT_ready, 1)

            def item(i):
                for c in range(CH):
                    act.wait_ge(a_done, i * CH + c + 1)
                    act.activation(gate_s[c % 2], bank(2 * (c % 2)), ACT.Silu).then_inc(silu_done, 1)
                    if c:
                        copy_hT(i, c - 1)
                copy_hT(i, CH - 1)
                copy_rows(i + 1, 0)
                act.wait_ge(d_done, i * CH + CH)
                for n in range(2):
                    act.activation(ye[:, n, :], bank(4 + n), ACT.Copy).then_inc(ye_ready, 1)
                copy_rows(i + 1, 1)

            copy_rows(0, 0)
            copy_rows(0, 1)
            with act.Fori(0, E) as i:
                item(i)
            act.wait_ge(items_ready, 2)
            more = act.value_load(items[0:1, 16:17], min_val=0, max_val=3)
            with act.If(more > 0):
                with act.Fori(0, more) as n:
                    item(n + E)
            ln_sqrt(3)

        @block.vector
        def _(dve):
            step = Steps(dve, dve_steps)

            def turned(stage):
                for t in range(TB):
                    dve.wait_ge(tp_done, 4 * stage + 2 * t + 1)
                    dve.tensor_copy(xT[:, 0:4, t * P:(t + 1) * P],
                                    bank(6).rearrange("p (k t) -> p k t", k=4)).then_inc(tp_dve, 1)

            step(dve.memset(scT, 0.0))
            dve.wait_ge(small_loaded, 32)
            dve.tensor_tensor(sm[:, 32:40], lbt, lbt, ALU.subtract).then_inc(lb_ready, 1)
            dve.wait_ge(lb_exp, 1)
            step(dve.reciprocal(sm[:, 32:40], lbt))
            step(dve.tensor_tensor(lbt, lbt, sm[:, 32:40], ALU.mult))
            step(dve.tensor_tensor(lbt, lbt, lbt, ALU.subtract))
            step(dve.tensor_scalar(one_m_lb, lbt, -1.0, 1.0, ALU.mult, ALU.add))
            dve.tensor_scalar(sm[:, 40:48], lbt, LB_FLOOR, None, ALU.max).then_inc(lb_ready, 1)
            dve.wait_ge(loglb_ready, 1)
            dve.tensor_scalar(nloglb, loglb, -1.0, None, ALU.mult).then_inc(lb_ready, 1)
            turned(0)

            def log_gates(g):
                z, k = zb[:, g * 1024:(g + 1) * 1024], hk[:, g * 1024:(g + 1) * 1024]
                dve.wait_ge(sp_log, g + 1)
                step(dve.scalar_tensor_tensor(ph_a, z, 0.0, ph_l, ALU.min, ALU.subtract))
                dve.scalar_tensor_tensor(k, z, 0.0, ph_l, ALU.max, ALU.add).then_inc(sp_sum, 1)
                dve.wait_ge(sp_sum, g + 1)
                for h in range(4):
                    cols = slice(h * T, (h + 1) * T)
                    ins = dve.scalar_tensor_tensor(ph_a[:, cols], k[:, cols], loglb[:, 4 * g + h:4 * g + h + 1],
                                                   ph_a[:, cols], ALU.subtract, ALU.max, reverse0=True)
                ins.then_inc(floor_max, 1)
                dve.wait_ge(floor_max, g + 1)
                dve.wait_ge(kexp_ready, g + 1)
                for h in range(4):
                    cols = slice(h * T, (h + 1) * T)
                    step.note(dve.tensor_scalar(k[:, cols], k[:, cols], one_m_lb[:, 4 * g + h:4 * g + h + 1], None,
                                                ALU.mult))
                dve.wait_ge(rlog_ready, g + 1)
                dve.wait_ge(dve_steps, step.n)
                step(dve.tensor_tensor(ph_a, ph_a, ph_l, ALU.add))
                for u in range(8):
                    cols = slice(u * P, (u + 1) * P)
                    ins = dve.tensor_tensor_scan(z[:, cols], ones, ph_a[:, cols], 0.0, ALU.mult, ALU.add)
                ins.then_inc(b_ready, 1)
                dve.wait_ge(b_ready, g + 1)

            def level_diff(g, l):
                m = BUF_LEVELS * g + l
                if m >= 2:
                    dve.wait_ge(kt_ready, m - 1)
                    dve.wait_ge(qt_ready, m - 1)
                half = HALVES[l]
                n = 1024 // (2 * half)
                b = zb[:, g * 1024:(g + 1) * 1024].rearrange("p (n s h) -> p n s h", s=2, h=half)
                e = lev_e[m % 2].rearrange("p (n s h) -> p n s h", s=2, h=half)
                ref = b[:, :, 0, half - 1:half].to_broadcast([P, n, half])
                dve.tensor_tensor(e[:, :, 0, :], ref, b[:, :, 0, :], ALU.subtract)
                dve.tensor_tensor(e[:, :, 1, :], b[:, :, 1, :], ref, ALU.subtract).then_inc(diff_ready, 1)

            def level_keys(g, l):
                m = BUF_LEVELS * g + l
                dve.wait_ge(exp_ready, m + 1)
                if l == len(HALVES):
                    dve.wait_ge(sc_done, 2 * (LEVELS * g + l - 1))
                elif g and l < 2:
                    dve.wait_ge(at_done, 4 * g)
                elif l >= 2:
                    dve.wait_ge(sc_done, 2 * (LEVELS * g + l - 1))
                dve.tensor_tensor(lev_k[m % 2], hk[:, g * 1024:(g + 1) * 1024], lev_e[m % 2], ALU.mult)\
                   .then_inc(kt_ready, 1)

            def level_select(g, l):
                c = LEVELS * g + l
                for h in range(2):
                    dve.wait_ge(sc_done, 2 * c + h + 1)
                    if c or h:
                        dve.wait_ge(sc_sel, 2 * c + h)
                    if g and l == 0:
                        dve.wait_ge(at_done, 4 * g)
                    mask = level_mask[:, l, :].unsqueeze(1).to_broadcast([P, 4, P])
                    dst = scT[:, h * N:(h + 1) * N].rearrange("p (u t) -> p u t", u=4)
                    src = bank(2 + 2 * (c % 2) + h).rearrange("p (u t) -> p u t", u=4)
                    dve.copy_predicated(dst, mask, src).then_inc(sc_sel, 1)

            log_gates(0)
            dve.wait_ge(mask_ready, 1)
            for g in range(2):
                level_diff(g, 0)
                for l in range(len(HALVES) + 1):
                    if l + 1 < len(HALVES):
                        level_diff(g, l + 1)
                    level_keys(g, l)
                    if l:
                        level_select(g, l - 1)
                level_select(g, LEVELS - 1)
                if g == 0:
                    log_gates(1)
            for t in range(TB):
                dve.wait_ge(sq_ready, t + 1)
                step(dve.tensor_reduce(ssq[:, t, :], lev_q[t].rearrange("p (h e) -> p h e", h=HG_HEADS), AX_X, ALU.add))
            dve.tensor_scalar(sm[:, 32:48], sm[:, 32:48], 1.0 / P, RMS_EPS, ALU.mult, ALU.add).then_inc(ms_ready, 1)
            dve.wait_ge(rms_ready, 1)
            step(dve.reciprocal(sm[:, 32:48], sm[:, 32:48]))
            for t in range(TB):
                o = ho[:, t, :].rearrange("p (h e) -> p h e", h=HG_HEADS)
                step(dve.tensor_tensor(o, o, ssq[:, t, :].unsqueeze(2).to_broadcast([P, HG_HEADS, P]), ALU.mult))
                dve.wait_ge(gn_ready, t + 1)
                dve.tensor_tensor(ho[:, t, :], ho[:, t, :], hg[:, t, :], ALU.mult).then_inc(on_ready, 1)
            turned(1)

            def ln_stats(k, r, steps):
                for t in range(TB):
                    for n in range(2):
                        steps(dve.bn_stats(stats[:, t, n, :], r[:, t, n * N:(n + 1) * N]))
                    steps(dve.bn_aggr(mv[:, t, :], stats[:, t, :, :].rearrange("p n s -> p (n s)")))
                dve.tensor_scalar(mv[:, :, 1], mv[:, :, 1], LN_EPS, None, ALU.add).then_inc(ln_var, 1)
                dve.wait_ge(ln_std, k + 1)
                steps(dve.reciprocal(std, std))
                dve.wait_ge(gb_loaded, 32 * (k + 1))
                for t in range(TB):
                    steps(dve.tensor_scalar(r[:, t, :], r[:, t, :], mv[:, t, 0:1], std[:, t:t + 1], ALU.subtract,
                                            ALU.mult))
                    dve.tensor_tensor(r[:, t, :], r[:, t, :], gb[:, 0, :], ALU.mult).then_inc(ln_scaled, 1)

            def residual(k):
                for n in range(2):
                    for t in range(TB):
                        order = 2 * t + n if k == 1 else 2 * n + t
                        dve.wait_ge(y_done, 4 * k + order + 1)
                        cols = slice(n * N, (n + 1) * N)
                        step.note(dve.scalar_tensor_tensor(xres[:, t, cols], xres[:, t, cols], ALPHA,
                                                           bank(2 + 2 * n + t), ALU.mult, ALU.add))
                dve.wait_ge(dve_steps, step.n)
                ln_stats(k, xres, step)

            residual(0)
            turned(2)
            for f in range(FFN_TILES):
                dve.wait_ge(ffn_silu, f + 1)
                dve.tensor_tensor(hT[:, f, :], ffn_s[f % 2], ps[:, f % 2, T:2 * T], ALU.mult).then_inc(ffn_h, 1)
            residual(1)
            turned(3)

            dve.wait_ge(f_log, 1)
            step(dve.scalar_tensor_tensor(fl, fz, 0.0, fl, ALU.min, ALU.subtract))
            dve.tensor_tensor_scan(fc, sq[0:FOX_HEADS, P:P + 1].to_broadcast([FOX_HEADS, T]), fl, 0.0,
                                   ALU.mult, ALU.add).then_inc(c_ready, 1)
            dve.wait_ge(cT_done, 1)
            dve.tensor_copy(A[:, 16000:16032], ps[:, 6, 0:32]).then_inc(cT_ready, 1)
            dve.wait_ge(cT_ready, 1)
            dve.wait_ge(fox_loaded, 32)

            def fox_max(h):
                dve.wait_ge(fx_qk, h + 1)
                if h >= 2:
                    dve.wait_ge(fx_exp, h - 1)
                for t in range(TB):
                    cols = slice(0, P) if t == 0 else slice(P, KW)
                    step.note(dve.scalar_tensor_tensor(flog[h % 2][:, cols], ps[:, 2 + h % 2, cols],
                                                       cT[:, t, h:h + 1], causal[:, cols], ALU.add, ALU.add))
                for t in range(TB):
                    cols = slice(0, P) if t == 0 else slice(P, KW)
                    dve.wait_ge(dve_steps, step.n - 1 + t)
                    ins = dve.tensor_reduce(nmax[:, 2 * h + t:2 * h + t + 1], flog[h % 2][:, cols], AX_X, ALU.max,
                                            negate=True)
                ins.then_inc(fx_max, 1)

            def fox_norm(h):
                dve.wait_ge(fx_pv, h + 1)
                step(dve.reciprocal(rinv[:, 2 * h:2 * h + 2], rsum[:, 2 * h:2 * h + 2]))
                dve.tensor_tensor(fo[:, :, h * FOX_DIM:(h + 1) * FOX_DIM],
                                  bank(6 + h % 2, 2 * FOX_DIM).rearrange("p (t e) -> p t e", t=TB),
                                  rinv[:, 2 * h:2 * h + 2].unsqueeze(2).to_broadcast([P, TB, FOX_DIM]),
                                  ALU.mult).then_inc(fx_out, 1)

            for h in range(FOX_HEADS + 2):
                if h < FOX_HEADS:
                    fox_max(h)
                if h >= 2:
                    fox_norm(h - 2)
            dve.wait_ge(fx_out, FOX_HEADS)
            for t in range(TB):
                dve.wait_ge(fg_sig, t + 1)
                dve.tensor_tensor(fo[:, t, :], fo[:, t, :], fg[:, t, :], ALU.mult).then_inc(og_ready, 1)
            turned(4)
            residual(2)
            turned(5)

            for t in range(TB):
                dve.wait_ge(x_ready, 4 + t + 1)
                dve.tensor_scalar(yacc[:, t, :], xres[:, t, :], ALPHA, None, ALU.mult).then_inc(yacc_up, 1)

            def by_token(a):
                return a.rearrange("p (t e) -> p t e", t=TB)

            def spread_e(a):
                return a.unsqueeze(2).to_broadcast([P, TB, E])

            w8b = w8.unsqueeze(1).to_broadcast([P, TB, E])
            lg, eq, f1, lg2, f2, tmp = rt[0], rt[1], rt[2], rt[3], rt[4], rt[5]
            m1, m2, kmax, w1, w2 = (rt[6][:, 0:2], rt[6][:, 2:4], rt[6][:, 4:6], rt[6][:, 6:8], rt[6][:, 8:10])
            comb, sel = rt[7], rt[8]
            dve.wait_ge(lg_done, 1)
            step(dve.tensor_copy(lg, ps[:, 0, 0:2 * E]))

            def first_largest(values, m, first):
                step(dve.tensor_reduce(m, by_token(values), AX_X, ALU.max))
                step(dve.tensor_tensor(by_token(eq), by_token(values), spread_e(m), ALU.is_ge))
                step(dve.tensor_tensor(by_token(eq), by_token(eq), w8b, ALU.mult))
                step(dve.tensor_reduce(kmax, by_token(eq), AX_X, ALU.max))
                step(dve.tensor_tensor(by_token(first), by_token(eq), spread_e(kmax), ALU.is_ge))

            first_largest(lg, m1, f1)
            step(dve.scalar_tensor_tensor(lg2, f1, MASKED, lg, ALU.mult, ALU.add))
            first_largest(lg2, m2, f2)
            dve.tensor_tensor(rt[9][:, 2:4], m2, m1, ALU.subtract).then_inc(e2_in, 1)
            dve.tensor_tensor(sel, f1, f2, ALU.add).then_inc(sel_ready, 1)
            dve.wait_ge(e2_out, 1)
            step(dve.tensor_scalar(w1, rt[9][:, 0:2], 1.0, None, ALU.add))
            step(dve.reciprocal(w1, w1))
            step(dve.tensor_tensor(w2, w1, rt[9][:, 0:2], ALU.mult))
            step(dve.tensor_tensor(by_token(tmp), by_token(f1), spread_e(w1), ALU.mult))
            step(dve.tensor_tensor(by_token(comb), by_token(f2), spread_e(w2), ALU.mult))
            step(dve.tensor_tensor(comb, comb, tmp, ALU.add))
            dve.wait_ge(sel_ready, 1)
            step(dve.tensor_scalar(tmp, sel, -NOT_CHOSEN, NOT_CHOSEN, ALU.mult, ALU.add))
            dve.wait_ge(rk_done, 1)
            step(dve.tensor_tensor(rank2[:, :, 0:E], by_token(ps[:, 1, 0:2 * E]), by_token(tmp), ALU.add))
            step(dve.tensor_scalar(rank2[:, :, E:2 * E], rank2[:, :, 0:E], -float(P), None, ALU.add))
            step(dve.tensor_copy(comb2[:, :, 0:E], by_token(comb)))
            step(dve.tensor_copy(comb2[:, :, E:2 * E], by_token(comb)))
            over, mx, cols_f = itf[:, 0:8], itf[:, 8:16], itf[:, 16:32]
            step(dve.tensor_scalar(over, ps[0:1, 1, 2 * E:3 * E], float(P), None, ALU.is_gt))
            step(dve.tensor_reduce(itf[:, 32:33], over, AX_X, ALU.add))
            step(dve.tensor_tensor(over, over, w8[0:1, :], ALU.mult))
            step(dve.max(mx, over))
            step(dve.tensor_scalar(cols_f[:, 0:8], w8[0:1, :], -1.0, float(E), ALU.mult, ALU.add))
            step(dve.tensor_scalar(cols_f[:, 8:16], mx, -1.0, 2.0 * E, ALU.mult, ALU.add))
            step(dve.tensor_scalar(cols_f[:, 8:16], cols_f[:, 8:16], 2.0 * E - 1, None, ALU.min))
            dve.tensor_copy(items[:, 0:16], cols_f).then_inc(items_ready, 1)
            dve.tensor_copy(items[:, 16:17], itf[:, 32:33]).then_inc(items_ready, 1)
            dve.wait_ge(items_ready, 2)

            PICK_STEPS = 5

            def build_pick(i, steps):
                col = dve.value_load(items[0:1, bass.ds(i, 1)], min_val=0, max_val=2 * E - 1)
                steps.note(dve.tensor_copy(cur[:, 0:2], rank2[:, :, bass.ds(col, 1)].squeeze(2)))
                steps(dve.tensor_copy(cur[:, 2:4], comb2[:, :, bass.ds(col, 1)].squeeze(2)))
                for t in range(TB):
                    steps.note(dve.tensor_scalar(pick[:, t, :], iota, cur[:, t:t + 1], None, ALU.is_equal))
                steps(dve.tensor_scalar(pickw[:, 0, :], iota, cur[:, 0:1], cur[:, 2:3], ALU.is_equal, ALU.mult))
                dve.tensor_scalar(pickw[:, 1, :], iota, cur[:, 1:2], cur[:, 3:4], ALU.is_equal, ALU.mult)\
                   .then_inc(pick_ready, 1)

            def item(i):
                for c in range(CH):
                    dve.wait_ge(b_done, i * CH + c + 1)
                    dve.wait_ge(silu_done, i * CH + c + 1)
                    dve.tensor_tensor(eh, gate_s[c % 2], bank(2 * (c % 2) + 1), ALU.mult).then_inc(h_ready, 1)
                    if c == 0:
                        dve.wait_ge(spr_done, i + 1)
                        dve.tensor_copy(A[:, 1536:1792], ps[:, 6, 0:2 * P]).then_inc(spr_ready, 1)
                    if c == 1:
                        build_pick(i + 1, Steps(dve, dve_item, i * PICK_STEPS + PICK_STEPS))
                for n in range(2):
                    for t in range(TB):
                        dve.wait_ge(sc2_done, 4 * i + 2 * n + t + 1)
                        if n == 0:
                            dve.wait_ge(yacc_up, 4 * i + 1 + t)
                        cols = slice(n * N, (n + 1) * N)
                        dve.tensor_tensor(yacc[:, t, cols], yacc[:, t, cols], bank(7 - t), ALU.add)\
                           .then_inc(yacc_up, 1)

            build_pick(0, Steps(dve, dve_item, 0))
            with dve.Fori(0, E) as i:
                item(i)
            more = dve.value_load(items[0:1, 16:17], min_val=0, max_val=3)
            with dve.If(more > 0):
                with dve.Fori(0, more) as n:
                    item(n + E)
            dve.wait_ge(yacc_up, (more + E) * 4 + 2)
            ln_stats(3, yacc, Steps(dve, dve_tail))

        @block.gpsimd
        def _(pool):
            with nc.allow_non_contiguous_dma("small parameters"):
                pool.dma_start(lbt, lb_logits[0].rearrange("(h p) -> p h", p=P)).then_inc(small_loaded, 16)
                pool.dma_start(fgb[:, :], fgate_b.rearrange("(p a) -> p a", a=1)).then_inc(small_loaded, 16)
            pool.wait_ge(levels_loaded, 16)
            pool.tensor_copy(level_mask.rearrange("p l n -> p (l n)"), lev_k[0]).then_inc(mask_ready, 1)
            for g in range(2):
                pool.wait_ge(q_ready, g + 1)
                for l in range(BUF_LEVELS):
                    m = BUF_LEVELS * g + l
                    pool.wait_ge(exp_ready, m + 1)
                    if g and l < 2:
                        pool.wait_ge(at_done, 4 * g)
                    elif l >= 2:
                        pool.wait_ge(sc_done, 2 * (LEVELS * g + l - 1))
                    pool.tensor_tensor(lev_q[m % 2], hq[:, g * 1024:(g + 1) * 1024], lev_e[m % 2], ALU.mult)\
                        .then_inc(qt_ready, 1)
            pool.wait_ge(kt_ready, 2 * BUF_LEVELS)
            pool.wait_ge(qt_ready, 2 * BUF_LEVELS)
            pool.dma_start(normw, norm_w[0:1, :].to_broadcast([P, P])).then_inc(normw_loaded, 16)
            pool.wait_ge(normw_loaded, 16)
            pool.wait_ge(hg_silu, 1)
            for t in range(TB):
                g3 = hg[:, t, :].rearrange("p (h e) -> p h e", h=HG_HEADS)
                pool.tensor_tensor(g3, g3, normw.unsqueeze(1).to_broadcast([P, HG_HEADS, P]), ALU.mult)\
                    .then_inc(gn_ready, 1)

            def load_ln(gains, biases, layer):
                pool.dma_start(gb[:, 0, :], gains[layer:layer + 1, :].to_broadcast([P, D])).then_inc(gb_loaded, 16)
                pool.dma_start(gb[:, 1, :], biases[layer:layer + 1, :].to_broadcast([P, D])).then_inc(gb_loaded, 16)

            def ln_bias(k, r):
                for t in range(TB):
                    pool.wait_ge(ln_scaled, 2 * k + t + 1)
                    pool.tensor_tensor(r[:, t, :], r[:, t, :], gb[:, 1, :], ALU.add).then_inc(x_ready, 1)
                pool.wait_ge(x_ready, 2 * k + 2)

            pool.wait_ge(tp_done, 8)
            load_ln(ln_mix_g, ln_mix_b, 0)
            ln_bias(0, xres)
            load_ln(ln_ffn_g, ln_ffn_b, 0)
            pool.dma_start(negsel.rearrange("p h m -> p (h m)"), c_negsel).then_inc(fox_loaded, 16)
            pool.dma_start(causal, c_causal).then_inc(fox_loaded, 16)
            pool.dma_start(iota, c_route[:, 0:P]).then_inc(route_loaded, 16)
            pool.dma_start(before, c_route[:, P:2 * P]).then_inc(route_loaded, 16)
            pool.dma_start(w8, c_route[:, 2 * P:2 * P + E]).then_inc(route_loaded, 16)
            pool.dma_start(w_router, router_w[0].rearrange("(k p) n -> p k n", p=P)).then_inc(route_loaded, 16)
            pool.dma_start(w_f, kv_v[:, :, 2 * D:2 * D + FOX_HEADS]).then_inc(route_loaded, 16)
            ln_bias(1, xres)
            load_ln(ln_mix_g, ln_mix_b, 1)
            ln_bias(2, xres)
            load_ln(ln_ffn_g, ln_ffn_b, 1)
            ln_bias(3, yacc)


_INS = ["x", "hg_w_in", "hg_lb_logits", "hg_norm_w", "hg_w_out", "kv_w", "kv_fgate_b", "fox_w_qg", "fox_w_out",
        "ln_mix_g", "ln_mix_b", "ln_ffn_g", "ln_ffn_b", "ffn_w_gu", "ffn_w_down", "moe_w_router", "moe_w_gu",
        "moe_w_down"]


def _constants():
    import numpy as np

    r = np.arange(P)
    square = np.concatenate([np.eye(P), np.ones((P, P))], axis=1).astype(np.float32)
    levels = []
    for half in HALVES:
        same = (r[:, None] // (2 * half)) == (r[None, :] // (2 * half))
        levels.append(same & ((r[:, None] // half) % 2 == 0) & ((r[None, :] // half) % 2 == 1))
    levels.append(r[:, None] == r[None, :])
    levels = np.concatenate(levels, axis=1).astype(np.float32)
    negsel = -np.repeat(np.eye(FOX_HEADS), P, axis=1).astype(np.float32)
    causal = np.concatenate([np.where(r[None, :] <= r[:, None], 0.0, MASKED), np.zeros((P, P)),
                             np.where(r[None, :] <= r[:, None], 0.0, MASKED)], axis=1).astype(np.float32)
    route = np.concatenate([np.broadcast_to(r, (P, P)), r[:, None] < r[None, :],
                            np.broadcast_to(E - np.arange(E), (P, E))], axis=1).astype(np.float32)
    return {"c_square": square, "c_levels": levels, "c_negsel": negsel, "c_causal": causal, "c_route": route}


def kernel(**inputs):
    import numpy as _np
    import concourse.bacc as _bacc
    from concourse import mybir as _mybir
    from concourse.bass_utils import run_bass_kernel_spmd as _run

    nc = _bacc.Bacc("TRN2", target_bir_lowering=False, num_devices=1)
    arrays, args = {}, []
    given = {name: _np.ascontiguousarray(inputs[name]) for name in _INS}
    for name, a in {**given, **_constants()}.items():
        arrays[f"in_{name}_dram"] = a
        args.append(nc.dram_tensor(f"in_{name}_dram", a.shape, _mybir.dt.from_np(a.dtype), kind="ExternalInput").ap())
    args.append(nc.dram_tensor("out_dram", (1, T, D), F32, kind="ExternalOutput").ap())
    build(nc, *args)
    r = _run(nc, [arrays], core_ids=[0])
    return r.results[0]["out_dram"]
```

```python
from contextlib import ExitStack

import concourse.bass as bass
from concourse import mybir

F32 = mybir.dt.float32
F32R = mybir.dt.float32r
I32 = mybir.dt.int32
U8 = mybir.dt.uint8
ALU = mybir.AluOpType
ACT = mybir.ActivationFunctionType
AX_X = mybir.AxisListType.X

P = 128
D = 1024
T = 256
TB = T // P
KT = D // P
N = 512
HG_HEADS = 8
FOX_HEADS = 16
FOX_DIM = 64
FFN = 2816
FFN_TILES = FFN // P
E = 8
F = 3584
CH = F // N
FT = N // P
ALPHA = 4 ** 0.25
LN_EPS = 1e-5
RMS_EPS = 1e-6
LB_FLOOR = 1e-30
LN_SHIFT = 50
LN2 = 0.6931471805599453
MASKED = -1e30
NOT_CHOSEN = 1e6

CORE = 4
SLOT = KT * N
HG_SLOTS = 8
S_HG_OUT = HG_SLOTS
S_GU = S_HG_OUT + 2
FFN_CH = 11
S_DOWN = S_GU + FFN_CH
DOWN_SLOTS = 6
S_KVQG = S_DOWN + DOWN_SLOTS
S_FOX_OUT = S_KVQG + 8
S_MOE = S_FOX_OUT + 2
MOE_PLACES = [CORE, S_MOE % CORE, (S_MOE + 1) % CORE, CORE + 1, CORE + 2, (S_MOE + 2) % CORE, (S_MOE + 3) % CORE]
MOE_RING = len(MOE_PLACES)

PC = 1024
BUFS = 4
MOE_SLOTS = 3 * CH
assert MOE_SLOTS % MOE_RING == 0
MOE_ORDER = [("a", 0), ("b", 0)]
for _c in range(1, CH):
    MOE_ORDER += [("a", _c), ("b", _c), ("d", _c - 1)]
MOE_ORDER += [("d", CH - 1)]
MOE_PIECES = 4 * MOE_SLOTS
assert MOE_PIECES % BUFS == 0


def moe_end(kind, c):
    return 4 * (MOE_ORDER.index((kind, c)) + 1)



HALVES = [64, 32, 16, 8, 4, 2, 1]
LEVELS = len(HALVES) + 1
BUF_LEVELS = len(HALVES) + 1


class Steps:

    def __init__(self, eng, sem, start=0):
        self.eng, self.sem, self.n = eng, sem, start

    def __call__(self, ins):
        ins.then_inc(self.sem, 1)
        self.n += 1
        self.eng.wait_ge(self.sem, self.n)

    def note(self, ins):
        ins.then_inc(self.sem, 1)
        self.n += 1


def build(nc, x, w_in, lb_logits, norm_w, w_out, kv_w, fgate_b, fox_qg, fox_out, ln_mix_g, ln_mix_b,
          ln_ffn_g, ln_ffn_b, ffn_gu, ffn_down, router_w, moe_gu, moe_down,
          c_square, c_levels, c_negsel, c_causal, c_route, out):
    with ExitStack() as ctx:
        def sb(name, shape, dt=F32):
            return ctx.enter_context(nc.sbuf_tensor(name, shape, dt))

        def sem(name):
            return ctx.enter_context(nc.semaphore(name))

        ARENA = 53000
        arena = sb("arena", [P, ARENA])
        arena_at = int(nc.sbuf_base) - 4 * ARENA

        def at(name, col, cols, dt=F32, rows=P):
            return nc.alloc_sbuf_tensor_at(name, [rows, cols], dt, offset=arena_at + 4 * col)

        xres = at("xres", 0, TB * D)[:, :].rearrange("p (t n) -> p t n", t=TB)
        gb = at("gb", 2048, 2 * D)[:, :].rearrange("p (t n) -> p t n", t=2)
        xT = at("xT", 4096, KT * T)[:, :].rearrange("p (k t) -> p k t", k=KT)
        sq = at("sq", 8192, 2 * P)[:, :]
        level_mask = at("level_mask", 8448, LEVELS * P, U8)[:, :].rearrange("p (l n) -> p l n", l=LEVELS)
        sm = at("sm", 8704, 96)[:, :]
        fgb = at("fgb", 8800, 1, rows=FOX_HEADS)[:, :]
        itf = at("itf", 8808, 40, rows=1)[:, :]
        items = at("items", 8856, 17, I32, rows=1)[:, :]
        wh = [at(f"wh{n}", 8904 + 2 * PC * n, PC, F32R) for n in range(BUFS)]
        wl = [at(f"wl{n}", 8904 + 2 * PC * n + PC, PC, F32R) for n in range(BUFS)]
        CORE_AT = 8904 + 2 * PC * BUFS
        A_AT = CORE_AT + CORE * SLOT
        A = at("scratch", A_AT, ARENA - A_AT)[:, :]
        places = [at(f"place{n}", CORE_AT + n * SLOT, SLOT) for n in range(CORE)]
        places += [at("place4", ARENA - SLOT, SLOT), at("place5", A_AT, SLOT), at("place6", A_AT + SLOT, SLOT)]

        ident = sq[:, 0:P]
        ones = sq[:, P:2 * P]
        ps = ctx.enter_context(nc.psum_tensor("ps", [P, 8, N], F32))

        def bank(n, cols=N):
            return ps[:, n, 0:cols]

        zb = A[:, 0:2048]
        hq = A[:, 2048:4096]
        hk = A[:, 4096:6144]
        hv = A[:, 6144:8192].rearrange("p (t n) -> p t n", t=TB)
        hg = A[:, 8192:10240].rearrange("p (t n) -> p t n", t=TB)
        ph_l, ph_a = A[:, 8192:9216], A[:, 9216:10240]
        lev_e = [A[:, 10240:11264], A[:, 11264:12288]]
        lev_q = [A[:, 12288:13312], A[:, 13312:14336]]
        lev_k = [A[:, 14336:15360], A[:, 15360:16384]]
        scT = A[:, 16384:17408]
        khatT = lev_k[0][:, 0:N]
        state = lev_q[0][:, 0:N]
        ho = gb
        lbt = sm[:, 0:8]
        one_m_lb = sm[:, 8:16]
        loglb = sm[:, 16:24]
        nloglb = sm[:, 24:32]
        ssq = sm[:, 32:48].rearrange("p (t h) -> p t h", t=TB)
        stats = sm[:, 48:72].rearrange("p (t n s) -> p t n s", t=TB, n=2)
        mv = sm[:, 72:76].rearrange("p (t s) -> p t s", t=TB)
        std = sm[:, 76:78]
        normw = A[:, 17408:17536]

        hT = A[:, 0:FFN_TILES * T].rearrange("p (f t) -> p f t", f=FFN_TILES)
        ffn_s = [A[:, 11264:11520], A[:, 11520:11776]]

        fk = A[:, 0:2048].rearrange("p (c t) -> p c t", t=T)
        fq = A[:, 2048:4096].rearrange("p (c t) -> p c t", t=T)
        fv = A[:, 4096:6144].rearrange("p (t n) -> p t n", t=TB)
        fg = A[:, 6144:8192].rearrange("p (t n) -> p t n", t=TB)
        fo = A[:, 8192:10240].rearrange("p (t n) -> p t n", t=TB)
        KW = 3 * P
        flog = [A[:, 10240:10240 + KW], A[:, 10624:10624 + KW]]
        fprob = [A[:, 11008:11008 + KW], A[:, 11392:11392 + KW]]
        fprobT = [A[:, 11776:11776 + KW], A[:, 12160:12160 + KW]]
        causal = A[:, 12544:12544 + KW]
        fz = A[0:FOX_HEADS, 12928:13184]
        fl = A[0:FOX_HEADS, 13184:13440]
        fc = A[0:FOX_HEADS, 13440:13696]
        nmax = A[:, 13696:13728]
        rsum = A[:, 13728:13760]
        rinv = A[:, 13760:13792]
        cT = A[:, 13792:13824].rearrange("p (t h) -> p t h", t=TB)
        iota = A[:, 13824:13952]
        before = A[:, 13952:14080]
        w8 = A[:, 14080:14088]
        w_router = A[:, 14088:14152].rearrange("p (k n) -> p k n", k=KT)
        w_f = A[:, 14152:14280].rearrange("p (k n) -> p k n", k=KT)
        negsel = A[0:FOX_HEADS, 14664:14680]

        x3h = at("x3h", 2048, TB * D, F32R)[:, :].rearrange("p (t n) -> p t n", t=TB)
        x3l = at("x3l", 0, TB * D, F32R)[:, :].rearrange("p (t n) -> p t n", t=TB)
        xeh = at("xeh", 4096, KT * P, F32R)[:, :].rearrange("p (k t) -> p k t", k=KT)
        xel = at("xel", 5120, KT * P, F32R)[:, :].rearrange("p (k t) -> p k t", k=KT)
        ehTh, ehTl = at("ehTh", 6144, N, F32R), at("ehTl", 6656, N, F32R)
        last_gain = at("last_gain", 7168, D)[:, :]
        yacc = A[:, 8192:10240].rearrange("p (t n) -> p t n", t=TB)
        ye = A[:, 10240:11264].rearrange("p (n c) -> p n c", n=2)
        gate_s = A[:, 11264:11776]
        pick = at("pick", A_AT + 11776, TB * P, F32R)[:, :].rearrange("p (t n) -> p t n", t=TB)
        pickw = A[:, 12032:12288].rearrange("p (t n) -> p t n", t=TB)
        last_bias = A[:, 12288:13312]
        eh = A[:, 13312:13824]
        rt = [A[:, 14680 + 16 * n:14696 + 16 * n] for n in range(12)]
        rank2 = A[:, 14872:14904].rearrange("p (t c) -> p t c", t=TB)
        comb2 = A[:, 14904:14936].rearrange("p (t c) -> p t c", t=TB)
        cur = A[:, 14936:14940]
        spread_all = A[:, 14944:15200]
        spread = spread_all.rearrange("p (t n) -> p t n", t=TB)

        w_ready = [sem(f"w_ready{r}") for r in range(len(places))]
        levels_loaded, mask_ready = sem("levels_loaded"), sem("mask_ready")
        consts_loaded, x_loaded, small_loaded = sem("consts_loaded"), sem("x_loaded"), sem("small_loaded")
        normw_loaded, gb_loaded, fox_loaded, route_loaded = (sem("normw_loaded"), sem("gb_loaded"),
                                                             sem("fox_loaded"), sem("route_loaded"))
        tp_done, tp_dve, tp_act = sem("tp_done"), sem("tp_copied_dve"), sem("tp_copied_act")
        pj_done, pj_out = sem("proj_done"), sem("proj_copied")
        lb_ready, loglb_ready, lb_exp = sem("lb_ready"), sem("loglb_ready"), sem("lb_exp")
        act_steps, dve_steps = sem("act_steps"), sem("dve_steps")
        sp_log, sp_sum, rlog_ready, kexp_ready, b_ready = (sem("softplus_log"), sem("softplus_sum"),
                                                          sem("floor_log"), sem("k_exp"), sem("b_ready"))
        q_ready, floor_max = sem("q_ready"), sem("floor_max")
        diff_ready, exp_ready, qt_ready, kt_ready = (sem("diff_ready"), sem("exp_ready"), sem("qt_ready"),
                                                     sem("kt_ready"))
        sc_done, sc_sel = sem("scores_done"), sem("scores_selected")
        at_done, at_out = sem("attn_done"), sem("attn_copied")
        sq_ready, ms_ready, rms_ready, gn_ready, on_ready = (sem("squares"), sem("mean_squares"), sem("rms"),
                                                             sem("gate_norm"), sem("hgrn_out"))
        hg_silu = sem("hgrn_gate_silu")
        y_done = sem("y_done")
        ln_var, ln_std, x_ready = sem("ln_var"), sem("ln_std"), sem("x_ready")
        ffn_done, ffn_silu, ffn_h, ffn_down_used = (sem("ffn_done"), sem("ffn_silu"), sem("ffn_h"),
                                                    sem("ffn_down_used"))
        f_log, c_ready, cT_done, cT_ready = sem("f_log"), sem("c_ready"), sem("cT_done"), sem("cT_ready")
        fx_qk, fx_max, fx_exp, fx_pt, fx_ptc, fx_pv, fx_out = (sem("fox_qk"), sem("fox_max"), sem("fox_exp"),
                                                              sem("fox_pT"), sem("fox_pT_copied"),
                                                              sem("fox_pv"), sem("fox_out"))
        fg_sig, og_ready = sem("fox_gate_sigmoid"), sem("fox_gated")
        lg_done, e2_in, e2_out, sel_ready, rk_done, pick_ready = (
            sem("router_logits"), sem("top2_difference"), sem("top2_exp"), sem("chosen_ready"),
            sem("ranks_done"), sem("pick_ready"))
        items_ready = sem("items_ready")
        x3_hi, x3_ready = sem("x3_hi"), sem("x3_ready")
        ga_done, xe_hi, xe_ready = sem("gather_done"), sem("xe_hi"), sem("xe_ready")
        hi_ready, lo_ready, pieces_used = sem("hi_ready"), sem("lo_ready"), sem("pieces_used")
        silu_done, h_ready = sem("silu_done"), sem("h_ready")
        htr_done, hT_hi, hT_ready = sem("hT_done"), sem("hT_hi"), sem("hT_ready")
        spr_done, spr_ready, ye_ready = sem("spread_done"), sem("spread_copied"), sem("ye_copied")
        sc2_done, yacc_up = sem("scatter_done"), sem("yacc_updates")
        dve_item = sem("dve_item_steps")
        dve_tail, out_done = sem("dve_tail_steps"), sem("out_done")

        w_in_v = w_in[0].rearrange("(k p) n -> p k n", p=P)
        w_out_v = w_out[0].rearrange("(k p) n -> p k n", p=P)
        gu_v = ffn_gu[0].rearrange("(k p) n -> p k n", p=P)
        down_v = ffn_down[0].rearrange("(f p) n -> p f n", p=P)
        kv_v = kv_w.rearrange("(k p) n -> p k n", p=P)
        qg_v = fox_qg[0].rearrange("(k p) n -> p k n", p=P)
        fo_v = fox_out[0].rearrange("(k p) n -> p k n", p=P)

        def slot(s):
            return places[s % CORE][:, :]

        def slot_k(s):
            return slot(s).rearrange("p (k n) -> p k n", k=KT)

        def loads_of(s):
            if s < S_HG_OUT:
                col = [1, 0, 2, 1, 0, 2, 3, 3][s] * D + [0, 0, 0, 1, 1, 1, 0, 1][s] * N
                return [(slot_k(s), w_in_v[:, :, col:col + N])]
            if s < S_GU:
                n = s - S_HG_OUT
                return [(slot_k(s), w_out_v[:, :, n * N:(n + 1) * N])]
            if s < S_DOWN:
                c = s - S_GU
                half = slot(s).rearrange("p (h k n) -> p h k n", h=2, k=KT)
                return [(half[:, h], gu_v[:, :, h * FFN + c * T:h * FFN + (c + 1) * T]) for h in range(2)]
            if s < S_KVQG:
                f0 = (s - S_DOWN) * FT
                f1 = min(f0 + FT, FFN_TILES)
                return [(slot(s)[:, 0:(f1 - f0) * D].rearrange("p (f n) -> p f n", n=D), down_v[:, f0:f1, :])]
            if s < S_FOX_OUT:
                n = s - S_KVQG
                src = [kv_v, kv_v, qg_v, qg_v, kv_v, kv_v, qg_v, qg_v][n]
                col = [0, N, 0, N, D, D + N, D, D + N][n]
                return [(slot_k(s), src[:, :, col:col + N])]
            n = s - S_FOX_OUT
            return [(slot_k(s), fo_v[:, :, n * N:(n + 1) * N])]

        filled = [0] * len(places)
        ready_at = []
        for s in range(S_MOE):
            filled[s % CORE] += 16 * len(loads_of(s))
            ready_at.append(filled[s % CORE])

        def slot_landed(pe, s):
            pe.wait_ge(w_ready[s % CORE], ready_at[s])

        FOX_TILE0 = 24

        def slot_read(s):
            if s < S_HG_OUT:
                return pj_done, [4, 8, 10, 14, 18, 20, 22, 24][s]
            if s < S_GU:
                return y_done, 2 * (s - S_HG_OUT) + 2
            if s < S_DOWN:
                return ffn_done, 2 * (s - S_GU) + 2
            if s < S_KVQG - 1:
                return ffn_down_used, s - S_DOWN + 1
            if s == S_KVQG - 1:
                return y_done, 8
            if s < S_FOX_OUT:
                return pj_done, FOX_TILE0 + 1 + [4, 8, 12, 16, 18, 20, 22, 24][s - S_KVQG]
            return y_done, 8 + 2 * (s - S_FOX_OUT) + 2

        def moe_place(j):
            return MOE_PLACES[j % MOE_RING]

        def moe_slot(j):
            return places[moe_place(j)][:, :]

        def moe_slot_landed(eng, i, j):
            eng.wait_ge(w_ready[moe_place(j)],
                        i * (16 * MOE_SLOTS // MOE_RING) + filled[moe_place(j)] + 16 * (j // MOE_RING + 1))

        def moe_load(sp, e, j):
            kind, c = MOE_ORDER[j]
            if kind == "d":
                src = moe_down[0, e, c * N:(c + 1) * N, :].rearrange("(f p) n -> p f n", p=P)
                dst = moe_slot(j).rearrange("p (f n) -> p f n", n=D)
            else:
                col = c * N + (F if kind == "b" else 0)
                src = moe_gu[0, e, :, col:col + N].rearrange("(k p) n -> p k n", p=P)
                dst = moe_slot(j).rearrange("p (k n) -> p k n", k=KT)
            sp.dma_start(dst, src).then_inc(w_ready[moe_place(j)], 16)

        block = ctx.enter_context(nc.Block())

        @block.sync
        def _(sp):
            sp.dma_start(xres[:, :, :], x[0].rearrange("(t p) n -> p t n", p=P)).then_inc(x_loaded, 16)
            for s in range(S_MOE):
                if s >= CORE:
                    sp.wait_ge(*slot_read(s - CORE))
                for dst, src in loads_of(s):
                    sp.dma_start(dst, src).then_inc(w_ready[s % CORE], 16)
            for j in range(MOE_RING):
                if moe_place(j) < CORE:
                    last = [s for s in range(S_MOE) if s % CORE == moe_place(j)][-1]
                    sp.wait_ge(*slot_read(last))
                elif moe_place(j) > CORE:
                    sp.wait_ge(tp_done, 20)
                moe_load(sp, 0, j)

            def rest_of(i, e):
                for j in range(MOE_RING, MOE_SLOTS):
                    sp.wait_ge(lo_ready, i * MOE_PIECES + 4 * (j - MOE_RING + 1))
                    moe_load(sp, e, j)

            def first_of(i, e):
                for j in range(MOE_RING):
                    sp.wait_ge(lo_ready, i * MOE_PIECES - 4 * (MOE_RING - j - 1))
                    moe_load(sp, e, j)

            with sp.Fori(0, E - 1) as i:
                rest_of(i, i)
                first_of(i + 1, i + 1)
            rest_of(E - 1, E - 1)
            sp.wait_ge(items_ready, 2)
            more = sp.value_load(items[0:1, 16:17], min_val=0, max_val=3)
            with sp.If(more > 0):
                with sp.Fori(0, more) as n:
                    col = sp.value_load(items[0:1, bass.ds(n + E, 1)], min_val=E, max_val=2 * E - 1)
                    first_of(n + E, col - E)
                    rest_of(n + E, col - E)
            for t in range(TB):
                sp.wait_ge(x_ready, 12 + 2 * (t + 1))
                sp.dma_start(out[0, t * P:(t + 1) * P, :], yacc[:, t, :]).then_inc(out_done, 16)
            sp.wait_ge(out_done, 16 * TB)

        @block.tensor
        def _(pe):
            def transpose_rows(stage, src, ready):
                for g in range(2 * TB):
                    t, half = divmod(g, 2)
                    pe.wait_ge(*ready(t, half))
                    if t:
                        pe.wait_ge((tp_dve, tp_act)[half], 2 * stage + 1)
                    for j in range(4):
                        k = 4 * half + j
                        mm = pe.transpose(ps[:, 6 + half, j * P:(j + 1) * P], src[:, t, k * P:(k + 1) * P], ident)
                    mm.then_inc(tp_done, 1)

            def xT_ready(stage):
                pe.wait_ge(tp_dve, 2 * stage + 2)
                pe.wait_ge(tp_act, 2 * stage + 2)

            def proj_bank(n):
                if n >= 2:
                    pe.wait_ge(pj_out, n - 1)
                return n % 2

            def feature_tile(n, s, col, width=P):
                b = proj_bank(n)
                w = slot_k(s)
                for k in range(KT):
                    mm = pe.matmul(ps[0:width, b, 0:T], w[:, k, col:col + width], xT[:, k, :],
                                   start=(k == 0), stop=(k == KT - 1))
                mm.then_inc(pj_done, 1)

            def token_tile(n, s, t):
                b = proj_bank(n)
                w = slot_k(s)
                for k in range(KT):
                    mm = pe.matmul(bank(b), xT[:, k, t * P:(t + 1) * P], w[:, k, :],
                                   start=(k == 0), stop=(k == KT - 1))
                mm.then_inc(pj_done, 1)

            def hg_tile(n):
                s, j = [(0, 0), (0, 1), (0, 2), (0, 3), (1, 0), (1, 1), (1, 2), (1, 3), (2, 0), (2, 1),
                        (3, 0), (3, 1), (3, 2), (3, 3), (4, 0), (4, 1), (4, 2), (4, 3), (5, 0), (5, 1),
                        (6, 0), (6, 1), (7, 0), (7, 1)][n]
                if j == 0:
                    slot_landed(pe, s)
                if s in (0, 1, 3, 4):
                    feature_tile(n, s, j * P)
                else:
                    token_tile(n, s, j)

            def level(g, l):
                m, c = BUF_LEVELS * g + l, LEVELS * g + l
                if l < len(HALVES):
                    pe.wait_ge(qt_ready, m + 1)
                    pe.wait_ge(kt_ready, m + 1)
                    kk, qq = lev_k[m % 2], lev_q[m % 2]
                else:
                    kk, qq = hk[:, g * 1024:(g + 1) * 1024], hq[:, g * 1024:(g + 1) * 1024]
                if c >= 2:
                    pe.wait_ge(sc_sel, 2 * (c - 1))
                for h in range(2):
                    b = 2 + 2 * (c % 2) + h
                    for u in range(4):
                        cols = slice((4 * h + u) * P, (4 * h + u + 1) * P)
                        mm = pe.matmul(ps[:, b, u * P:(u + 1) * P], kk[:, cols], qq[:, cols],
                                       start=True, stop=True)
                    mm.then_inc(sc_done, 1)

            def attend_state(g):
                if g:
                    pe.wait_ge(at_out, 4 * g)
                pe.wait_ge(kt_ready, BUF_LEVELS * (g + 1))
                kk = lev_k[1]
                for h in range(4):
                    mm = pe.transpose(ps[:, 6, h * P:(h + 1) * P], kk[:, 2 * h * P:(2 * h + 1) * P], ident)
                mm.then_inc(at_done, 1)

            def attend(g):
                pe.wait_ge(at_out, 4 * g + 1)
                pe.wait_ge(pj_out, 10 + 10 * g)
                for h in range(4):
                    mm = pe.matmul(ps[:, 7, h * P:(h + 1) * P], khatT[:, h * P:(h + 1) * P],
                                   hv[:, 0, (4 * g + h) * P:(4 * g + h + 1) * P], start=True, stop=True)
                mm.then_inc(at_done, 1)
                pe.wait_ge(sc_sel, 2 * LEVELS * (g + 1))
                for h in range(4):
                    mm = pe.matmul(ps[:, 6, h * P:(h + 1) * P], scT[:, 2 * h * P:(2 * h + 1) * P],
                                   hv[:, 0, (4 * g + h) * P:(4 * g + h + 1) * P], start=True, stop=True)
                mm.then_inc(at_done, 1)
                pe.wait_ge(at_out, 4 * g + 2)
                pe.wait_ge(qt_ready, BUF_LEVELS * (g + 1))
                qq = lev_q[1]
                for h in range(4):
                    pe.matmul(ps[:, 7, h * P:(h + 1) * P], scT[:, (2 * h + 1) * P:(2 * h + 2) * P],
                              hv[:, 1, (4 * g + h) * P:(4 * g + h + 1) * P], start=True, stop=False)
                    mm = pe.matmul(ps[:, 7, h * P:(h + 1) * P], qq[:, (2 * h + 1) * P:(2 * h + 2) * P],
                                   state[:, h * P:(h + 1) * P], start=False, stop=True)
                mm.then_inc(at_done, 1)

            def out_projection(s0):
                for n in range(2):
                    slot_landed(pe, s0 + n)
                    w = slot_k(s0 + n)
                    for t in range(TB):
                        for k in range(KT):
                            mm = pe.matmul(bank(2 + 2 * n + t), xT[:, k, t * P:(t + 1) * P], w[:, k, :],
                                           start=(k == 0), stop=(k == KT - 1))
                        mm.then_inc(y_done, 1)

            pe.wait_ge(consts_loaded, 16)
            transpose_rows(0, xres, lambda t, half: (x_loaded, 16))
            xT_ready(0)
            for n in range(10):
                hg_tile(n)
            for l in range(LEVELS):
                hg_tile(10 + l)
                if l == LEVELS - 1:
                    pe.wait_ge(q_ready, 1)
                    pe.wait_ge(b_ready, 1)
                level(0, l)
            attend_state(0)
            hg_tile(18)
            attend(0)
            hg_tile(19)
            hg_tile(20)
            for n, levels in ((21, (0,)), (22, (1, 2)), (23, (3, 4, 5, 6, 7))):
                hg_tile(n)
                for l in levels:
                    if l == LEVELS - 1:
                        pe.wait_ge(q_ready, 2)
                        pe.wait_ge(b_ready, 2)
                    level(1, l)
            attend_state(1)
            attend(1)
            transpose_rows(1, ho, lambda t, half: (on_ready, t + 1))
            xT_ready(1)
            out_projection(S_HG_OUT)

            transpose_rows(2, xres, lambda t, half: (x_ready, 2 * t + half + 1))
            xT_ready(2)
            for c in range(FFN_CH):
                s = S_GU + c
                slot_landed(pe, s)
                w = slot(s).rearrange("p (h k n) -> p h k n", h=2, k=KT)
                for j in range(2):
                    f = 2 * c + j
                    if f >= 2:
                        pe.wait_ge(ffn_h, f - 1)
                    for h in range(2):
                        for k in range(KT):
                            mm = pe.matmul(ps[:, f % 2, h * T:(h + 1) * T], w[:, h, k, j * P:(j + 1) * P],
                                           xT[:, k, :], start=(k == 0), stop=(k == KT - 1))
                    mm.then_inc(ffn_done, 1)
            for f in range(FFN_TILES):
                s = S_DOWN + f // FT
                if f % FT == 0:
                    slot_landed(pe, s)
                pe.wait_ge(ffn_h, f + 1)
                w = slot(s).rearrange("p (f n) -> p f n", n=D)
                for t in range(TB):
                    for n in range(2):
                        mm = pe.matmul(bank(2 + 2 * n + t), hT[:, f, t * P:(t + 1) * P],
                                       w[:, f % FT, n * N:(n + 1) * N],
                                       start=(f == 0), stop=(f == FFN_TILES - 1))
                        if f == FFN_TILES - 1:
                            mm.then_inc(y_done, 1)
                if f % FT == FT - 1:
                    mm.then_inc(ffn_down_used, 1)

            transpose_rows(3, xres, lambda t, half: (x_ready, 4 + 2 * t + half + 1))
            xT_ready(3)
            pe.wait_ge(route_loaded, 80)
            for k in range(KT):
                mm = pe.matmul(ps[0:FOX_HEADS, 0, 0:T], w_f[:, k, :], xT[:, k, :],
                               start=(k == 0), stop=(k == KT - 1))
            mm.then_inc(pj_done, 1)
            for n in range(16):
                s = S_KVQG + n // 4
                if n % 4 == 0:
                    slot_landed(pe, s)
                feature_tile(FOX_TILE0 + 1 + n, s, (n % 4) * P)

            def fox_token_tile(n):
                s = S_KVQG + 4 + n // 2
                if n % 2 == 0:
                    slot_landed(pe, s)
                token_tile(FOX_TILE0 + 17 + n, s, n % 2)

            fox_token_tile(0)
            fox_token_tile(1)
            pe.wait_ge(c_ready, 1)
            for t in range(TB):
                mm = pe.transpose(ps[:, 6, t * FOX_HEADS:(t + 1) * FOX_HEADS], fc[:, t * P:(t + 1) * P],
                                  sq[0:FOX_HEADS, 0:FOX_HEADS])
            mm.then_inc(cT_done, 1)
            pe.wait_ge(fox_loaded, 32)

            def fox_scores(h):
                if h >= 2:
                    pe.wait_ge(fx_max, h - 1)
                if h == 0:
                    pe.wait_ge(pj_out, FOX_TILE0 + 17)
                rows = slice((h % 2) * 64, (h % 2) * 64 + 64)
                for t in range(TB):
                    dst = ps[:, 2 + h % 2, t * P:t * P + (t + 1) * P]
                    pe.matmul(dst, negsel[:, h:h + 1].to_broadcast([FOX_HEADS, P]), fc[:, 0:(t + 1) * P], start=True, stop=False)
                    mm = pe.matmul(dst, fq[rows, h // 2, t * P:(t + 1) * P], fk[rows, h // 2, 0:(t + 1) * P],
                                   start=False, stop=True)
                mm.then_inc(fx_qk, 1)

            def fox_turn(h):
                pe.wait_ge(fx_exp, h + 1)
                if h >= 2:
                    pe.wait_ge(fx_ptc, h - 1)
                for j in range(3):
                    mm = pe.transpose(ps[:, 4 + h % 2, j * P:(j + 1) * P], fprob[h % 2][:, j * P:(j + 1) * P], ident)
                mm.then_inc(fx_pt, 1)

            def fox_values(h):
                pe.wait_ge(fx_ptc, h + 1)
                if h == 0:
                    pe.wait_ge(cT_ready, 1)
                    pe.wait_ge(pj_out, FOX_TILE0 + 19)
                if h == 8:
                    pe.wait_ge(pj_out, FOX_TILE0 + 21)
                if h >= 2:
                    pe.wait_ge(fx_out, h - 1)
                cols = slice(h * FOX_DIM, (h + 1) * FOX_DIM)
                pT = fprobT[h % 2]
                pe.matmul(ps[:, 6 + h % 2, 0:64], pT[:, 0:P], fv[:, 0, cols], start=True, stop=True)
                pe.matmul(ps[:, 6 + h % 2, 64:128], pT[:, P:2 * P], fv[:, 0, cols], start=True, stop=False)
                pe.matmul(ps[:, 6 + h % 2, 64:128], pT[:, 2 * P:3 * P], fv[:, 1, cols], start=False,
                          stop=True).then_inc(fx_pv, 1)

            for h in range(FOX_HEADS + 2):
                if h < FOX_HEADS:
                    fox_scores(h)
                if 1 <= h <= FOX_HEADS:
                    fox_turn(h - 1)
                if h >= 2:
                    fox_values(h - 2)
                if h % 2 == 1 and h < 12:
                    fox_token_tile(2 + h // 2)
            transpose_rows(4, fo, lambda t, half: (og_ready, t + 1))
            xT_ready(4)
            out_projection(S_FOX_OUT)

            transpose_rows(5, xres, lambda t, half: (x_ready, 8 + 2 * t + half + 1))
            xT_ready(5)
            for t in range(TB):
                for k in range(KT):
                    mm = pe.matmul(ps[:, 0, t * E:(t + 1) * E], xT[:, k, t * P:(t + 1) * P], w_router[:, k, :],
                                   start=(k == 0), stop=(k == KT - 1))
            mm.then_inc(lg_done, 1)
            pe.wait_ge(sel_ready, 1)
            sel = rt[8]
            pe.matmul(ps[:, 1, 0:E], before, sel[:, 0:E], start=True, stop=True)
            pe.matmul(ps[:, 1, E:2 * E], ones, sel[:, 0:E], start=True, stop=False)
            pe.matmul(ps[:, 1, E:2 * E], before, sel[:, E:2 * E], start=False, stop=True)
            pe.matmul(ps[0:1, 1, 2 * E:3 * E], ones[:, 0:1], sel[:, 0:E], start=True, stop=False)
            pe.matmul(ps[0:1, 1, 2 * E:3 * E], ones[:, 0:1], sel[:, E:2 * E], start=False,
                      stop=True).then_inc(rk_done, 1)

            def gather(i, half):
                if half == 0:
                    pe.wait_ge(pick_ready, i + 1)
                for j in range(4):
                    k = 4 * half + j
                    for t in range(TB):
                        for part in (x3h, x3l):
                            mm = pe.matmul(ps[:, 7 - half, j * P:(j + 1) * P], part[:, t, k * P:(k + 1) * P],
                                           pick[:, t, :], start=(t == 0 and part is x3h),
                                           stop=(t == TB - 1 and part is x3l))
                mm.then_inc(ga_done, 1)

            def three_products(dst, xh, xl, piece, cols, start, stop):
                h, l = wh[piece % BUFS][:, cols], wl[piece % BUFS][:, cols]
                pe.matmul(dst, xh, h, start=start, stop=False)
                pe.matmul(dst, xh, l, start=False, stop=False)
                return pe.matmul(dst, xl, h, start=False, stop=stop)

            def gate_or_up(i, c, kind):
                b = 2 * (c % 2) + (kind == "b")
                for k in range(KT):
                    piece = 4 * MOE_ORDER.index((kind, c)) + k // 2
                    if k % 2 == 0:
                        pe.wait_ge(lo_ready, i * MOE_PIECES + piece + 1)
                    cols = slice((k % 2) * N, (k % 2 + 1) * N)
                    mm = three_products(bank(b), xeh[:, k, :], xel[:, k, :], piece, cols, k == 0, k == KT - 1)
                    if k % 2:
                        mm.then_inc(pieces_used, 1)

            def turn_h(i, c):
                pe.wait_ge(h_ready, i * CH + c + 1)
                for f in range(FT):
                    mm = pe.transpose(ps[:, 6, f * P:(f + 1) * P], eh[:, f * P:(f + 1) * P], ident)
                mm.then_inc(htr_done, 1)

            def down(i, c):
                pe.wait_ge(hT_ready, i * CH + c + 1)
                for f in range(FT):
                    piece = 4 * MOE_ORDER.index(("d", c)) + f
                    pe.wait_ge(lo_ready, i * MOE_PIECES + piece + 1)
                    rows = slice(f * P, (f + 1) * P)
                    for n in range(2):
                        mm = three_products(bank(4 + n), ehTh[:, rows], ehTl[:, rows], piece,
                                            slice(n * N, (n + 1) * N), c == 0 and f == 0,
                                            c == CH - 1 and f == FT - 1)
                    mm.then_inc(pieces_used, 1)

            def item(i):
                pe.wait_ge(xe_ready, 2 * i + 2)
                gate_or_up(i, 0, "a")
                gate_or_up(i, 0, "b")
                pe.wait_ge(yacc_up, 4 * i + 2)
                for t in range(TB):
                    mm = pe.transpose(ps[:, 6, t * P:(t + 1) * P], pickw[:, t, :], ident)
                mm.then_inc(spr_done, 1)
                for c in range(1, CH):
                    gate_or_up(i, c, "a")
                    if c == 1:
                        pe.wait_ge(spr_ready, i + 1)
                    turn_h(i, c - 1)
                    gate_or_up(i, c, "b")
                    down(i, c - 1)
                turn_h(i, CH - 1)
                gather(i + 1, 0)
                down(i, CH - 1)
                gather(i + 1, 1)
                for n in range(2):
                    for t in range(TB):
                        pe.wait_ge(ye_ready, 2 * i + n + 1)
                        if n == 0:
                            pe.wait_ge(xe_ready, 2 * i + 3 + t)
                        pe.matmul(bank([7, 6, 2, 3][2 * n + t]), spread[:, t, :], ye[:, n, :], start=True,
                                  stop=True).then_inc(sc2_done, 1)

            pe.wait_ge(x3_ready, TB)
            gather(0, 0)
            gather(0, 1)
            with pe.Fori(0, E) as i:
                item(i)
            more = pe.value_load(items[0:1, 16:17], min_val=0, max_val=3)
            with pe.If(more > 0):
                with pe.Fori(0, more) as n:
                    item(n + E)

        @block.scalar
        def _(act):
            step = Steps(act, act_steps)

            def turned(stage):
                for t in range(TB):
                    act.wait_ge(tp_done, 4 * stage + 2 * t + 2)
                    act.activation(xT[:, 4:8, t * P:(t + 1) * P],
                                   bank(7).rearrange("p (k t) -> p k t", k=4), ACT.Copy).then_inc(tp_act, 1)

            def copy_tile(n, dst, scale=1.0, cols=N):
                act.wait_ge(pj_done, n + 1)
                act.activation(dst, bank(n % 2, cols), ACT.Copy, scale=scale).then_inc(pj_out, 1)

            act.dma_start(sq[:, :], c_square).then_inc(consts_loaded, 16)
            act.dma_start(lev_k[0], c_levels).then_inc(levels_loaded, 16)
            act.wait_ge(lb_ready, 1)
            act.activation(lbt, sm[:, 32:40], ACT.Exp).then_inc(lb_exp, 1)
            act.wait_ge(lb_ready, 2)
            step(act.activation(loglb, sm[:, 40:48], ACT.Ln, scale=2.0 ** LN_SHIFT))
            act.activation(loglb, loglb, ACT.Copy, bias=-LN_SHIFT * LN2).then_inc(loglb_ready, 1)
            turned(0)

            def hg_copy(n):
                if n in (0, 1, 2, 3, 10, 11, 12, 13):
                    h = n if n < 4 else n - 6
                    copy_tile(n, zb[:, h * T:(h + 1) * T], cols=T)
                elif n in (4, 5, 6, 7, 14, 15, 16, 17):
                    h = n - 4 if n < 8 else n - 10
                    copy_tile(n, hq[:, h * T:(h + 1) * T], cols=T)
                elif n < 20:
                    t, g = n % 2, n // 18
                    copy_tile(n, hv[:, t, g * N:(g + 1) * N])
                else:
                    t, g = n % 2, (n - 20) // 2
                    copy_tile(n, hg[:, t, g * N:(g + 1) * N])

            def log_gates_a(g):
                z = zb[:, g * 1024:(g + 1) * 1024]
                act.wait_ge(pj_out, 4 + 10 * g)
                if g:
                    act.wait_ge(b_ready, 1)
                step(act.activation(ph_l, z, ACT.Abs))
                step(act.activation(ph_l, ph_l, ACT.Exp, scale=-1.0))
                act.activation(ph_l, ph_l, ACT.Ln, bias=1.0).then_inc(sp_log, 1)

            def log_gates_b(g):
                k = hk[:, g * 1024:(g + 1) * 1024]
                act.wait_ge(sp_sum, g + 1)
                for h in range(4):
                    ins = act.activation(ph_l[:, h * T:(h + 1) * T], zb[:, (4 * g + h) * T:(4 * g + h + 1) * T],
                                         ACT.Abs, bias=nloglb[:, 4 * g + h:4 * g + h + 1])
                step(ins)
                step(act.activation(ph_l, ph_l, ACT.Exp, scale=-1.0))
                act.activation(ph_l, ph_l, ACT.Ln, bias=1.0).then_inc(rlog_ready, 1)
                act.wait_ge(floor_max, g + 1)
                act.activation(k, k, ACT.Exp, scale=-1.0).then_inc(kexp_ready, 1)

            def silu_q(g):
                act.wait_ge(pj_out, 8 + 10 * g)
                q = hq[:, g * 1024:(g + 1) * 1024]
                act.activation(q, q, ACT.Silu).then_inc(q_ready, 1)

            def level_exp(g, l):
                m = BUF_LEVELS * g + l
                e = lev_e[m % 2]
                if l < len(HALVES):
                    act.wait_ge(diff_ready, len(HALVES) * g + l + 1)
                    act.activation(e, e, ACT.Exp).then_inc(exp_ready, 1)
                    return
                act.wait_ge(kt_ready, m - 1)
                act.wait_ge(qt_ready, m - 1)
                for h in range(4):
                    b = zb[:, (4 * g + h) * T:(4 * g + h + 1) * T]
                    act.activation(e[:, h * T:h * T + P], b[:, 0:P], ACT.Exp, scale=-1.0, bias=b[:, P - 1:P])
                    ins = act.activation(e[:, h * T + P:(h + 1) * T], b[:, P:T], ACT.Exp)
                ins.then_inc(exp_ready, 1)

            def attn_copies(g, first, last):
                for n in range(first, last):
                    act.wait_ge(at_done, 4 * g + n + 1)
                    dst = [khatT, state, ho[:, 0, g * N:(g + 1) * N], ho[:, 1, g * N:(g + 1) * N]][n]
                    act.activation(dst, bank(6 + n % 2), ACT.Copy).then_inc(at_out, 1)

            for n in range(4):
                hg_copy(n)
            act.wait_ge(lb_ready, 3)
            log_gates_a(0)
            hg_copy(4)
            hg_copy(5)
            log_gates_b(0)
            for n in range(6, 10):
                hg_copy(n)
            silu_q(0)
            for l in range(len(HALVES)):
                level_exp(0, l)
                hg_copy(10 + l)
            level_exp(0, len(HALVES))
            hg_copy(17)
            attn_copies(0, 0, 1)
            hg_copy(18)
            attn_copies(0, 1, 4)
            hg_copy(19)
            log_gates_a(1)
            log_gates_b(1)
            silu_q(1)
            act.wait_ge(b_ready, 2)
            hg_copy(20)
            level_exp(1, 0)
            level_exp(1, 1)
            hg_copy(21)
            level_exp(1, 2)
            level_exp(1, 3)
            hg_copy(22)
            for l in range(4, len(HALVES) + 1):
                level_exp(1, l)
                if l == 4:
                    hg_copy(23)
            act.wait_ge(pj_out, 24)
            act.activation(A[:, 8192:10240], A[:, 8192:10240], ACT.Silu).then_inc(hg_silu, 1)
            attn_copies(1, 0, 4)
            act.wait_ge(at_out, 8)
            act.wait_ge(at_done, 8)
            for t in range(TB):
                act.activation(lev_q[t], ho[:, t, :], ACT.Square).then_inc(sq_ready, 1)
            act.wait_ge(ms_ready, 1)
            act.activation(sm[:, 32:48], sm[:, 32:48], ACT.Sqrt).then_inc(rms_ready, 1)
            turned(1)

            def ln_sqrt(k):
                act.wait_ge(ln_var, k + 1)
                act.activation(std, mv[:, :, 1], ACT.Sqrt).then_inc(ln_std, 1)

            ln_sqrt(0)
            turned(2)
            for f in range(FFN_TILES):
                act.wait_ge(ffn_done, f + 1)
                if f >= 2:
                    act.wait_ge(ffn_h, f - 1)
                act.activation(ffn_s[f % 2], ps[:, f % 2, 0:T], ACT.Silu).then_inc(ffn_silu, 1)
            ln_sqrt(1)
            turned(3)

            act.wait_ge(pj_done, FOX_TILE0 + 1)
            act.wait_ge(small_loaded, 32)
            act.activation(fz, ps[0:FOX_HEADS, 0, 0:T], ACT.Identity, bias=fgb[:, 0:1]).then_inc(pj_out, 1)
            act.wait_ge(pj_out, FOX_TILE0 + 1)
            step(act.activation(fl, fz, ACT.Abs))
            step(act.activation(fl, fl, ACT.Exp, scale=-1.0))
            act.activation(fl, fl, ACT.Ln, bias=1.0).then_inc(f_log, 1)
            for n in range(8):
                copy_tile(FOX_TILE0 + 1 + n, fk[:, n, :], cols=T)
            for n in range(8):
                copy_tile(FOX_TILE0 + 9 + n, fq[:, n, :], scale=FOX_DIM ** -0.5, cols=T)

            def fox_copy(n):
                dst = fv if n < 4 else fg
                c = (n % 4) // 2
                copy_tile(FOX_TILE0 + 17 + n, dst[:, n % 2, c * N:(c + 1) * N])

            fox_copy(0)
            fox_copy(1)
            for h in range(FOX_HEADS + 1):
                if h < FOX_HEADS:
                    act.wait_ge(fx_max, h + 1)
                    if h >= 2:
                        act.wait_ge(fx_pt, h - 1)
                    for t in range(TB):
                        cols = slice(0, P) if t == 0 else slice(P, KW)
                        c = 2 * h + t
                        ins = act.activation(fprob[h % 2][:, cols], flog[h % 2][:, cols], ACT.Exp,
                                             bias=nmax[:, c:c + 1], accum_out=rsum[:, c:c + 1])
                    ins.then_inc(fx_exp, 1)
                if h >= 1:
                    act.wait_ge(fx_pt, h)
                    if h >= 3:
                        act.wait_ge(fx_pv, h - 2)
                    act.activation(fprobT[(h - 1) % 2], bank(4 + (h - 1) % 2, KW), ACT.Copy).then_inc(fx_ptc, 1)
                if h % 2 == 1 and h < 12:
                    fox_copy(2 + h // 2)
            act.wait_ge(pj_out, FOX_TILE0 + 25)
            for t in range(TB):
                act.activation(fg[:, t, :], fg[:, t, :], ACT.Sigmoid).then_inc(fg_sig, 1)
            turned(4)
            def hi(i, piece):
                i, piece = i + piece // MOE_PIECES, piece % MOE_PIECES
                j = piece // 4
                if piece % 4 == 0:
                    moe_slot_landed(act, i, j)
                if piece >= BUFS or not (isinstance(i, int) and i == 0):
                    act.wait_ge(pieces_used, i * MOE_PIECES + piece - BUFS + 1)
                act.activation(wh[piece % BUFS][:, :], moe_slot(j)[:, (piece % 4) * PC:(piece % 4 + 1) * PC],
                               ACT.Copy).then_inc(hi_ready, 1)

            for piece in range(BUFS):
                hi(0, piece)
            ln_sqrt(2)
            turned(5)
            for t in range(TB):
                act.wait_ge(x_ready, 8 + 2 * t + 2)
                act.activation(x3h[:, t, :], xres[:, t, :], ACT.Copy).then_inc(x3_hi, 1)
            act.wait_ge(e2_in, 1)
            act.activation(rt[9][:, 0:2], rt[9][:, 2:4], ACT.Exp).then_inc(e2_out, 1)

            def rows_hi(i, half):
                act.wait_ge(ga_done, 2 * i + half + 1)
                act.activation(xeh[:, 4 * half:4 * half + 4, :],
                               bank(7 - half).rearrange("p (k t) -> p k t", k=4), ACT.Copy).then_inc(xe_hi, 1)

            def hT_high(i, c):
                act.wait_ge(htr_done, i * CH + c + 1)
                act.activation(ehTh[:, :], bank(6), ACT.Copy).then_inc(hT_hi, 1)

            def item(i, first, last):
                done = first
                for c in range(CH):
                    a_end = moe_end("a", c)
                    for piece in range(done, a_end + BUFS):
                        hi(i, piece)
                    done = a_end + BUFS
                    if c:
                        hT_high(i, c - 1)
                        act.wait_ge(h_ready, i * CH + c)
                    act.wait_ge(pieces_used, i * MOE_PIECES + a_end)
                    act.activation(gate_s, bank(2 * (c % 2)), ACT.Silu).then_inc(silu_done, 1)
                for piece in range(done, MOE_PIECES):
                    hi(i, piece)
                hT_high(i, CH - 1)
                rows_hi(i + 1, 0)
                for piece in range(MOE_PIECES, last - 1):
                    hi(i, piece)
                act.wait_ge(pieces_used, (i + 1) * MOE_PIECES)
                for n in range(2):
                    act.activation(ye[:, n, :], bank(4 + n), ACT.Copy).then_inc(ye_ready, 1)
                rows_hi(i + 1, 1)
                if last > MOE_PIECES:
                    hi(i, last - 1)

            rows_hi(0, 0)
            rows_hi(0, 1)
            with act.Fori(0, E - 1) as i:
                item(i, BUFS, MOE_PIECES + BUFS)
            item(E - 1, BUFS, MOE_PIECES)
            act.wait_ge(items_ready, 2)
            more = act.value_load(items[0:1, 16:17], min_val=0, max_val=3)
            with act.If(more > 0):
                with act.Fori(0, more) as n:
                    item(n + E, 0, MOE_PIECES)
            ln_sqrt(3)

        @block.vector
        def _(dve):
            step = Steps(dve, dve_steps)

            def turned(stage):
                for t in range(TB):
                    dve.wait_ge(tp_done, 4 * stage + 2 * t + 1)
                    dve.tensor_copy(xT[:, 0:4, t * P:(t + 1) * P],
                                    bank(6).rearrange("p (k t) -> p k t", k=4)).then_inc(tp_dve, 1)

            step(dve.memset(scT, 0.0))
            dve.wait_ge(small_loaded, 32)
            dve.tensor_tensor(sm[:, 32:40], lbt, lbt, ALU.subtract).then_inc(lb_ready, 1)
            dve.wait_ge(lb_exp, 1)
            step(dve.reciprocal(sm[:, 32:40], lbt))
            step(dve.tensor_tensor(lbt, lbt, sm[:, 32:40], ALU.mult))
            step(dve.tensor_tensor(lbt, lbt, lbt, ALU.subtract))
            step(dve.tensor_scalar(one_m_lb, lbt, -1.0, 1.0, ALU.mult, ALU.add))
            dve.tensor_scalar(sm[:, 40:48], lbt, LB_FLOOR, None, ALU.max).then_inc(lb_ready, 1)
            dve.wait_ge(loglb_ready, 1)
            dve.tensor_scalar(nloglb, loglb, -1.0, None, ALU.mult).then_inc(lb_ready, 1)
            turned(0)

            def log_gates(g):
                z, k = zb[:, g * 1024:(g + 1) * 1024], hk[:, g * 1024:(g + 1) * 1024]
                dve.wait_ge(sp_log, g + 1)
                step(dve.scalar_tensor_tensor(ph_a, z, 0.0, ph_l, ALU.min, ALU.subtract))
                dve.scalar_tensor_tensor(k, z, 0.0, ph_l, ALU.max, ALU.add).then_inc(sp_sum, 1)
                dve.wait_ge(sp_sum, g + 1)
                for h in range(4):
                    cols = slice(h * T, (h + 1) * T)
                    ins = dve.scalar_tensor_tensor(ph_a[:, cols], k[:, cols], loglb[:, 4 * g + h:4 * g + h + 1],
                                                   ph_a[:, cols], ALU.subtract, ALU.max, reverse0=True)
                ins.then_inc(floor_max, 1)
                dve.wait_ge(floor_max, g + 1)
                dve.wait_ge(kexp_ready, g + 1)
                for h in range(4):
                    cols = slice(h * T, (h + 1) * T)
                    step.note(dve.tensor_scalar(k[:, cols], k[:, cols], one_m_lb[:, 4 * g + h:4 * g + h + 1], None,
                                                ALU.mult))
                dve.wait_ge(rlog_ready, g + 1)
                dve.wait_ge(dve_steps, step.n)
                step(dve.tensor_tensor(ph_a, ph_a, ph_l, ALU.add))
                for u in range(8):
                    cols = slice(u * P, (u + 1) * P)
                    ins = dve.tensor_tensor_scan(z[:, cols], ones, ph_a[:, cols], 0.0, ALU.mult, ALU.add)
                ins.then_inc(b_ready, 1)
                dve.wait_ge(b_ready, g + 1)

            def level_diff(g, l):
                m = BUF_LEVELS * g + l
                if m >= 2:
                    dve.wait_ge(kt_ready, m - 1)
                    dve.wait_ge(qt_ready, m - 1)
                half = HALVES[l]
                n = 1024 // (2 * half)
                b = zb[:, g * 1024:(g + 1) * 1024].rearrange("p (n s h) -> p n s h", s=2, h=half)
                e = lev_e[m % 2].rearrange("p (n s h) -> p n s h", s=2, h=half)
                ref = b[:, :, 0, half - 1:half].to_broadcast([P, n, half])
                dve.tensor_tensor(e[:, :, 0, :], ref, b[:, :, 0, :], ALU.subtract)
                dve.tensor_tensor(e[:, :, 1, :], b[:, :, 1, :], ref, ALU.subtract).then_inc(diff_ready, 1)

            def level_keys(g, l):
                m = BUF_LEVELS * g + l
                dve.wait_ge(exp_ready, m + 1)
                if l == len(HALVES):
                    dve.wait_ge(sc_done, 2 * (LEVELS * g + l - 1))
                elif g and l < 2:
                    dve.wait_ge(at_done, 4 * g)
                elif l >= 2:
                    dve.wait_ge(sc_done, 2 * (LEVELS * g + l - 1))
                dve.tensor_tensor(lev_k[m % 2], hk[:, g * 1024:(g + 1) * 1024], lev_e[m % 2], ALU.mult)\
                   .then_inc(kt_ready, 1)

            def level_select(g, l):
                c = LEVELS * g + l
                for h in range(2):
                    dve.wait_ge(sc_done, 2 * c + h + 1)
                    if c or h:
                        dve.wait_ge(sc_sel, 2 * c + h)
                    if g and l == 0:
                        dve.wait_ge(at_done, 4 * g)
                    mask = level_mask[:, l, :].unsqueeze(1).to_broadcast([P, 4, P])
                    dst = scT[:, h * N:(h + 1) * N].rearrange("p (u t) -> p u t", u=4)
                    src = bank(2 + 2 * (c % 2) + h).rearrange("p (u t) -> p u t", u=4)
                    dve.copy_predicated(dst, mask, src).then_inc(sc_sel, 1)

            log_gates(0)
            dve.wait_ge(mask_ready, 1)
            for g in range(2):
                level_diff(g, 0)
                for l in range(len(HALVES) + 1):
                    if l + 1 < len(HALVES):
                        level_diff(g, l + 1)
                    level_keys(g, l)
                    if l:
                        level_select(g, l - 1)
                level_select(g, LEVELS - 1)
                if g == 0:
                    log_gates(1)
            for t in range(TB):
                dve.wait_ge(sq_ready, t + 1)
                step(dve.tensor_reduce(ssq[:, t, :], lev_q[t].rearrange("p (h e) -> p h e", h=HG_HEADS), AX_X, ALU.add))
            dve.tensor_scalar(sm[:, 32:48], sm[:, 32:48], 1.0 / P, RMS_EPS, ALU.mult, ALU.add).then_inc(ms_ready, 1)
            dve.wait_ge(rms_ready, 1)
            step(dve.reciprocal(sm[:, 32:48], sm[:, 32:48]))
            for t in range(TB):
                o = ho[:, t, :].rearrange("p (h e) -> p h e", h=HG_HEADS)
                step(dve.tensor_tensor(o, o, ssq[:, t, :].unsqueeze(2).to_broadcast([P, HG_HEADS, P]), ALU.mult))
                dve.wait_ge(gn_ready, t + 1)
                dve.tensor_tensor(ho[:, t, :], ho[:, t, :], hg[:, t, :], ALU.mult).then_inc(on_ready, 1)
            turned(1)

            def layer_norm(k, r, gain, bias, steps, summed=None):
                for t in range(TB):
                    for n in range(2):
                        if summed is not None:
                            summed(t, n)
                        steps(dve.bn_stats(stats[:, t, n, :], r[:, t, n * N:(n + 1) * N]))
                    steps(dve.bn_aggr(mv[:, t, :], stats[:, t, :, :].rearrange("p n s -> p (n s)")))
                dve.tensor_scalar(mv[:, :, 1], mv[:, :, 1], LN_EPS, None, ALU.add).then_inc(ln_var, 1)
                dve.wait_ge(ln_std, k + 1)
                steps(dve.reciprocal(std, std))
                dve.wait_ge(gb_loaded, 32 * (k + 1))
                for t in range(TB):
                    for n in range(2):
                        cols = slice(n * N, (n + 1) * N)
                        steps(dve.scalar_tensor_tensor(r[:, t, cols], r[:, t, cols], mv[:, t, 0:1], gain[:, cols],
                                                       ALU.subtract, ALU.mult))
                        dve.scalar_tensor_tensor(r[:, t, cols], r[:, t, cols], std[:, t:t + 1], bias[:, cols],
                                                 ALU.mult, ALU.add).then_inc(x_ready, 1)

            def residual(k):
                def summed(t, n):
                    order = 2 * t + n if k == 1 else 2 * n + t
                    dve.wait_ge(y_done, 4 * k + order + 1)
                    cols = slice(n * N, (n + 1) * N)
                    step(dve.scalar_tensor_tensor(xres[:, t, cols], xres[:, t, cols], ALPHA,
                                                  bank(2 + 2 * n + t), ALU.mult, ALU.add))

                layer_norm(k, xres, gb[:, 0, :], gb[:, 1, :], step, summed)

            residual(0)
            turned(2)
            for f in range(FFN_TILES):
                dve.wait_ge(ffn_silu, f + 1)
                dve.tensor_tensor(hT[:, f, :], ffn_s[f % 2], ps[:, f % 2, T:2 * T], ALU.mult).then_inc(ffn_h, 1)
            residual(1)
            turned(3)

            dve.wait_ge(f_log, 1)
            step(dve.scalar_tensor_tensor(fl, fz, 0.0, fl, ALU.min, ALU.subtract))
            dve.tensor_tensor_scan(fc, sq[0:FOX_HEADS, P:P + 1].to_broadcast([FOX_HEADS, T]), fl, 0.0,
                                   ALU.mult, ALU.add).then_inc(c_ready, 1)
            dve.wait_ge(cT_done, 1)
            dve.tensor_copy(A[:, 13792:13824], ps[:, 6, 0:32]).then_inc(cT_ready, 1)
            dve.wait_ge(cT_ready, 1)
            dve.wait_ge(fox_loaded, 32)

            def fox_max(h):
                dve.wait_ge(fx_qk, h + 1)
                if h >= 2:
                    dve.wait_ge(fx_exp, h - 1)
                for t in range(TB):
                    cols = slice(0, P) if t == 0 else slice(P, KW)
                    step.note(dve.scalar_tensor_tensor(flog[h % 2][:, cols], ps[:, 2 + h % 2, cols],
                                                       cT[:, t, h:h + 1], causal[:, cols], ALU.add, ALU.add))
                for t in range(TB):
                    cols = slice(0, P) if t == 0 else slice(P, KW)
                    dve.wait_ge(dve_steps, step.n - 1 + t)
                    ins = dve.tensor_reduce(nmax[:, 2 * h + t:2 * h + t + 1], flog[h % 2][:, cols], AX_X, ALU.max,
                                            negate=True)
                ins.then_inc(fx_max, 1)

            def fox_norm(h):
                dve.wait_ge(fx_pv, h + 1)
                step(dve.reciprocal(rinv[:, 2 * h:2 * h + 2], rsum[:, 2 * h:2 * h + 2]))
                dve.tensor_tensor(fo[:, :, h * FOX_DIM:(h + 1) * FOX_DIM],
                                  bank(6 + h % 2, 2 * FOX_DIM).rearrange("p (t e) -> p t e", t=TB),
                                  rinv[:, 2 * h:2 * h + 2].unsqueeze(2).to_broadcast([P, TB, FOX_DIM]),
                                  ALU.mult).then_inc(fx_out, 1)

            for h in range(FOX_HEADS + 2):
                if h < FOX_HEADS:
                    fox_max(h)
                if h >= 2:
                    fox_norm(h - 2)
            dve.wait_ge(fx_out, FOX_HEADS)
            for t in range(TB):
                dve.wait_ge(fg_sig, t + 1)
                dve.tensor_tensor(fo[:, t, :], fo[:, t, :], fg[:, t, :], ALU.mult).then_inc(og_ready, 1)
            turned(4)

            def lo(i, piece):
                i, piece = i + piece // MOE_PIECES, piece % MOE_PIECES
                j = piece // 4
                dve.wait_ge(hi_ready, i * MOE_PIECES + piece + 1)
                dve.tensor_tensor(wl[piece % BUFS][:, :], moe_slot(j)[:, (piece % 4) * PC:(piece % 4 + 1) * PC],
                                  wh[piece % BUFS][:, :].bitcast(F32), ALU.subtract).then_inc(lo_ready, 1)

            residual(2)
            turned(5)

            for t in range(TB):
                dve.wait_ge(x_ready, 8 + 2 * t + 2)
                dve.tensor_scalar(yacc[:, t, :], xres[:, t, :], ALPHA, None, ALU.mult).then_inc(yacc_up, 1)

            def by_token(a):
                return a.rearrange("p (t e) -> p t e", t=TB)

            def spread_e(a):
                return a.unsqueeze(2).to_broadcast([P, TB, E])

            w8b = w8.unsqueeze(1).to_broadcast([P, TB, E])
            lg, eq, f1, lg2, f2, tmp = rt[0], rt[1], rt[2], rt[3], rt[4], rt[5]
            m1, m2, kmax, w1, w2 = (rt[6][:, 0:2], rt[6][:, 2:4], rt[6][:, 4:6], rt[6][:, 6:8], rt[6][:, 8:10])
            comb, sel = rt[7], rt[8]
            dve.wait_ge(lg_done, 1)
            step(dve.tensor_copy(lg, ps[:, 0, 0:2 * E]))

            def first_largest(values, m, first):
                step(dve.tensor_reduce(m, by_token(values), AX_X, ALU.max))
                step(dve.tensor_tensor(by_token(eq), by_token(values), spread_e(m), ALU.is_ge))
                step(dve.tensor_tensor(by_token(eq), by_token(eq), w8b, ALU.mult))
                step(dve.tensor_reduce(kmax, by_token(eq), AX_X, ALU.max))
                step(dve.tensor_tensor(by_token(first), by_token(eq), spread_e(kmax), ALU.is_ge))

            first_largest(lg, m1, f1)
            step(dve.scalar_tensor_tensor(lg2, f1, MASKED, lg, ALU.mult, ALU.add))
            first_largest(lg2, m2, f2)
            dve.tensor_tensor(rt[9][:, 2:4], m2, m1, ALU.subtract).then_inc(e2_in, 1)
            dve.tensor_tensor(sel, f1, f2, ALU.add).then_inc(sel_ready, 1)
            dve.wait_ge(yacc_up, TB)
            for t in range(TB):
                dve.wait_ge(x3_hi, t + 1)
                dve.tensor_tensor(x3l[:, t, :], xres[:, t, :], x3h[:, t, :].bitcast(F32), ALU.subtract)\
                   .then_inc(x3_ready, 1)
            dve.wait_ge(e2_out, 1)
            step(dve.tensor_scalar(w1, rt[9][:, 0:2], 1.0, None, ALU.add))
            step(dve.reciprocal(w1, w1))
            step(dve.tensor_tensor(w2, w1, rt[9][:, 0:2], ALU.mult))
            step(dve.tensor_tensor(by_token(tmp), by_token(f1), spread_e(w1), ALU.mult))
            step(dve.tensor_tensor(by_token(comb), by_token(f2), spread_e(w2), ALU.mult))
            step(dve.tensor_tensor(comb, comb, tmp, ALU.add))
            dve.wait_ge(sel_ready, 1)
            step(dve.tensor_scalar(tmp, sel, -NOT_CHOSEN, NOT_CHOSEN, ALU.mult, ALU.add))
            dve.wait_ge(rk_done, 1)
            step(dve.tensor_tensor(rank2[:, :, 0:E], by_token(ps[:, 1, 0:2 * E]), by_token(tmp), ALU.add))
            step(dve.tensor_scalar(rank2[:, :, E:2 * E], rank2[:, :, 0:E], -float(P), None, ALU.add))
            step(dve.tensor_copy(comb2[:, :, 0:E], by_token(comb)))
            step(dve.tensor_copy(comb2[:, :, E:2 * E], by_token(comb)))
            over, mx, cols_f = itf[:, 0:8], itf[:, 8:16], itf[:, 16:32]
            step(dve.tensor_scalar(over, ps[0:1, 1, 2 * E:3 * E], float(P), None, ALU.is_gt))
            step(dve.tensor_reduce(itf[:, 32:33], over, AX_X, ALU.add))
            step(dve.tensor_tensor(over, over, w8[0:1, :], ALU.mult))
            step(dve.max(mx, over))
            step(dve.tensor_scalar(cols_f[:, 0:8], w8[0:1, :], -1.0, float(E), ALU.mult, ALU.add))
            step(dve.tensor_scalar(cols_f[:, 8:16], mx, -1.0, 2.0 * E, ALU.mult, ALU.add))
            step(dve.tensor_scalar(cols_f[:, 8:16], cols_f[:, 8:16], 2.0 * E - 1, None, ALU.min))
            dve.tensor_copy(items[:, 0:16], cols_f).then_inc(items_ready, 1)
            dve.tensor_copy(items[:, 16:17], itf[:, 32:33]).then_inc(items_ready, 1)
            dve.wait_ge(items_ready, 2)

            PICK_STEPS = 5

            def build_pick(i, steps):
                col = dve.value_load(items[0:1, bass.ds(i, 1)], min_val=0, max_val=2 * E - 1)
                steps.note(dve.tensor_copy(cur[:, 0:2], rank2[:, :, bass.ds(col, 1)].squeeze(2)))
                steps(dve.tensor_copy(cur[:, 2:4], comb2[:, :, bass.ds(col, 1)].squeeze(2)))
                for t in range(TB):
                    steps.note(dve.tensor_scalar(pick[:, t, :], iota, cur[:, t:t + 1], None, ALU.is_equal))
                steps(dve.tensor_scalar(pickw[:, 0, :], iota, cur[:, 0:1], cur[:, 2:3], ALU.is_equal, ALU.mult))
                dve.tensor_scalar(pickw[:, 1, :], iota, cur[:, 1:2], cur[:, 3:4], ALU.is_equal, ALU.mult)\
                   .then_inc(pick_ready, 1)

            def rows_lo(i, half):
                dve.wait_ge(xe_hi, 2 * i + half + 1)
                rows = slice(4 * half, 4 * half + 4)
                dve.tensor_tensor(xel[:, rows, :], bank(7 - half).rearrange("p (k t) -> p k t", k=4),
                                  xeh[:, rows, :].bitcast(F32), ALU.subtract).then_inc(xe_ready, 1)

            def hT_low(i, c):
                dve.wait_ge(hT_hi, i * CH + c + 1)
                dve.tensor_tensor(ehTl[:, :], bank(6), ehTh[:, :].bitcast(F32), ALU.subtract).then_inc(hT_ready, 1)

            def add_outputs(i, n):
                for t in range(TB):
                    dve.wait_ge(sc2_done, 4 * i + 2 * n + t + 1)
                    if n == 0:
                        dve.wait_ge(yacc_up, 4 * i + 1 + t)
                    cols = slice(n * N, (n + 1) * N)
                    dve.tensor_tensor(yacc[:, t, cols], yacc[:, t, cols], bank([7, 6, 2, 3][2 * n + t]), ALU.add)\
                       .then_inc(yacc_up, 1)

            def item(i, first, last):
                done = first
                for c in range(CH):
                    if c:
                        for piece in range(done, moe_end("a", c) + BUFS):
                            lo(i, piece)
                        done = moe_end("a", c) + BUFS
                        hT_low(i, c - 1)
                    b_end = moe_end("b", c)
                    for piece in range(done, b_end + BUFS):
                        lo(i, piece)
                    done = b_end + BUFS
                    dve.wait_ge(pieces_used, i * MOE_PIECES + b_end)
                    dve.wait_ge(silu_done, i * CH + c + 1)
                    dve.tensor_tensor(eh, gate_s, bank(2 * (c % 2) + 1), ALU.mult).then_inc(h_ready, 1)
                    if c == 0:
                        dve.wait_ge(spr_done, i + 1)
                        dve.tensor_copy(spread_all, ps[:, 6, 0:2 * P]).then_inc(spr_ready, 1)
                    if c == 1:
                        build_pick(i + 1, Steps(dve, dve_item, i * PICK_STEPS + PICK_STEPS))
                for piece in range(done, MOE_PIECES):
                    lo(i, piece)
                hT_low(i, CH - 1)
                rows_lo(i + 1, 0)
                for piece in range(MOE_PIECES, last - 1):
                    lo(i, piece)
                rows_lo(i + 1, 1)
                add_outputs(i, 0)
                if last > MOE_PIECES:
                    lo(i, last - 1)
                add_outputs(i, 1)

            build_pick(0, Steps(dve, dve_item, 0))
            for piece in range(BUFS):
                lo(0, piece)
            rows_lo(0, 0)
            rows_lo(0, 1)
            with dve.Fori(0, E - 1) as i:
                item(i, BUFS, MOE_PIECES + BUFS)
            item(E - 1, BUFS, MOE_PIECES)
            more = dve.value_load(items[0:1, 16:17], min_val=0, max_val=3)
            with dve.If(more > 0):
                with dve.Fori(0, more) as n:
                    item(n + E, 0, MOE_PIECES)
            dve.wait_ge(yacc_up, (more + E) * 4 + 2)
            layer_norm(3, yacc, last_gain, last_bias, Steps(dve, dve_tail))

        @block.gpsimd
        def _(pool):
            with nc.allow_non_contiguous_dma("small parameters"):
                pool.dma_start(lbt, lb_logits[0].rearrange("(h p) -> p h", p=P)).then_inc(small_loaded, 16)
                pool.dma_start(fgb[:, :], fgate_b.rearrange("(p a) -> p a", a=1)).then_inc(small_loaded, 16)
            pool.wait_ge(levels_loaded, 16)
            pool.tensor_copy(level_mask.rearrange("p l n -> p (l n)"), lev_k[0]).then_inc(mask_ready, 1)
            for g in range(2):
                pool.wait_ge(q_ready, g + 1)
                for l in range(BUF_LEVELS):
                    m = BUF_LEVELS * g + l
                    pool.wait_ge(exp_ready, m + 1)
                    if g and l < 2:
                        pool.wait_ge(at_done, 4 * g)
                    elif l >= 2:
                        pool.wait_ge(sc_done, 2 * (LEVELS * g + l - 1))
                    pool.tensor_tensor(lev_q[m % 2], hq[:, g * 1024:(g + 1) * 1024], lev_e[m % 2], ALU.mult)\
                        .then_inc(qt_ready, 1)
            pool.wait_ge(kt_ready, 2 * BUF_LEVELS)
            pool.wait_ge(qt_ready, 2 * BUF_LEVELS)
            pool.dma_start(normw, norm_w[0:1, :].to_broadcast([P, P])).then_inc(normw_loaded, 16)
            pool.wait_ge(normw_loaded, 16)
            pool.wait_ge(hg_silu, 1)
            for t in range(TB):
                g3 = hg[:, t, :].rearrange("p (h e) -> p h e", h=HG_HEADS)
                pool.tensor_tensor(g3, g3, normw.unsqueeze(1).to_broadcast([P, HG_HEADS, P]), ALU.mult)\
                    .then_inc(gn_ready, 1)

            def load_ln(gains, biases, layer, gain, bias):
                pool.dma_start(gain, gains[layer:layer + 1, :].to_broadcast([P, D])).then_inc(gb_loaded, 16)
                pool.dma_start(bias, biases[layer:layer + 1, :].to_broadcast([P, D])).then_inc(gb_loaded, 16)

            pool.wait_ge(tp_done, 8)
            load_ln(ln_mix_g, ln_mix_b, 0, gb[:, 0, :], gb[:, 1, :])
            pool.dma_start(negsel, c_negsel).then_inc(fox_loaded, 16)
            pool.dma_start(causal, c_causal).then_inc(fox_loaded, 16)
            pool.dma_start(iota, c_route[:, 0:P]).then_inc(route_loaded, 16)
            pool.dma_start(before, c_route[:, P:2 * P]).then_inc(route_loaded, 16)
            pool.dma_start(w8, c_route[:, 2 * P:2 * P + E]).then_inc(route_loaded, 16)
            pool.dma_start(w_router, router_w[0].rearrange("(k p) n -> p k n", p=P)).then_inc(route_loaded, 16)
            pool.dma_start(w_f, kv_v[:, :, 2 * D:2 * D + FOX_HEADS]).then_inc(route_loaded, 16)
            pool.wait_ge(x_ready, 4)
            load_ln(ln_ffn_g, ln_ffn_b, 0, gb[:, 0, :], gb[:, 1, :])
            pool.wait_ge(x_ready, 8)
            load_ln(ln_mix_g, ln_mix_b, 1, gb[:, 0, :], gb[:, 1, :])
            pool.wait_ge(rk_done, 1)
            load_ln(ln_ffn_g, ln_ffn_b, 1, last_gain, last_bias)


_INS = ["x", "hg_w_in", "hg_lb_logits", "hg_norm_w", "hg_w_out", "kv_w", "kv_fgate_b", "fox_w_qg", "fox_w_out",
        "ln_mix_g", "ln_mix_b", "ln_ffn_g", "ln_ffn_b", "ffn_w_gu", "ffn_w_down", "moe_w_router", "moe_w_gu",
        "moe_w_down"]


def _constants():
    import numpy as np

    r = np.arange(P)
    square = np.concatenate([np.eye(P), np.ones((P, P))], axis=1).astype(np.float32)
    levels = []
    for half in HALVES:
        same = (r[:, None] // (2 * half)) == (r[None, :] // (2 * half))
        levels.append(same & ((r[:, None] // half) % 2 == 0) & ((r[None, :] // half) % 2 == 1))
    levels.append(r[:, None] == r[None, :])
    levels = np.concatenate(levels, axis=1).astype(np.float32)
    negsel = -np.eye(FOX_HEADS).astype(np.float32)
    causal = np.concatenate([np.where(r[None, :] <= r[:, None], 0.0, MASKED), np.zeros((P, P)),
                             np.where(r[None, :] <= r[:, None], 0.0, MASKED)], axis=1).astype(np.float32)
    route = np.concatenate([np.broadcast_to(r, (P, P)), r[:, None] < r[None, :],
                            np.broadcast_to(E - np.arange(E), (P, E))], axis=1).astype(np.float32)
    return {"c_square": square, "c_levels": levels, "c_negsel": negsel, "c_causal": causal, "c_route": route}


def kernel(**inputs):
    import numpy as _np
    import concourse.bacc as _bacc
    from concourse import mybir as _mybir
    from concourse.bass_utils import run_bass_kernel_spmd as _run

    nc = _bacc.Bacc("TRN2", target_bir_lowering=False, num_devices=1)
    arrays, args = {}, []
    given = {name: _np.ascontiguousarray(inputs[name]) for name in _INS}
    for name, a in {**given, **_constants()}.items():
        arrays[f"in_{name}_dram"] = a
        args.append(nc.dram_tensor(f"in_{name}_dram", a.shape, _mybir.dt.from_np(a.dtype), kind="ExternalInput").ap())
    args.append(nc.dram_tensor("out_dram", (1, T, D), F32, kind="ExternalOutput").ap())
    build(nc, *args)
    r = _run(nc, [arrays], core_ids=[0])
    return r.results[0]["out_dram"]
```

```python
from contextlib import ExitStack

import concourse.bass as bass
from concourse import mybir

F32 = mybir.dt.float32
F32R = mybir.dt.float32r
I32 = mybir.dt.int32
U8 = mybir.dt.uint8
ALU = mybir.AluOpType
ACT = mybir.ActivationFunctionType
AX_X = mybir.AxisListType.X

P = 128
D = 1024
T = 256
TB = T // P
KT = D // P
N = 512
HG_HEADS = 8
FOX_HEADS = 16
FOX_DIM = 64
FFN = 2816
FFN_TILES = FFN // P
E = 8
F = 3584
CH = F // N
FT = N // P
ALPHA = 4 ** 0.25
LN_EPS = 1e-5
RMS_EPS = 1e-6
LB_FLOOR = 1e-30
LN_SHIFT = 50
LN2 = 0.6931471805599453
MASKED = -1e30
NOT_CHOSEN = 1e6

CORE = 4
SLOT = KT * N
HG_SLOTS = 8
S_HG_OUT = HG_SLOTS
S_GU = S_HG_OUT + 2
FFN_CH = 11
S_DOWN = S_GU + FFN_CH
DOWN_SLOTS = 6
S_KVQG = S_DOWN + DOWN_SLOTS
S_FOX_OUT = S_KVQG + 8
S_MOE = S_FOX_OUT + 2
MOE_PLACES = [CORE, S_MOE % CORE, (S_MOE + 1) % CORE, CORE + 1, CORE + 2, (S_MOE + 2) % CORE, (S_MOE + 3) % CORE]
MOE_RING = len(MOE_PLACES)

PC = 1024
BUFS = 4
P_HG_OUT = 4 * S_HG_OUT
P_GU = 4 * S_GU
P_DOWN = P_GU + 4 * FFN_CH
P_KVQG = P_DOWN + FFN_TILES
P_FOX_OUT = P_KVQG + 4 * 8
P_MOE = P_FOX_OUT + 4 * 2
MOE_SLOTS = 3 * CH
assert MOE_SLOTS % MOE_RING == 0
MOE_ORDER = [("a", 0), ("b", 0)]
for _c in range(1, CH):
    MOE_ORDER += [("a", _c), ("b", _c), ("d", _c - 1)]
MOE_ORDER += [("d", CH - 1)]
MOE_PIECES = 4 * MOE_SLOTS
assert MOE_PIECES % BUFS == 0


def moe_end(kind, c):
    return 4 * (MOE_ORDER.index((kind, c)) + 1)


HALVES = [64, 32, 16, 8, 4, 2, 1]
LEVELS = len(HALVES) + 1
BUF_LEVELS = len(HALVES) + 1


class Steps:

    def __init__(self, eng, sem, start=0):
        self.eng, self.sem, self.n = eng, sem, start

    def __call__(self, ins):
        ins.then_inc(self.sem, 1)
        self.n += 1
        self.eng.wait_ge(self.sem, self.n)

    def note(self, ins):
        ins.then_inc(self.sem, 1)
        self.n += 1


def build(nc, x, w_in, lb_logits, norm_w, w_out, kv_w, fgate_b, fox_qg, fox_out, ln_mix_g, ln_mix_b,
          ln_ffn_g, ln_ffn_b, ffn_gu, ffn_down, router_w, moe_gu, moe_down,
          c_square, c_levels, c_negsel, c_causal, c_route, out):
    with ExitStack() as ctx:
        def sb(name, shape, dt=F32):
            return ctx.enter_context(nc.sbuf_tensor(name, shape, dt))

        def sem(name):
            return ctx.enter_context(nc.semaphore(name))

        ARENA = 53000
        arena = sb("arena", [P, ARENA])
        arena_at = int(nc.sbuf_base) - 4 * ARENA

        def at(name, col, cols, dt=F32, rows=P):
            return nc.alloc_sbuf_tensor_at(name, [rows, cols], dt, offset=arena_at + 4 * col)

        xres = at("xres", 0, TB * D)[:, :].rearrange("p (t n) -> p t n", t=TB)
        gb = at("gb", 2048, 2 * D)[:, :].rearrange("p (t n) -> p t n", t=2)
        xTh = at("xTh", 4096, KT * T, F32R)[:, :].rearrange("p (k t) -> p k t", k=KT)
        xTl = at("xTl", 6144, KT * T, F32R)[:, :].rearrange("p (k t) -> p k t", k=KT)
        sq = at("sq", 8192, 2 * P)[:, :]
        level_mask = at("level_mask", 8448, LEVELS * P, U8)[:, :].rearrange("p (l n) -> p l n", l=LEVELS)
        sm = at("sm", 8704, 96)[:, :]
        fgb = at("fgb", 8800, 1, rows=FOX_HEADS)[:, :]
        itf = at("itf", 8808, 40, rows=1)[:, :]
        items = at("items", 8856, 17, I32, rows=1)[:, :]
        wh = [at(f"wh{n}", 8904 + 2 * PC * n, PC, F32R) for n in range(BUFS)]
        wl = [at(f"wl{n}", 8904 + 2 * PC * n + PC, PC, F32R) for n in range(BUFS)]
        CORE_AT = 8904 + 2 * PC * BUFS
        A_AT = CORE_AT + CORE * SLOT
        A = at("scratch", A_AT, ARENA - A_AT)[:, :]
        places = [at(f"place{n}", CORE_AT + n * SLOT, SLOT) for n in range(CORE)]
        places += [at("place4", ARENA - SLOT, SLOT), at("place5", A_AT, SLOT), at("place6", A_AT + SLOT, SLOT)]

        ident = sq[:, 0:P]
        ones = sq[:, P:2 * P]
        ps = ctx.enter_context(nc.psum_tensor("ps", [P, 8, N], F32))

        def bank(n, cols=N):
            return ps[:, n, 0:cols]

        zb = A[:, 0:2048]
        hq = A[:, 2048:4096]
        hk = A[:, 4096:6144]
        hv = A[:, 6144:8192].rearrange("p (t n) -> p t n", t=TB)
        hg = A[:, 8192:10240].rearrange("p (t n) -> p t n", t=TB)
        ph_l, ph_a = A[:, 8192:9216], A[:, 9216:10240]
        lev_e = [A[:, 10240:11264], A[:, 11264:12288]]
        lev_q = [A[:, 12288:13312], A[:, 13312:14336]]
        lev_k = [A[:, 14336:15360], A[:, 15360:16384]]
        scT = A[:, 16384:17408]

        def half_of(a, half, which):
            return a.rearrange("p (n s h) -> p n s h", s=2, h=half)[:, :, which, :]

        khatT = lev_k[0][:, 0:N]
        state = lev_q[0][:, 0:N]
        ho = gb
        lbt = sm[:, 0:8]
        one_m_lb = sm[:, 8:16]
        loglb = sm[:, 16:24]
        nloglb = sm[:, 24:32]
        ssq = sm[:, 32:48].rearrange("p (t h) -> p t h", t=TB)
        stats = sm[:, 48:72].rearrange("p (t n s) -> p t n s", t=TB, n=2)
        mv = sm[:, 72:76].rearrange("p (t s) -> p t s", t=TB)
        std = sm[:, 76:78]
        normw = A[:, 17408:17536]

        hTh, hTl = (at(f"ffn_hT_{part}", A_AT + FFN_TILES * T * n, FFN_TILES * T, F32R)[:, :]
                    .rearrange("p (f t) -> p f t", t=T) for n, part in enumerate(("high", "low")))
        ffn_s = [A[:, 11264:11520], A[:, 11520:11776]]
        ffn_p = [A[:, 14680:14936], A[:, 14936:15192]]

        fk = A[:, 0:2048].rearrange("p (c t) -> p c t", t=T)
        fq = A[:, 2048:4096].rearrange("p (c t) -> p c t", t=T)
        fv = A[:, 4096:6144].rearrange("p (t n) -> p t n", t=TB)
        fg = A[:, 6144:8192].rearrange("p (t n) -> p t n", t=TB)
        fo = A[:, 8192:10240].rearrange("p (t n) -> p t n", t=TB)
        KW = 3 * P
        flog = [A[:, 10240:10240 + KW], A[:, 10624:10624 + KW]]
        fprob = [A[:, 11008:11008 + KW], A[:, 11392:11392 + KW]]
        fprobT = [A[:, 11776:11776 + KW], A[:, 12160:12160 + KW]]
        causal = A[:, 12544:12544 + KW]
        fz = A[0:FOX_HEADS, 12928:13184]
        fl = A[0:FOX_HEADS, 13184:13440]
        fc = A[0:FOX_HEADS, 13440:13696]
        nmax = A[:, 13696:13728]
        rsum = A[:, 13728:13760]
        rinv = A[:, 13760:13792]
        cT = A[:, 13792:13824].rearrange("p (t h) -> p t h", t=TB)
        iota = A[:, 13824:13952]
        before = A[:, 13952:14080]
        w8 = A[:, 14080:14088]
        w_small = A[:, 14088:14280]
        wsh, wsl = at("wsh", A_AT + 14280, 192, F32R)[:, :], at("wsl", A_AT + 14472, 192, F32R)[:, :]
        negsel = A[0:FOX_HEADS, 14664:14680]

        lgT = A[0:E, 12928:13184]

        def router_part(a):
            return a[:, 0:KT * E].rearrange("p (k n) -> p k n", k=KT)

        def fgate_part(a):
            return a[:, KT * E:].rearrange("p (k n) -> p k n", k=KT)

        x3h = at("x3h", 2048, TB * D, F32R)[:, :].rearrange("p (t n) -> p t n", t=TB)
        x3l = at("x3l", 0, TB * D, F32R)[:, :].rearrange("p (t n) -> p t n", t=TB)
        xeh = at("xeh", 4096, KT * P, F32R)[:, :].rearrange("p (k t) -> p k t", k=KT)
        xel = at("xel", 5120, KT * P, F32R)[:, :].rearrange("p (k t) -> p k t", k=KT)
        ehTh, ehTl = at("ehTh", 6144, N, F32R), at("ehTl", 6656, N, F32R)
        last_gain = at("last_gain", 7168, D)[:, :]
        yacc = A[:, 8192:10240].rearrange("p (t n) -> p t n", t=TB)
        yeh = at("yeh", A_AT + 10240, D, F32R)[:, :].rearrange("p (n c) -> p n c", n=2)
        yel = [at("yel0", A_AT + 11264, N, F32R)[:, :], at("yel1", A_AT + 13312, N, F32R)[:, :]]
        gate_s = A[:, 11264:11776]
        pick = at("pick", A_AT + 11776, TB * P, F32R)[:, :].rearrange("p (t n) -> p t n", t=TB)
        slot_weight = A[:, 12032:12033]
        last_bias = A[:, 12288:13312]
        eh = A[:, 13312:13824]
        rt = [A[:, 14680 + 16 * n:14696 + 16 * n] for n in range(12)]
        rank2 = A[:, 14872:14904].rearrange("p (t c) -> p t c", t=TB)
        comb2 = A[:, 14904:14936].rearrange("p (t c) -> p t c", t=TB)
        cur = A[:, 14936:14940]
        spread_all = at("spread", A_AT + 14944, TB * P, F32R)[:, :]
        spread = spread_all.rearrange("p (t n) -> p t n", t=TB)

        w_ready = [sem(f"w_ready{r}") for r in range(len(places))]
        levels_loaded, mask_ready = sem("levels_loaded"), sem("mask_ready")
        consts_loaded, x_loaded, small_loaded = sem("consts_loaded"), sem("x_loaded"), sem("small_loaded")
        normw_loaded, gb_loaded, fox_loaded, route_loaded = (sem("normw_loaded"), sem("gb_loaded"),
                                                             sem("fox_loaded"), sem("route_loaded"))
        tp_done, tp_hi, tp_lo = sem("tp_done"), sem("tp_hi"), sem("tp_lo")
        pj_done, pj_out = sem("proj_done"), sem("proj_copied")
        lb_ready, loglb_ready, lb_exp = sem("lb_ready"), sem("loglb_ready"), sem("lb_exp")
        act_steps, dve_steps = sem("act_steps"), sem("dve_steps")
        sp_log, sp_sum, rlog_ready, kexp_ready, b_ready = (sem("softplus_log"), sem("softplus_sum"),
                                                          sem("floor_log"), sem("k_exp"), sem("b_ready"))
        q_ready, floor_max = sem("q_ready"), sem("floor_max")
        diff_ready, exp_ready, qt_ready, kt_ready = (sem("diff_ready"), sem("exp_ready"), sem("qt_ready"),
                                                     sem("kt_ready"))
        sc_done, sc_sel = sem("scores_done"), sem("scores_selected")
        at_done, at_out = sem("attn_done"), sem("attn_copied")
        sq_ready, ms_ready, rms_ready, gn_ready, on_ready = (sem("squares"), sem("mean_squares"), sem("rms"),
                                                             sem("gate_norm"), sem("hgrn_out"))
        hg_silu = sem("hgrn_gate_silu")
        y_first = sem("y_first_block")
        ln_var, ln_std, x_ready = sem("ln_var"), sem("ln_std"), sem("x_ready")
        ffn_silu, ffn_prod, ffn_hi, ffn_h = sem("ffn_silu"), sem("ffn_product"), sem("ffn_hi"), sem("ffn_h")
        small_hi, small_lo = sem("small_hi"), sem("small_lo")
        f_log, c_ready, cT_done, cT_ready = sem("f_log"), sem("c_ready"), sem("cT_done"), sem("cT_ready")
        fx_qk, fx_max, fx_exp, fx_pt, fx_ptc, fx_pv, fx_out = (sem("fox_qk"), sem("fox_max"), sem("fox_exp"),
                                                              sem("fox_pT"), sem("fox_pT_copied"),
                                                              sem("fox_pv"), sem("fox_out"))
        fg_sig, og_ready = sem("fox_gate_sigmoid"), sem("fox_gated")
        lgT_done, lgT_copied = sem("router_logits_turned"), sem("router_logits_copied")
        lg_done, e2_in, e2_out, sel_ready, rk_done, pick_ready = (
            sem("router_logits"), sem("top2_difference"), sem("top2_exp"), sem("chosen_ready"),
            sem("ranks_done"), sem("pick_ready"))
        weights_ready = sem("item_weights")
        items_ready = sem("items_ready")
        x3_hi, x3_ready = sem("x3_hi"), sem("x3_ready")
        ga_done, xe_hi, xe_ready = sem("gather_done"), sem("xe_hi"), sem("xe_ready")
        hi_ready, lo_ready, pieces_used = sem("hi_ready"), sem("lo_ready"), sem("pieces_used")
        silu_done, h_ready = sem("silu_done"), sem("h_ready")
        htr_done, hT_hi, hT_ready = sem("hT_done"), sem("hT_hi"), sem("hT_ready")
        spr_done, spr_ready, ye_ready = sem("spread_done"), sem("spread_copied"), sem("ye_ready")
        ye_hi = sem("ye_hi")
        sc2_done, yacc_up = sem("scatter_done"), sem("yacc_updates")
        dve_item = sem("dve_item_steps")
        dve_tail, out_done = sem("dve_tail_steps"), sem("out_done")

        w_in_v = w_in[0].rearrange("(k p) n -> p k n", p=P)
        w_out_v = w_out[0].rearrange("(k p) n -> p k n", p=P)
        gu_v = ffn_gu[0].rearrange("(k p) n -> p k n", p=P)
        down_v = ffn_down[0].rearrange("(f p) n -> p f n", p=P)
        kv_v = kv_w.rearrange("(k p) n -> p k n", p=P)
        qg_v = fox_qg[0].rearrange("(k p) n -> p k n", p=P)
        fo_v = fox_out[0].rearrange("(k p) n -> p k n", p=P)

        def slot(s):
            return places[s % CORE][:, :]

        def slot_k(s):
            return slot(s).rearrange("p (k n) -> p k n", k=KT)

        def loads_of(s):
            if s < S_HG_OUT:
                col = [1, 0, 2, 1, 0, 2, 3, 3][s] * D + [0, 0, 0, 1, 1, 1, 0, 1][s] * N
                return [(slot_k(s), w_in_v[:, :, col:col + N])]
            if s < S_GU:
                n = s - S_HG_OUT
                return [(slot_k(s), w_out_v[:, :, n * N:(n + 1) * N])]
            if s < S_DOWN:
                c = s - S_GU
                half = slot(s).rearrange("p (h k n) -> p h k n", h=2, k=KT)
                return [(half[:, h], gu_v[:, :, h * FFN + c * T:h * FFN + (c + 1) * T]) for h in range(2)]
            if s < S_KVQG:
                f0 = (s - S_DOWN) * FT
                f1 = min(f0 + FT, FFN_TILES)
                return [(slot(s)[:, 0:(f1 - f0) * D].rearrange("p (f n) -> p f n", n=D), down_v[:, f0:f1, :])]
            if s < S_FOX_OUT:
                n = s - S_KVQG
                src = [kv_v, kv_v, qg_v, qg_v, kv_v, kv_v, qg_v, qg_v][n]
                col = [0, N, 0, N, D, D + N, D, D + N][n]
                return [(slot_k(s), src[:, :, col:col + N])]
            n = s - S_FOX_OUT
            return [(slot_k(s), fo_v[:, :, n * N:(n + 1) * N])]

        filled = [0] * len(places)
        ready_at = []
        for s in range(S_MOE):
            filled[s % CORE] += 16 * len(loads_of(s))
            ready_at.append(filled[s % CORE])

        def slot_landed(pe, s):
            pe.wait_ge(w_ready[s % CORE], ready_at[s])

        FOX_TILE0 = 24

        def slot_read(s):
            return lo_ready, slot_piece(s + 1)

        def hg_tile_of(p):
            return {0: p, 1: p, 2: 8, 3: p - 2, 4: p - 2, 5: 18, 6: 20, 7: 22}[p // 4]

        def hg_bank(n):
            return (2 + n) % 6 if n < 8 else n % 2

        def hg_bank_free(n):
            return max(0, n - 5) if n < 8 else 6 if n < 10 else n - 1

        def hg_pieces_of(n):
            return [1, 2, 3, 4, 5, 6, 7, 8, 12, 12, 13, 14, 15, 16, 17, 18, 19, 20, 24, 24, 28, 28, 32, 32][n]

        def slot_piece(s):
            return 4 * s - (4 * DOWN_SLOTS - FFN_TILES if s >= S_KVQG else 0)

        assert slot_piece(S_MOE) == P_MOE
        piece_at = [(s, q) for s in range(S_MOE) for q in range(slot_piece(s + 1) - slot_piece(s))]

        def piece_src(p):
            s, q = piece_at[p]
            if S_GU <= s < S_DOWN:
                w = slot(s).rearrange("p (h k n) -> p h k n", h=2, k=KT)
                return w[:, q % 2, :, (q // 2) * P:(q // 2 + 1) * P]
            if s in (0, 1, 3, 4) or S_KVQG <= s < S_KVQG + 4:
                return slot_k(s)[:, :, q * P:(q + 1) * P]
            return slot(s)[:, q * PC:(q + 1) * PC].rearrange("p (k n) -> p k n", k=KT)

        def moe_piece_src(piece):
            return moe_slot(piece // 4)[:, (piece % 4) * PC:(piece % 4 + 1) * PC]

        def part(w, p):
            return w[p % BUFS][:, :].rearrange("p (k n) -> p k n", k=KT)

        def moe_place(j):
            return MOE_PLACES[j % MOE_RING]

        def moe_slot(j):
            return places[moe_place(j)][:, :]

        def moe_slot_landed(eng, i, j):
            eng.wait_ge(w_ready[moe_place(j)],
                        i * (16 * MOE_SLOTS // MOE_RING) + filled[moe_place(j)] + 16 * (j // MOE_RING + 1))

        def moe_load(sp, e, j):
            kind, c = MOE_ORDER[j]
            if kind == "d":
                src = moe_down[0, e, c * N:(c + 1) * N, :].rearrange("(f p) n -> p f n", p=P)
                dst = moe_slot(j).rearrange("p (f n) -> p f n", n=D)
            else:
                col = c * N + (F if kind == "b" else 0)
                src = moe_gu[0, e, :, col:col + N].rearrange("(k p) n -> p k n", p=P)
                dst = moe_slot(j).rearrange("p (k n) -> p k n", k=KT)
            sp.dma_start(dst, src).then_inc(w_ready[moe_place(j)], 16)

        block = ctx.enter_context(nc.Block())

        @block.sync
        def _(sp):
            with nc.allow_non_contiguous_dma("small parameters"):
                sp.dma_start(lbt, lb_logits[0].rearrange("(h p) -> p h", p=P)).then_inc(small_loaded, 16)
                sp.dma_start(fgb[:, :], fgate_b.rearrange("(p a) -> p a", a=1)).then_inc(small_loaded, 16)
            sp.dma_start(xres[:, :, :], x[0].rearrange("(t p) n -> p t n", p=P)).then_inc(x_loaded, 16)
            for s in range(S_MOE):
                if s >= CORE:
                    sp.wait_ge(*slot_read(s - CORE))
                for dst, src in loads_of(s):
                    sp.dma_start(dst, src).then_inc(w_ready[s % CORE], 16)
            for j in range(MOE_RING):
                if moe_place(j) < CORE:
                    last = [s for s in range(S_MOE) if s % CORE == moe_place(j)][-1]
                    sp.wait_ge(*slot_read(last))
                elif moe_place(j) > CORE:
                    sp.wait_ge(tp_done, 20)
                moe_load(sp, 0, j)

            def rest_of(i, e):
                for j in range(MOE_RING, MOE_SLOTS):
                    sp.wait_ge(lo_ready, P_MOE + i * MOE_PIECES + 4 * (j - MOE_RING + 1))
                    moe_load(sp, e, j)

            def first_of(i, e):
                for j in range(MOE_RING):
                    sp.wait_ge(lo_ready, P_MOE + i * MOE_PIECES - 4 * (MOE_RING - j - 1))
                    moe_load(sp, e, j)

            with sp.Fori(0, E - 1) as i:
                rest_of(i, i)
                first_of(i + 1, i + 1)
            rest_of(E - 1, E - 1)
            sp.wait_ge(items_ready, 2)
            more = sp.value_load(items[0:1, 16:17], min_val=0, max_val=3)
            with sp.If(more > 0):
                with sp.Fori(0, more) as n:
                    col = sp.value_load(items[0:1, bass.ds(n + E, 1)], min_val=E, max_val=2 * E - 1)
                    first_of(n + E, col - E)
                    rest_of(n + E, col - E)
            for t in range(TB):
                sp.wait_ge(x_ready, 12 + 2 * (t + 1))
                sp.dma_start(out[0, t * P:(t + 1) * P, :], yacc[:, t, :]).then_inc(out_done, 16)
            sp.wait_ge(out_done, 16 * TB)

        @block.tensor
        def _(pe):
            def transpose_rows(stage, src, ready):
                for g in range(2 * TB):
                    t, half = divmod(g, 2)
                    pe.wait_ge(*ready(t, half))
                    if t:
                        pe.wait_ge(tp_lo, 4 * stage + half + 1)
                    for j in range(4):
                        k = 4 * half + j
                        mm = pe.transpose(ps[:, 6 + half, j * P:(j + 1) * P], src[:, t, k * P:(k + 1) * P], ident)
                    mm.then_inc(tp_done, 1)

            def xT_ready(stage):
                pe.wait_ge(tp_lo, 4 * stage + 4)

            def proj_bank(n):
                if n >= 2:
                    pe.wait_ge(pj_out, n - 1)
                return n % 2

            def level(g, l):
                m, c = BUF_LEVELS * g + l, LEVELS * g + l
                if l < len(HALVES):
                    pe.wait_ge(qt_ready, m + 1)
                    pe.wait_ge(kt_ready, m + 1)
                    kk, qq = lev_k[m % 2], lev_q[m % 2]
                else:
                    kk, qq = hk[:, g * 1024:(g + 1) * 1024], hq[:, g * 1024:(g + 1) * 1024]
                if c >= 2:
                    pe.wait_ge(sc_sel, 2 * (c - 1))
                if l < len(HALVES):
                    for u in range(8):
                        cols = slice(u * P, (u + 1) * P)
                        mm = pe.matmul(ps[:, 2 + 2 * (c % 2), u * 64:(u + 1) * 64]
                                       .rearrange("p (n h) -> p n h", h=HALVES[l]),
                                       kk[:, cols], half_of(qq[:, cols], HALVES[l], 1), start=True, stop=True)
                    mm.then_inc(sc_done, 2)
                else:
                    for h in range(2):
                        for u in range(4):
                            cols = slice((4 * h + u) * P, (4 * h + u + 1) * P)
                            mm = pe.matmul(ps[:, 2 + 2 * (c % 2) + h, u * P:(u + 1) * P], kk[:, cols],
                                           qq[:, cols], start=True, stop=True)
                        mm.then_inc(sc_done, 1)

            def attend_state(g):
                if g:
                    pe.wait_ge(at_out, 4 * g)
                pe.wait_ge(kt_ready, BUF_LEVELS * (g + 1))
                kk = lev_k[1]
                for h in range(4):
                    mm = pe.transpose(ps[:, 6, h * P:(h + 1) * P], kk[:, 2 * h * P:(2 * h + 1) * P], ident)
                mm.then_inc(at_done, 1)

            def attend(g):
                pe.wait_ge(at_out, 4 * g + 1)
                pe.wait_ge(pj_out, 10 + 10 * g)
                for h in range(4):
                    mm = pe.matmul(ps[:, 7, h * P:(h + 1) * P], khatT[:, h * P:(h + 1) * P],
                                   hv[:, 0, (4 * g + h) * P:(4 * g + h + 1) * P], start=True, stop=True)
                mm.then_inc(at_done, 1)
                pe.wait_ge(sc_sel, 2 * LEVELS * (g + 1))
                for h in range(4):
                    mm = pe.matmul(ps[:, 6, h * P:(h + 1) * P], scT[:, 2 * h * P:(2 * h + 1) * P],
                                   hv[:, 0, (4 * g + h) * P:(4 * g + h + 1) * P], start=True, stop=True)
                mm.then_inc(at_done, 1)
                pe.wait_ge(at_out, 4 * g + 2)
                pe.wait_ge(qt_ready, BUF_LEVELS * (g + 1))
                qq = lev_q[1]
                for h in range(4):
                    pe.matmul(ps[:, 7, h * P:(h + 1) * P], scT[:, (2 * h + 1) * P:(2 * h + 2) * P],
                              hv[:, 1, (4 * g + h) * P:(4 * g + h + 1) * P], start=True, stop=False)
                    mm = pe.matmul(ps[:, 7, h * P:(h + 1) * P], qq[:, (2 * h + 1) * P:(2 * h + 2) * P],
                                   state[:, h * P:(h + 1) * P], start=False, stop=True)
                mm.then_inc(at_done, 1)

            def three_products(dst, xh, xl, h, l, start, stop):
                pe.matmul(dst, xh, h, start=start, stop=False)
                pe.matmul(dst, xh, l, start=False, stop=False)
                return pe.matmul(dst, xl, h, start=False, stop=stop)

            def three_products_turned(dst, h, l, xh, xl, start, stop):
                pe.matmul(dst, h, xh, start=start, stop=False)
                pe.matmul(dst, h, xl, start=False, stop=False)
                return pe.matmul(dst, l, xh, start=False, stop=stop)

            def piece_ready(p):
                pe.wait_ge(lo_ready, p + 1)

            def token_rows(p, q, t, dst):
                for k in (2 * q, 2 * q + 1):
                    cols, rows = slice((k % 2) * N, (k % 2 + 1) * N), slice(t * P, (t + 1) * P)
                    mm = three_products(dst, xTh[:, k, rows], xTl[:, k, rows],
                                        wh[p % BUFS][:, cols], wl[p % BUFS][:, cols], k == 0, k == KT - 1)
                return mm

            def token_piece(p, q, banks):
                piece_ready(p)
                token_rows(p, q, 0, bank(banks[0]))
                token_rows(p, q, 1, bank(banks[1])).then_inc(pieces_used, 1)

            def feature_piece(p, dst):
                piece_ready(p)
                h, l = part(wh, p), part(wl, p)
                for k in range(KT):
                    mm = three_products_turned(dst, h[:, k, :], l[:, k, :], xTh[:, k, :], xTl[:, k, :],
                                               k == 0, k == KT - 1)
                mm.then_inc(pieces_used, 1)

            def out_projection(p0):
                for q in range(4):
                    token_piece(p0 + q, q, (2, 3))
                for q in range(4):
                    piece_ready(p0 + 4 + q)
                    mm = token_rows(p0 + 4 + q, q, 0, bank(4))
                mm.then_inc(y_first, 1)
                for q in range(4):
                    token_rows(p0 + 4 + q, q, 1, bank(5)).then_inc(pieces_used, 1)

            def hg_piece(p):
                n, tokens = hg_tile_of(p), p // 4 not in (0, 1, 3, 4)
                free = hg_bank_free(n + tokens)
                if free and not (tokens and p % 4):
                    pe.wait_ge(pj_out, free)
                if tokens:
                    token_piece(p, p % 4, (0, 1))
                else:
                    feature_piece(p, ps[:, hg_bank(n), 0:T])

            pe.wait_ge(consts_loaded, 16)
            transpose_rows(0, xres, lambda t, half: (x_loaded, 16))
            xT_ready(0)
            for p in range(13):
                hg_piece(p)
            for l in range(LEVELS):
                hg_piece(13 + l)
                if l == LEVELS - 1:
                    hg_piece(14 + l)
                    pe.wait_ge(q_ready, 1)
                    pe.wait_ge(b_ready, 1)
                level(0, l)
            attend_state(0)
            hg_piece(22)
            hg_piece(23)
            attend(0)
            hg_piece(24)
            for l in range(LEVELS):
                if l < LEVELS - 1:
                    hg_piece(25 + l)
                else:
                    pe.wait_ge(q_ready, 2)
                    pe.wait_ge(b_ready, 2)
                level(1, l)
            attend_state(1)
            attend(1)
            transpose_rows(1, ho, lambda t, half: (on_ready, 2 * t + half + 1))
            xT_ready(1)
            out_projection(P_HG_OUT)

            transpose_rows(2, xres, lambda t, half: (x_ready, 2 * t + half + 1))
            xT_ready(2)
            for f in range(FFN_TILES):
                if f >= 2:
                    pe.wait_ge(ffn_prod, f - 1)
                for h in range(2):
                    feature_piece(P_GU + 2 * f + h, ps[:, f % 2, h * T:(h + 1) * T])

            def down_piece(f, t):
                rows, p = slice(t * P, (t + 1) * P), P_DOWN + f
                for n in range(2):
                    cols = slice(n * N, (n + 1) * N)
                    mm = three_products(bank(2 + 2 * n + t), hTh[:, f, rows], hTl[:, f, rows],
                                        wh[p % BUFS][:, cols], wl[p % BUFS][:, cols],
                                        f == 0, f == FFN_TILES - 1)
                return mm

            for f in range(FFN_TILES):
                piece_ready(P_DOWN + f)
                pe.wait_ge(ffn_h, f + 1)
                mm = down_piece(f, 0)
                if f < FFN_TILES - BUFS:
                    down_piece(f, 1).then_inc(pieces_used, 1)
            mm.then_inc(y_first, 1)
            for f in range(FFN_TILES - BUFS, FFN_TILES):
                down_piece(f, 1).then_inc(pieces_used, 1)

            transpose_rows(3, xres, lambda t, half: (x_ready, 4 + 2 * t + half + 1))
            xT_ready(3)
            pe.wait_ge(small_lo, 1)
            for k in range(KT):
                mm = three_products_turned(ps[0:FOX_HEADS, 0, 0:T], fgate_part(wsh)[:, k, :],
                                           fgate_part(wsl)[:, k, :], xTh[:, k, :], xTl[:, k, :],
                                           k == 0, k == KT - 1)
            mm.then_inc(pj_done, 1)
            for n in range(16):
                b = proj_bank(FOX_TILE0 + 1 + n)
                feature_piece(P_KVQG + n, ps[:, b, 0:T])

            def fox_token_piece(m):
                n = FOX_TILE0 + 17 + 2 * (m // 4)
                if m % 4 == 0:
                    proj_bank(n + 1)
                token_piece(P_KVQG + 16 + m, m % 4, (n % 2, (n + 1) % 2))

            for m in range(4):
                fox_token_piece(m)
            pe.wait_ge(c_ready, 1)
            for t in range(TB):
                mm = pe.transpose(ps[:, 6, t * FOX_HEADS:(t + 1) * FOX_HEADS], fc[:, t * P:(t + 1) * P],
                                  sq[0:FOX_HEADS, 0:FOX_HEADS])
            mm.then_inc(cT_done, 1)
            pe.wait_ge(fox_loaded, 32)

            def fox_scores(h):
                if h >= 2:
                    pe.wait_ge(fx_max, h - 1)
                if h == 0:
                    pe.wait_ge(pj_out, FOX_TILE0 + 17)
                rows = slice((h % 2) * 64, (h % 2) * 64 + 64)
                for t in range(TB):
                    dst = ps[:, 2 + h % 2, t * P:t * P + (t + 1) * P]
                    pe.matmul(dst, negsel[:, h:h + 1].to_broadcast([FOX_HEADS, P]), fc[:, 0:(t + 1) * P],
                              start=True, stop=False)
                    mm = pe.matmul(dst, fq[rows, h // 2, t * P:(t + 1) * P], fk[rows, h // 2, 0:(t + 1) * P],
                                   start=False, stop=True)
                mm.then_inc(fx_qk, 1)

            def fox_turn(h):
                pe.wait_ge(fx_exp, h + 1)
                if h >= 2:
                    pe.wait_ge(fx_ptc, h - 1)
                for j in range(3):
                    mm = pe.transpose(ps[:, 4 + h % 2, j * P:(j + 1) * P], fprob[h % 2][:, j * P:(j + 1) * P], ident)
                mm.then_inc(fx_pt, 1)

            def fox_values(h):
                pe.wait_ge(fx_ptc, h + 1)
                if h == 0:
                    pe.wait_ge(cT_ready, 1)
                    pe.wait_ge(pj_out, FOX_TILE0 + 19)
                if h == 8:
                    pe.wait_ge(pj_out, FOX_TILE0 + 21)
                if h >= 2:
                    pe.wait_ge(fx_out, h - 1)
                cols = slice(h * FOX_DIM, (h + 1) * FOX_DIM)
                pT = fprobT[h % 2]
                pe.matmul(ps[:, 6 + h % 2, 0:64], pT[:, 0:P], fv[:, 0, cols], start=True, stop=True)
                pe.matmul(ps[:, 6 + h % 2, 64:128], pT[:, P:2 * P], fv[:, 0, cols], start=True, stop=False)
                pe.matmul(ps[:, 6 + h % 2, 64:128], pT[:, 2 * P:3 * P], fv[:, 1, cols], start=False,
                          stop=True).then_inc(fx_pv, 1)

            for h in range(FOX_HEADS + 2):
                if h < FOX_HEADS:
                    fox_scores(h)
                if 1 <= h <= FOX_HEADS:
                    fox_turn(h - 1)
                if h >= 2:
                    fox_values(h - 2)
                if h < 12:
                    fox_token_piece(4 + h)
            transpose_rows(4, fo, lambda t, half: (og_ready, t + 1))
            xT_ready(4)
            out_projection(P_FOX_OUT)

            transpose_rows(5, xres, lambda t, half: (x_ready, 8 + 2 * t + half + 1))
            xT_ready(5)
            for k in range(KT):
                mm = three_products_turned(ps[0:E, 0, 0:T], router_part(wsh)[:, k, :], router_part(wsl)[:, k, :],
                                           xTh[:, k, :], xTl[:, k, :], k == 0, k == KT - 1)
            mm.then_inc(lgT_done, 1)
            pe.wait_ge(lgT_copied, 1)
            for t in range(TB):
                mm = pe.transpose(ps[:, 6, t * E:(t + 1) * E], lgT[:, t * P:(t + 1) * P], sq[0:E, 0:E])
            mm.then_inc(lg_done, 1)
            pe.wait_ge(sel_ready, 1)
            sel = rt[8]
            pe.matmul(ps[:, 1, 0:E], before, sel[:, 0:E], start=True, stop=True)
            pe.matmul(ps[:, 1, E:2 * E], ones, sel[:, 0:E], start=True, stop=False)
            pe.matmul(ps[:, 1, E:2 * E], before, sel[:, E:2 * E], start=False, stop=True)
            pe.matmul(ps[0:1, 1, 2 * E:3 * E], ones[:, 0:1], sel[:, 0:E], start=True, stop=False)
            pe.matmul(ps[0:1, 1, 2 * E:3 * E], ones[:, 0:1], sel[:, E:2 * E], start=False,
                      stop=True).then_inc(rk_done, 1)

            def gather(i, half):
                if half == 0:
                    pe.wait_ge(pick_ready, i + 1)
                for j in range(4):
                    k = 4 * half + j
                    for t in range(TB):
                        for part in (x3h, x3l):
                            mm = pe.matmul(ps[:, 7 - half, j * P:(j + 1) * P], part[:, t, k * P:(k + 1) * P],
                                           pick[:, t, :], start=(t == 0 and part is x3h),
                                           stop=(t == TB - 1 and part is x3l))
                mm.then_inc(ga_done, 1)

            def gate_or_up(i, c, kind):
                b = 2 * (c % 2) + (kind == "b")
                for k in range(KT):
                    piece = P_MOE + 4 * MOE_ORDER.index((kind, c)) + k // 2
                    if c == 0 and kind == "a" and k in (0, 4):
                        pe.wait_ge(xe_ready, 2 * i + 1 + k // 4)
                    if k % 2 == 0:
                        piece_ready(i * MOE_PIECES + piece)
                    cols = slice((k % 2) * N, (k % 2 + 1) * N)
                    mm = three_products(bank(b), xeh[:, k, :], xel[:, k, :], wh[piece % BUFS][:, cols],
                                        wl[piece % BUFS][:, cols], k == 0, k == KT - 1)
                    if k % 2:
                        mm.then_inc(pieces_used, 1)

            def turn_h(i, c):
                pe.wait_ge(h_ready, i * CH + c + 1)
                for f in range(FT):
                    mm = pe.transpose(ps[:, 6, f * P:(f + 1) * P], eh[:, f * P:(f + 1) * P], ident)
                mm.then_inc(htr_done, 1)

            def down(i, c):
                pe.wait_ge(hT_ready, i * CH + c + 1)
                for f in range(FT):
                    piece = P_MOE + 4 * MOE_ORDER.index(("d", c)) + f
                    piece_ready(i * MOE_PIECES + piece)
                    rows = slice(f * P, (f + 1) * P)
                    for n in range(2):
                        cols = slice(n * N, (n + 1) * N)
                        mm = three_products(bank(4 + n), ehTh[:, rows], ehTl[:, rows], wh[piece % BUFS][:, cols],
                                            wl[piece % BUFS][:, cols], c == 0 and f == 0,
                                            c == CH - 1 and f == FT - 1)
                    mm.then_inc(pieces_used, 1)

            def item(i):
                gate_or_up(i, 0, "a")
                gate_or_up(i, 0, "b")
                pe.wait_ge(yacc_up, 4 * i + 2)
                pe.wait_ge(weights_ready, i + 1)
                for t in range(TB):
                    pe.transpose(ps[:, 6, t * P:(t + 1) * P], pick[:, t, :].bitcast(F32), ident)
                for t in range(TB):
                    mm = pe.matmul(ps[:, 6, 2 * P:2 * P + 1], pick[:, t, :].bitcast(F32), cur[:, 2 + t:3 + t],
                                   start=(t == 0), stop=(t == TB - 1))
                mm.then_inc(spr_done, 1)
                for c in range(1, CH):
                    gate_or_up(i, c, "a")
                    if c == 1:
                        pe.wait_ge(spr_ready, i + 1)
                    turn_h(i, c - 1)
                    gate_or_up(i, c, "b")
                    down(i, c - 1)
                turn_h(i, CH - 1)
                gather(i + 1, 0)
                down(i, CH - 1)
                gather(i + 1, 1)
                for n in range(2):
                    for t in range(TB):
                        pe.wait_ge(ye_ready, 2 * i + n + 1)
                        if n == 0:
                            pe.wait_ge(xe_ready, 2 * i + 3 + t)
                        dst = bank([7, 6, 2, 3][2 * n + t])
                        pe.matmul(dst, spread[:, t, :], yeh[:, n, :], start=True, stop=False)
                        pe.matmul(dst, spread[:, t, :], yel[n], start=False, stop=True).then_inc(sc2_done, 1)

            pe.wait_ge(x3_ready, TB)
            gather(0, 0)
            gather(0, 1)
            with pe.Fori(0, E) as i:
                item(i)
            more = pe.value_load(items[0:1, 16:17], min_val=0, max_val=3)
            with pe.If(more > 0):
                with pe.Fori(0, more) as n:
                    item(n + E)

        @block.scalar
        def _(act):
            step = Steps(act, act_steps)

            def turned(stage, t):
                for half in range(2):
                    act.wait_ge(tp_done, 4 * stage + 2 * t + half + 1)
                    act.activation(xTh[:, 4 * half:4 * half + 4, t * P:(t + 1) * P],
                                   bank(6 + half).rearrange("p (k t) -> p k t", k=4), ACT.Copy).then_inc(tp_hi, 1)

            def hi(p):
                wait = p - BUFS + 1
                if p >= P_MOE:
                    if p == P_MOE:
                        moe_slot_landed(act, 0, 0)
                    src, dst = moe_piece_src(p - P_MOE), wh[p % BUFS][:, :]
                else:
                    if piece_at[p][1] == 0:
                        slot_landed(act, piece_at[p][0])
                    src, dst = piece_src(p), part(wh, p)
                if wait > 0:
                    act.wait_ge(pieces_used, wait)
                act.activation(dst, src, ACT.Copy).then_inc(hi_ready, 1)

            split = [0]

            def ahead(p):
                for n in range(split[0], min(p, P_MOE + BUFS)):
                    hi(n)
                    split[0] = n + 1

            def wait_piece(p, beyond=BUFS):
                ahead(p + beyond)
                act.wait_ge(pieces_used, p)

            def copy_tile(n, dst, cols=N):
                wait_piece(hg_pieces_of(n), BUFS if cols == T else 2)
                act.activation(dst, bank(hg_bank(n), cols), ACT.Copy).then_inc(pj_out, 1)

            act.dma_start(sq[:, :], c_square).then_inc(consts_loaded, 16)
            act.dma_start(lev_k[0], c_levels).then_inc(levels_loaded, 16)
            act.wait_ge(lb_ready, 1)
            act.activation(lbt, sm[:, 32:40], ACT.Exp).then_inc(lb_exp, 1)
            act.wait_ge(lb_ready, 2)
            step(act.activation(loglb, sm[:, 40:48], ACT.Ln, scale=2.0 ** LN_SHIFT))
            act.activation(loglb, loglb, ACT.Copy, bias=-LN_SHIFT * LN2).then_inc(loglb_ready, 1)
            turned(0, 0)
            turned(0, 1)

            def hg_copy(n):
                if n in (0, 1, 2, 3, 10, 11, 12, 13):
                    h = n if n < 4 else n - 6
                    copy_tile(n, zb[:, h * T:(h + 1) * T], cols=T)
                elif n in (4, 5, 6, 7, 14, 15, 16, 17):
                    h = n - 4 if n < 8 else n - 10
                    copy_tile(n, hq[:, h * T:(h + 1) * T], cols=T)
                elif n < 20:
                    t, g = n % 2, n // 18
                    copy_tile(n, hv[:, t, g * N:(g + 1) * N])
                else:
                    t, g = n % 2, (n - 20) // 2
                    copy_tile(n, hg[:, t, g * N:(g + 1) * N])

            def log_gates_a(g, p):
                z = zb[:, g * 1024:(g + 1) * 1024]
                act.wait_ge(pj_out, 4 + 10 * g)
                if g:
                    act.wait_ge(b_ready, 1)
                step(act.activation(ph_l, z, ACT.Abs))
                ahead(p - 1)
                step(act.activation(ph_l, ph_l, ACT.Exp, scale=-1.0))
                ahead(p)
                act.activation(ph_l, ph_l, ACT.Ln, bias=1.0).then_inc(sp_log, 1)

            def log_gates_b(g, p):
                k = hk[:, g * 1024:(g + 1) * 1024]
                act.wait_ge(sp_sum, g + 1)
                for h in range(4):
                    ins = act.activation(ph_l[:, h * T:(h + 1) * T], zb[:, (4 * g + h) * T:(4 * g + h + 1) * T],
                                         ACT.Abs, bias=nloglb[:, 4 * g + h:4 * g + h + 1])
                step(ins)
                ahead(p - 1)
                step(act.activation(ph_l, ph_l, ACT.Exp, scale=-1.0))
                ahead(p)
                act.activation(ph_l, ph_l, ACT.Ln, bias=1.0).then_inc(rlog_ready, 1)
                act.wait_ge(floor_max, g + 1)
                act.activation(k, k, ACT.Exp, scale=-1.0).then_inc(kexp_ready, 1)

            def silu_q(g):
                act.wait_ge(pj_out, 8 + 10 * g)
                q = hq[:, g * 1024:(g + 1) * 1024]
                act.activation(q, q, ACT.Silu).then_inc(q_ready, 1)

            def level_exp(g, l):
                m = BUF_LEVELS * g + l
                e = lev_e[m % 2]
                if l < len(HALVES):
                    act.wait_ge(diff_ready, len(HALVES) * g + l + 1)
                    act.activation(e, e, ACT.Exp).then_inc(exp_ready, 1)
                    return
                act.wait_ge(kt_ready, m - 1)
                act.wait_ge(qt_ready, m - 1)
                for h in range(4):
                    b = zb[:, (4 * g + h) * T:(4 * g + h + 1) * T]
                    act.activation(e[:, h * T:h * T + P], b[:, 0:P], ACT.Exp, scale=-1.0, bias=b[:, P - 1:P])
                    ins = act.activation(e[:, h * T + P:(h + 1) * T], b[:, P:T], ACT.Exp)
                ins.then_inc(exp_ready, 1)

            def attn_copies(g, first, last):
                for n in range(first, last):
                    act.wait_ge(at_done, 4 * g + n + 1)
                    dst = [khatT, state, ho[:, 0, g * N:(g + 1) * N], ho[:, 1, g * N:(g + 1) * N]][n]
                    act.activation(dst, bank(6 + n % 2), ACT.Copy).then_inc(at_out, 1)

            for n in range(4):
                hg_copy(n)
            act.wait_ge(lb_ready, 3)
            log_gates_a(0, 10)
            hg_copy(4)
            hg_copy(5)
            log_gates_b(0, 12)
            hg_copy(6)
            hg_copy(7)
            hg_copy(8)
            hg_copy(9)
            silu_q(0)
            level_exp(0, 0)
            level_exp(0, 1)
            ahead(15)
            level_exp(0, 2)
            hg_copy(10)
            level_exp(0, 3)
            for l in range(4, len(HALVES) + 1):
                hg_copy(7 + l)
                level_exp(0, l)
            hg_copy(15)
            log_gates_a(1, 22)
            hg_copy(16)
            hg_copy(17)
            log_gates_b(1, 24)
            attn_copies(0, 0, 1)
            silu_q(1)
            hg_copy(18)
            hg_copy(19)
            attn_copies(0, 1, 4)
            level_exp(1, 0)
            level_exp(1, 1)
            ahead(27)
            level_exp(1, 2)
            ahead(28)
            level_exp(1, 3)
            ahead(29)
            level_exp(1, 4)
            ahead(30)
            act.wait_ge(b_ready, 2)
            hg_copy(20)
            hg_copy(21)
            level_exp(1, 5)
            ahead(31)
            level_exp(1, 6)
            ahead(32)
            level_exp(1, 7)
            hg_copy(22)
            hg_copy(23)
            act.wait_ge(pj_out, 24)
            act.activation(A[:, 8192:10240], A[:, 8192:10240], ACT.Silu).then_inc(hg_silu, 1)
            attn_copies(1, 0, 3)
            act.wait_ge(kt_ready, 2 * BUF_LEVELS)
            act.wait_ge(qt_ready, 2 * BUF_LEVELS)
            for t in range(TB):
                act.wait_ge(at_out, 7 + t)
                act.activation(lev_e[t], ho[:, t, :], ACT.Square).then_inc(sq_ready, 1)
                if t == 0:
                    attn_copies(1, 3, 4)
            for t in range(TB):
                act.wait_ge(ms_ready, t + 1)
                act.activation(ssq[:, t, :], ssq[:, t, :], ACT.Sqrt).then_inc(rms_ready, 1)
            turned(1, 0)
            turned(1, 1)

            def ln_sqrt(k, t):
                act.wait_ge(ln_var, TB * k + t + 1)
                act.activation(std[:, t:t + 1], mv[:, t, 1:2], ACT.Sqrt).then_inc(ln_std, 1)

            def load_sqrt():
                act.wait_ge(consts_loaded, 16)
                act.activation(sm[:, 78:79], ones[:, 0:1], ACT.Sqrt)

            def layer_norm(k, last, stage):
                ahead(last)
                load_sqrt()
                ln_sqrt(k, 0)
                ahead(last + 1)
                turned(stage, 0)
                ln_sqrt(k, 1)
                turned(stage, 1)
                ahead(last + BUFS)

            layer_norm(0, P_GU, 2)
            act.wait_ge(route_loaded, 80)
            act.activation(wsh, w_small, ACT.Copy).then_inc(small_hi, 1)

            def h_high(f):
                act.wait_ge(ffn_prod, f + 1)
                act.activation(hTh[:, f, :], ffn_p[f % 2], ACT.Copy).then_inc(ffn_hi, 1)

            for f in range(FFN_TILES):
                wait_piece(P_GU + 2 * f + 2)
                if f >= 2:
                    act.wait_ge(ffn_prod, f - 1)
                act.activation(ffn_s[f % 2], ps[:, f % 2, 0:T], ACT.Silu).then_inc(ffn_silu, 1)
                if f:
                    h_high(f - 1)
            ahead(P_DOWN + BUFS)
            h_high(FFN_TILES - 1)
            layer_norm(1, P_KVQG, 3)

            act.wait_ge(pj_done, 1)
            act.wait_ge(small_loaded, 32)
            act.activation(fz, ps[0:FOX_HEADS, 0, 0:T], ACT.Identity, bias=fgb[:, 0:1]).then_inc(pj_out, 1)
            act.wait_ge(pj_out, FOX_TILE0 + 1)
            step(act.activation(fl, fz, ACT.Abs))
            step(act.activation(fl, fl, ACT.Exp, scale=-1.0))
            act.activation(fl, fl, ACT.Ln, bias=1.0).then_inc(f_log, 1)
            for n in range(16):
                wait_piece(P_KVQG + n + 1)
                act.activation((fk, fq)[n // 8][:, n % 8, :], bank((FOX_TILE0 + 1 + n) % 2, T), ACT.Copy,
                               scale=1.0 if n < 8 else FOX_DIM ** -0.5).then_inc(pj_out, 1)

            def fox_copies(m):
                wait_piece(P_KVQG + 16 + 4 * (m + 1))
                for t in range(TB):
                    act.activation((fv, fg)[m // 2][:, t, (m % 2) * N:(m % 2 + 1) * N],
                                   bank((FOX_TILE0 + 17 + t) % 2), ACT.Copy).then_inc(pj_out, 1)

            fox_copies(0)
            for h in range(FOX_HEADS + 1):
                if h <= 12:
                    wait_piece(P_KVQG + 20 + h)
                if h < FOX_HEADS:
                    act.wait_ge(fx_max, h + 1)
                    if h >= 2:
                        act.wait_ge(fx_pt, h - 1)
                    for t in range(TB):
                        cols = slice(0, P) if t == 0 else slice(P, KW)
                        c = 2 * h + t
                        ins = act.activation(fprob[h % 2][:, cols], flog[h % 2][:, cols], ACT.Exp,
                                             bias=nmax[:, c:c + 1], accum_out=rsum[:, c:c + 1])
                    ins.then_inc(fx_exp, 1)
                if h >= 1:
                    act.wait_ge(fx_pt, h)
                    if h >= 3:
                        act.wait_ge(fx_pv, h - 2)
                    act.activation(fprobT[(h - 1) % 2], bank(4 + (h - 1) % 2, KW), ACT.Copy).then_inc(fx_ptc, 1)
                if h in (3, 7, 11):
                    fox_copies((h + 1) // 4)
            act.wait_ge(pj_out, FOX_TILE0 + 25)
            for t in range(TB):
                act.activation(fg[:, t, :], fg[:, t, :], ACT.Sigmoid).then_inc(fg_sig, 1)
            turned(4, 0)
            turned(4, 1)
            layer_norm(2, P_MOE, 5)
            for t in range(TB):
                act.activation(x3h[:, t, :], xres[:, t, :], ACT.Copy).then_inc(x3_hi, 1)
            act.wait_ge(lgT_done, 1)
            act.activation(lgT, ps[0:E, 0, 0:T], ACT.Copy).then_inc(lgT_copied, 1)
            act.wait_ge(e2_in, 1)
            act.activation(rt[9][:, 0:2], rt[9][:, 2:4], ACT.Exp).then_inc(e2_out, 1)

            def hi(i, piece):
                i, piece = i + piece // MOE_PIECES, piece % MOE_PIECES
                if piece % 4 == 0:
                    moe_slot_landed(act, i, piece // 4)
                act.wait_ge(pieces_used, P_MOE + i * MOE_PIECES + piece - BUFS + 1)
                act.activation(wh[(P_MOE + piece) % BUFS][:, :], moe_piece_src(piece), ACT.Copy)\
                   .then_inc(hi_ready, 1)

            def rows_hi(i, half):
                act.wait_ge(ga_done, 2 * i + half + 1)
                act.activation(xeh[:, 4 * half:4 * half + 4, :],
                               bank(7 - half).rearrange("p (k t) -> p k t", k=4), ACT.Copy).then_inc(xe_hi, 1)

            def hT_high(i, c):
                act.wait_ge(htr_done, i * CH + c + 1)
                act.activation(ehTh[:, :], bank(6), ACT.Copy).then_inc(hT_hi, 1)

            def item(i, first, last):
                done = first
                for c in range(CH):
                    a_end = moe_end("a", c)
                    for piece in range(done, a_end + BUFS - 1):
                        hi(i, piece)
                    if c:
                        hT_high(i, c - 1)
                    hi(i, a_end + BUFS - 1)
                    done = a_end + BUFS
                    if c:
                        act.wait_ge(h_ready, i * CH + c)
                    act.wait_ge(pieces_used, P_MOE + i * MOE_PIECES + a_end)
                    act.activation(gate_s, bank(2 * (c % 2)), ACT.Silu).then_inc(silu_done, 1)
                for piece in range(done, MOE_PIECES - 1):
                    hi(i, piece)
                hT_high(i, CH - 1)
                hi(i, MOE_PIECES - 1)
                rows_hi(i + 1, 0)
                for piece in range(MOE_PIECES, last - 2):
                    hi(i, piece)
                act.wait_ge(pieces_used, P_MOE + (i + 1) * MOE_PIECES)
                act.wait_ge(spr_ready, i + 1)
                for n in range(2):
                    act.activation(yeh[:, n, :], bank(4 + n), ACT.Identity, scale=slot_weight)\
                       .then_inc(ye_hi, 1)
                rows_hi(i + 1, 1)
                for piece in range(max(MOE_PIECES, last - 2), last):
                    hi(i, piece)

            rows_hi(0, 0)
            rows_hi(0, 1)
            with act.Fori(0, E - 1) as i:
                item(i, BUFS, MOE_PIECES + BUFS)
            item(E - 1, BUFS, MOE_PIECES)
            act.wait_ge(items_ready, 2)
            more = act.value_load(items[0:1, 16:17], min_val=0, max_val=3)
            with act.If(more > 0):
                with act.Fori(0, more) as n:
                    item(n + E, 0, MOE_PIECES)
            load_sqrt()
            for t in range(TB):
                ln_sqrt(3, t)

        @block.vector
        def _(dve):
            step = Steps(dve, dve_steps)

            def turned(stage, t):
                for half in range(2):
                    rows = (slice(None), slice(4 * half, 4 * half + 4), slice(t * P, (t + 1) * P))
                    dve.wait_ge(tp_hi, 4 * stage + 2 * t + half + 1)
                    dve.tensor_tensor(xTl[rows], bank(6 + half).rearrange("p (k t) -> p k t", k=4),
                                      xTh[rows].bitcast(F32), ALU.subtract).then_inc(tp_lo, 1)

            def lo(p):
                dve.wait_ge(hi_ready, p + 1)
                if p >= P_MOE:
                    dve.tensor_tensor(wl[p % BUFS][:, :], moe_piece_src(p - P_MOE), wh[p % BUFS][:, :].bitcast(F32),
                                      ALU.subtract).then_inc(lo_ready, 1)
                else:
                    dve.tensor_tensor(part(wl, p), piece_src(p), part(wh, p).bitcast(F32),
                                      ALU.subtract).then_inc(lo_ready, 1)

            split = [0]

            def ahead(p):
                for n in range(split[0], min(p, P_MOE + BUFS)):
                    lo(n)
                    split[0] = n + 1

            def wait_piece(p):
                ahead(p + BUFS)
                dve.wait_ge(pieces_used, p)

            step(dve.memset(scT, 0.0))
            dve.wait_ge(small_loaded, 32)
            dve.tensor_tensor(sm[:, 32:40], lbt, lbt, ALU.subtract).then_inc(lb_ready, 1)
            dve.wait_ge(lb_exp, 1)
            step(dve.reciprocal(sm[:, 32:40], lbt))
            step(dve.tensor_tensor(lbt, lbt, sm[:, 32:40], ALU.mult))
            step(dve.tensor_tensor(lbt, lbt, lbt, ALU.subtract))
            step(dve.tensor_scalar(one_m_lb, lbt, -1.0, 1.0, ALU.mult, ALU.add))
            dve.tensor_scalar(sm[:, 40:48], lbt, LB_FLOOR, None, ALU.max).then_inc(lb_ready, 1)
            dve.wait_ge(loglb_ready, 1)
            dve.tensor_scalar(nloglb, loglb, -1.0, None, ALU.mult).then_inc(lb_ready, 1)
            turned(0, 0)
            turned(0, 1)

            def log_gates_a(g):
                z, k = zb[:, g * 1024:(g + 1) * 1024], hk[:, g * 1024:(g + 1) * 1024]
                dve.wait_ge(sp_log, g + 1)
                step(dve.scalar_tensor_tensor(ph_a, z, 0.0, ph_l, ALU.min, ALU.subtract))
                dve.scalar_tensor_tensor(k, z, 0.0, ph_l, ALU.max, ALU.add).then_inc(sp_sum, 1)
                dve.wait_ge(sp_sum, g + 1)
                for h in range(4):
                    cols = slice(h * T, (h + 1) * T)
                    ins = dve.scalar_tensor_tensor(ph_a[:, cols], k[:, cols], loglb[:, 4 * g + h:4 * g + h + 1],
                                                   ph_a[:, cols], ALU.subtract, ALU.max, reverse0=True)
                ins.then_inc(floor_max, 1)

            def log_gates_b(g, p):
                z, k = zb[:, g * 1024:(g + 1) * 1024], hk[:, g * 1024:(g + 1) * 1024]
                dve.wait_ge(floor_max, g + 1)
                dve.wait_ge(kexp_ready, g + 1)
                for h in range(4):
                    cols = slice(h * T, (h + 1) * T)
                    step.note(dve.tensor_scalar(k[:, cols], k[:, cols], one_m_lb[:, 4 * g + h:4 * g + h + 1], None,
                                                ALU.mult))
                ahead(p)
                dve.wait_ge(rlog_ready, g + 1)
                dve.wait_ge(dve_steps, step.n)
                step(dve.tensor_tensor(ph_a, ph_a, ph_l, ALU.add))
                for u in range(8):
                    cols = slice(u * P, (u + 1) * P)
                    ins = dve.tensor_tensor_scan(z[:, cols], ones, ph_a[:, cols], 0.0, ALU.mult, ALU.add)
                ins.then_inc(b_ready, 1)

            def level_diff(g, l):
                m = BUF_LEVELS * g + l
                if m >= 2:
                    dve.wait_ge(kt_ready, m - 1)
                    dve.wait_ge(qt_ready, m - 1)
                half = HALVES[l]
                n = 1024 // (2 * half)
                b = zb[:, g * 1024:(g + 1) * 1024].rearrange("p (n s h) -> p n s h", s=2, h=half)
                e = lev_e[m % 2].rearrange("p (n s h) -> p n s h", s=2, h=half)
                ref = b[:, :, 0, half - 1:half].to_broadcast([P, n, half])
                dve.tensor_tensor(e[:, :, 0, :], ref, b[:, :, 0, :], ALU.subtract)
                dve.tensor_tensor(e[:, :, 1, :], b[:, :, 1, :], ref, ALU.subtract).then_inc(diff_ready, 1)

            def level_keys(g, l):
                m = BUF_LEVELS * g + l
                dve.wait_ge(exp_ready, m + 1)
                if l == len(HALVES):
                    dve.wait_ge(sc_done, 2 * (LEVELS * g + l - 1))
                elif g and l < 2:
                    dve.wait_ge(at_done, 4 * g)
                elif l >= 2:
                    dve.wait_ge(sc_done, 2 * (LEVELS * g + l - 1))
                k, e, dst = hk[:, g * 1024:(g + 1) * 1024], lev_e[m % 2], lev_k[m % 2]
                if 2 <= m and l < len(HALVES):
                    k, e, dst = (half_of(a, HALVES[l], 0) for a in (k, e, dst))
                dve.tensor_tensor(dst, k, e, ALU.mult).then_inc(kt_ready, 1)

            def level_select(g, l):
                c = LEVELS * g + l
                if l < len(HALVES):
                    dve.wait_ge(sc_done, 2 * c + 2)
                    if c:
                        dve.wait_ge(sc_sel, 2 * c)
                    if g and l == 0:
                        dve.wait_ge(at_done, 4 * g)
                    half = HALVES[l]
                    n = P // (2 * half)
                    mask = half_of(level_mask[:, l, :], half, 1).unsqueeze(1).to_broadcast([P, 8, n, half])
                    dst = scT.rearrange("p (u n s h) -> p u n s h", n=n, s=2, h=half)[:, :, :, 1, :]
                    src = bank(2 + 2 * (c % 2)).rearrange("p (u n h) -> p u n h", n=n, h=half)
                    dve.copy_predicated(dst, mask, src).then_inc(sc_sel, 2)
                    return
                for h in range(2):
                    dve.wait_ge(sc_done, 2 * c + h + 1)
                    dve.wait_ge(sc_sel, 2 * c + h)
                    mask = level_mask[:, l, :].unsqueeze(1).to_broadcast([P, 4, P])
                    dst = scT[:, h * N:(h + 1) * N].rearrange("p (u t) -> p u t", u=4)
                    src = bank(2 + 2 * (c % 2) + h).rearrange("p (u t) -> p u t", u=4)
                    dve.copy_predicated(dst, mask, src).then_inc(sc_sel, 1)

            ahead(10)
            log_gates_a(0)
            ahead(12)
            log_gates_b(0, 13)
            dve.wait_ge(mask_ready, 1)
            for g in range(2):
                dve.wait_ge(b_ready, g + 1)
                level_diff(g, 0)
                for l in range(len(HALVES) + 1):
                    if l + 1 < len(HALVES):
                        level_diff(g, l + 1)
                    ahead(14 + l if g == 0 else min(26 + l, P_HG_OUT))
                    level_keys(g, l)
                    if l >= 2:
                        level_select(g, l - 2)
                level_select(g, LEVELS - 2)
                if g == 0:
                    ahead(22)
                    log_gates_a(1)
                    ahead(24)
                level_select(g, LEVELS - 1)
                if g == 0:
                    log_gates_b(1, 24)
            ahead(P_HG_OUT + 2)
            def mean_square(t):
                dve.wait_ge(sq_ready, t + 1)
                step(dve.tensor_reduce(ssq[:, t, :], lev_e[t].rearrange("p (h e) -> p h e", h=HG_HEADS), AX_X, ALU.add))
                dve.tensor_scalar(ssq[:, t, :], ssq[:, t, :], 1.0 / P, RMS_EPS, ALU.mult, ALU.add)\
                   .then_inc(ms_ready, 1)

            def gated(t):
                dve.wait_ge(gn_ready, t + 1)
                dve.wait_ge(sq_ready, t + 1)
                step.note(dve.tensor_tensor(ho[:, t, :], ho[:, t, :], hg[:, t, :], ALU.mult))

            def rms_scaled(t):
                dve.wait_ge(rms_ready, t + 1)
                step(dve.reciprocal(ssq[:, t, :], ssq[:, t, :]))
                for half in range(2):
                    o = ho[:, t, half * N:(half + 1) * N].rearrange("p (h e) -> p h e", h=4)
                    dve.tensor_tensor(o, o, ssq[:, t, 4 * half:4 * half + 4].unsqueeze(2).to_broadcast([P, 4, P]),
                                      ALU.mult).then_inc(on_ready, 1)

            mean_square(0)
            gated(0)
            mean_square(1)
            gated(1)
            rms_scaled(0)
            rms_scaled(1)
            turned(1, 0)
            turned(1, 1)

            def statistics(r, t, n, steps):
                steps(dve.bn_stats(stats[:, t, n, :], r[:, t, n * N:(n + 1) * N]))

            def variance(t, steps):
                steps(dve.bn_aggr(mv[:, t, :], stats[:, t, :, :].rearrange("p n s -> p (n s)")))
                dve.tensor_scalar(mv[:, t, 1:2], mv[:, t, 1:2], LN_EPS, None, ALU.add).then_inc(ln_var, 1)

            def normalise(k, t, r, gain, bias, steps):
                dve.wait_ge(ln_std, TB * k + t + 1)
                steps(dve.reciprocal(std[:, t:t + 1], std[:, t:t + 1]))
                dve.wait_ge(gb_loaded, 32 * (k + 1))
                for n in range(2):
                    cols = slice(n * N, (n + 1) * N)
                    steps(dve.scalar_tensor_tensor(r[:, t, cols], r[:, t, cols], mv[:, t, 0:1], gain[:, cols],
                                                   ALU.subtract, ALU.mult))
                    dve.scalar_tensor_tensor(r[:, t, cols], r[:, t, cols], std[:, t:t + 1], bias[:, cols],
                                             ALU.mult, ALU.add).then_inc(x_ready, 1)

            def residual(k, last, stage):
                def add(t, n):
                    cols = slice(n * N, (n + 1) * N)
                    step(dve.scalar_tensor_tensor(xres[:, t, cols], xres[:, t, cols], ALPHA,
                                                  bank(2 + 2 * n + t), ALU.mult, ALU.add))
                    statistics(xres, t, n, step)

                if k == 1:
                    ahead(last)
                    dve.wait_ge(y_first, k + 1)
                    add(0, 0)
                else:
                    wait_piece(last - 4)
                    add(0, 0)
                    add(1, 0)
                    ahead(last)
                    dve.wait_ge(y_first, k + 1)
                add(0, 1)
                variance(0, step)
                ahead(last + 1)
                normalise(k, 0, xres, gb[:, 0, :], gb[:, 1, :], step)
                dve.wait_ge(pieces_used, last)
                if k == 1:
                    add(1, 0)
                add(1, 1)
                variance(1, step)
                turned(stage, 0)
                normalise(k, 1, xres, gb[:, 0, :], gb[:, 1, :], step)
                turned(stage, 1)
                ahead(last + 4)

            residual(0, P_GU, 2)
            dve.wait_ge(small_hi, 1)
            dve.tensor_tensor(wsl, w_small, wsh.bitcast(F32), ALU.subtract).then_inc(small_lo, 1)

            def h_low(f):
                dve.wait_ge(ffn_hi, f + 1)
                dve.tensor_tensor(hTl[:, f, :], ffn_p[f % 2], hTh[:, f, :].bitcast(F32), ALU.subtract)\
                   .then_inc(ffn_h, 1)

            for f in range(FFN_TILES):
                wait_piece(P_GU + 2 * f + 2)
                dve.wait_ge(ffn_silu, f + 1)
                if f >= 2:
                    dve.wait_ge(ffn_h, f - 1)
                dve.tensor_tensor(ffn_p[f % 2], ffn_s[f % 2], ps[:, f % 2, T:2 * T], ALU.mult).then_inc(ffn_prod, 1)
                if f:
                    h_low(f - 1)
            h_low(FFN_TILES - 1)
            residual(1, P_KVQG, 3)

            dve.wait_ge(f_log, 1)
            step(dve.scalar_tensor_tensor(fl, fz, 0.0, fl, ALU.min, ALU.subtract))
            dve.tensor_tensor_scan(fc, sq[0:FOX_HEADS, P:P + 1].to_broadcast([FOX_HEADS, T]), fl, 0.0,
                                   ALU.mult, ALU.add).then_inc(c_ready, 1)
            wait_piece(P_KVQG + 20)
            dve.wait_ge(cT_done, 1)
            dve.tensor_copy(A[:, 13792:13824], ps[:, 6, 0:32]).then_inc(cT_ready, 1)
            dve.wait_ge(cT_ready, 1)
            dve.wait_ge(fox_loaded, 32)

            def fox_max(h):
                dve.wait_ge(fx_qk, h + 1)
                if h >= 2:
                    dve.wait_ge(fx_exp, h - 1)
                for t in range(TB):
                    cols = slice(0, P) if t == 0 else slice(P, KW)
                    step.note(dve.scalar_tensor_tensor(flog[h % 2][:, cols], ps[:, 2 + h % 2, cols],
                                                       cT[:, t, h:h + 1], causal[:, cols], ALU.add, ALU.add))
                for t in range(TB):
                    cols = slice(0, P) if t == 0 else slice(P, KW)
                    dve.wait_ge(dve_steps, step.n - 1 + t)
                    ins = dve.tensor_reduce(nmax[:, 2 * h + t:2 * h + t + 1], flog[h % 2][:, cols], AX_X, ALU.max,
                                            negate=True)
                ins.then_inc(fx_max, 1)

            def fox_norm(h):
                dve.wait_ge(fx_pv, h + 1)
                step(dve.reciprocal(rinv[:, 2 * h:2 * h + 2], rsum[:, 2 * h:2 * h + 2]))
                dve.tensor_tensor(fo[:, :, h * FOX_DIM:(h + 1) * FOX_DIM],
                                  bank(6 + h % 2, 2 * FOX_DIM).rearrange("p (t e) -> p t e", t=TB),
                                  rinv[:, 2 * h:2 * h + 2].unsqueeze(2).to_broadcast([P, TB, FOX_DIM]),
                                  ALU.mult).then_inc(fx_out, 1)

            for h in range(FOX_HEADS + 2):
                if h <= 12:
                    ahead(P_KVQG + 20 + h + BUFS)
                if h < FOX_HEADS:
                    fox_max(h)
                if h >= 2:
                    fox_norm(h - 2)
            dve.wait_ge(fx_out, FOX_HEADS)
            for t in range(TB):
                dve.wait_ge(fg_sig, t + 1)
                dve.tensor_tensor(fo[:, t, :], fo[:, t, :], fg[:, t, :], ALU.mult).then_inc(og_ready, 1)
            turned(4, 0)
            turned(4, 1)
            residual(2, P_MOE, 5)

            for t in range(TB):
                dve.wait_ge(x_ready, 8 + 2 * t + 2)
                dve.tensor_scalar(yacc[:, t, :], xres[:, t, :], ALPHA, None, ALU.mult).then_inc(yacc_up, 1)

            def by_token(a):
                return a.rearrange("p (t e) -> p t e", t=TB)

            def spread_e(a):
                return a.unsqueeze(2).to_broadcast([P, TB, E])

            w8b = w8.unsqueeze(1).to_broadcast([P, TB, E])
            lg, eq, f1, lg2, f2, tmp = rt[0], rt[1], rt[2], rt[3], rt[4], rt[5]
            m1, m2, kmax, w1, w2 = (rt[6][:, 0:2], rt[6][:, 2:4], rt[6][:, 4:6], rt[6][:, 6:8], rt[6][:, 8:10])
            comb, sel = rt[7], rt[8]
            dve.wait_ge(yacc_up, TB)
            for t in range(TB):
                dve.wait_ge(x3_hi, t + 1)
                dve.tensor_tensor(x3l[:, t, :], xres[:, t, :], x3h[:, t, :].bitcast(F32), ALU.subtract)\
                   .then_inc(x3_ready, 1)
            dve.wait_ge(lg_done, 1)
            step(dve.tensor_copy(lg, ps[:, 6, 0:2 * E]))

            def rows_lo(i, half):
                dve.wait_ge(xe_hi, 2 * i + half + 1)
                rows = slice(4 * half, 4 * half + 4)
                dve.tensor_tensor(xel[:, rows, :], bank(7 - half).rearrange("p (k t) -> p k t", k=4),
                                  xeh[:, rows, :].bitcast(F32), ALU.subtract).then_inc(xe_ready, 1)

            def first_largest(values, m, first):
                step(dve.tensor_reduce(m, by_token(values), AX_X, ALU.max))
                step(dve.tensor_tensor(by_token(eq), by_token(values), spread_e(m), ALU.is_ge))
                step(dve.tensor_tensor(by_token(eq), by_token(eq), w8b, ALU.mult))
                step(dve.tensor_reduce(kmax, by_token(eq), AX_X, ALU.max))
                step(dve.tensor_tensor(by_token(first), by_token(eq), spread_e(kmax), ALU.is_ge))

            first_largest(lg, m1, f1)
            step(dve.scalar_tensor_tensor(lg2, f1, MASKED, lg, ALU.mult, ALU.add))
            first_largest(lg2, m2, f2)
            dve.tensor_tensor(rt[9][:, 2:4], m2, m1, ALU.subtract).then_inc(e2_in, 1)
            dve.tensor_tensor(sel, f1, f2, ALU.add).then_inc(sel_ready, 1)
            dve.wait_ge(sel_ready, 1)
            step(dve.tensor_scalar(tmp, sel, -NOT_CHOSEN, NOT_CHOSEN, ALU.mult, ALU.add))
            dve.wait_ge(rk_done, 1)
            step(dve.tensor_tensor(rank2[:, :, 0:E], by_token(ps[:, 1, 0:2 * E]), by_token(tmp), ALU.add))
            PICK_STEPS = 2

            def choose(col, steps):
                steps(dve.tensor_copy(cur[:, 0:2], rank2[:, :, bass.ds(col, 1)].squeeze(2)))
                steps.note(dve.tensor_scalar(pick[:, 0, :], iota, cur[:, 0:1], None, ALU.is_equal))
                dve.tensor_scalar(pick[:, 1, :], iota, cur[:, 1:2], None, ALU.is_equal).then_inc(pick_ready, 1)

            def take_weights(col):
                dve.tensor_copy(cur[:, 2:4], comb2[:, :, bass.ds(col, 1)].squeeze(2)).then_inc(weights_ready, 1)

            picks = Steps(dve, dve_item, 0)
            choose(0, picks)
            dve.wait_ge(e2_out, 1)
            step(dve.tensor_scalar(w1, rt[9][:, 0:2], 1.0, None, ALU.add))
            step(dve.reciprocal(w1, w1))
            step(dve.tensor_tensor(w2, w1, rt[9][:, 0:2], ALU.mult))
            step.note(dve.tensor_tensor(by_token(rt[10]), by_token(f1), spread_e(w1), ALU.mult))
            step(dve.tensor_tensor(by_token(comb), by_token(f2), spread_e(w2), ALU.mult))
            step(dve.tensor_tensor(comb, comb, rt[10], ALU.add))
            step.note(dve.tensor_scalar(rank2[:, :, E:2 * E], rank2[:, :, 0:E], -float(P), None, ALU.add))
            step.note(dve.tensor_copy(comb2[:, :, 0:E], by_token(comb)))
            step(dve.tensor_copy(comb2[:, :, E:2 * E], by_token(comb)))
            take_weights(0)
            rows_lo(0, 0)
            over, mx, cols_f = itf[:, 0:8], itf[:, 8:16], itf[:, 16:32]
            step(dve.tensor_scalar(over, ps[0:1, 1, 2 * E:3 * E], float(P), None, ALU.is_gt))
            step(dve.tensor_reduce(itf[:, 32:33], over, AX_X, ALU.add))
            step(dve.tensor_tensor(over, over, w8[0:1, :], ALU.mult))
            step(dve.max(mx, over))
            step(dve.tensor_scalar(cols_f[:, 0:8], w8[0:1, :], -1.0, float(E), ALU.mult, ALU.add))
            step(dve.tensor_scalar(cols_f[:, 8:16], mx, -1.0, 2.0 * E, ALU.mult, ALU.add))
            step(dve.tensor_scalar(cols_f[:, 8:16], cols_f[:, 8:16], 2.0 * E - 1, None, ALU.min))
            dve.tensor_copy(items[:, 0:16], cols_f).then_inc(items_ready, 1)
            dve.tensor_copy(items[:, 16:17], itf[:, 32:33]).then_inc(items_ready, 1)
            dve.wait_ge(items_ready, 2)
            rows_lo(0, 1)

            def lo(i, piece):
                i, piece = i + piece // MOE_PIECES, piece % MOE_PIECES
                b = (P_MOE + piece) % BUFS
                dve.wait_ge(hi_ready, P_MOE + i * MOE_PIECES + piece + 1)
                dve.tensor_tensor(wl[b][:, :], moe_piece_src(piece), wh[b][:, :].bitcast(F32),
                                  ALU.subtract).then_inc(lo_ready, 1)

            def hT_low(i, c):
                dve.wait_ge(hT_hi, i * CH + c + 1)
                dve.tensor_tensor(ehTl[:, :], bank(6), ehTh[:, :].bitcast(F32), ALU.subtract).then_inc(hT_ready, 1)

            def add_outputs(i, n):
                for t in range(TB):
                    dve.wait_ge(sc2_done, 4 * i + 2 * n + t + 1)
                    if n == 0:
                        dve.wait_ge(yacc_up, 4 * i + 1 + t)
                    cols = slice(n * N, (n + 1) * N)
                    dve.tensor_tensor(yacc[:, t, cols], yacc[:, t, cols], bank([7, 6, 2, 3][2 * n + t]), ALU.add)\
                       .then_inc(yacc_up, 1)

            def item(i, first, last):
                done = first
                for c in range(CH):
                    if c:
                        for piece in range(done, moe_end("a", c) + BUFS - 1):
                            lo(i, piece)
                        hT_low(i, c - 1)
                        done = moe_end("a", c) + BUFS - 1
                    b_end = moe_end("b", c)
                    for piece in range(done, b_end + BUFS):
                        lo(i, piece)
                    done = b_end + BUFS
                    dve.wait_ge(pieces_used, P_MOE + i * MOE_PIECES + b_end)
                    dve.wait_ge(silu_done, i * CH + c + 1)
                    dve.tensor_tensor(eh, gate_s, bank(2 * (c % 2) + 1), ALU.mult).then_inc(h_ready, 1)
                    if c == 0:
                        dve.wait_ge(spr_done, i + 1)
                        dve.tensor_copy(slot_weight, ps[:, 6, 2 * P:2 * P + 1])
                        dve.tensor_copy(spread_all, ps[:, 6, 0:2 * P]).then_inc(spr_ready, 1)
                    if c == 1:
                        col = dve.value_load(items[0:1, bass.ds(i + 1, 1)], min_val=0, max_val=2 * E - 1)
                        steps = Steps(dve, dve_item, i * PICK_STEPS + PICK_STEPS)
                        choose(col, steps)
                        take_weights(col)
                for piece in range(done, MOE_PIECES - 1):
                    lo(i, piece)
                hT_low(i, CH - 1)
                lo(i, MOE_PIECES - 1)
                rows_lo(i + 1, 0)
                for piece in range(MOE_PIECES, last - 2):
                    lo(i, piece)
                for n in range(2):
                    dve.wait_ge(spr_ready, i + 1)
                    dve.wait_ge(ye_hi, 2 * i + n + 1)
                    dve.scalar_tensor_tensor(yel[n], bank(4 + n), slot_weight, yeh[:, n, :].bitcast(F32),
                                             ALU.mult, ALU.subtract).then_inc(ye_ready, 1)
                rows_lo(i + 1, 1)
                if last > MOE_PIECES:
                    lo(i, last - 2)
                add_outputs(i, 0)
                if last > MOE_PIECES:
                    lo(i, last - 1)
                add_outputs(i, 1)

            with dve.Fori(0, E - 1) as i:
                item(i, BUFS, MOE_PIECES + BUFS)
            item(E - 1, BUFS, MOE_PIECES)
            more = dve.value_load(items[0:1, 16:17], min_val=0, max_val=3)
            with dve.If(more > 0):
                with dve.Fori(0, more) as n:
                    item(n + E, 0, MOE_PIECES)
            dve.wait_ge(yacc_up, (more + E) * 4 + 2)
            tail = Steps(dve, dve_tail)
            for t in range(TB):
                for n in range(2):
                    statistics(yacc, t, n, tail)
            for t in range(TB):
                variance(t, tail)
            for t in range(TB):
                normalise(3, t, yacc, last_gain, last_bias, tail)

        @block.gpsimd
        def _(pool):
            pool.wait_ge(levels_loaded, 16)
            pool.tensor_copy(level_mask.rearrange("p l n -> p (l n)"), lev_k[0]).then_inc(mask_ready, 1)
            for g in range(2):
                pool.wait_ge(q_ready, g + 1)
                for l in range(BUF_LEVELS):
                    m = BUF_LEVELS * g + l
                    pool.wait_ge(exp_ready, m + 1)
                    if g and l < 2:
                        pool.wait_ge(at_done, 4 * g)
                    elif l >= 2:
                        pool.wait_ge(sc_done, 2 * (LEVELS * g + l - 1))
                    q, e, dst = hq[:, g * 1024:(g + 1) * 1024], lev_e[m % 2], lev_q[m % 2]
                    if l < len(HALVES):
                        q, e, dst = (half_of(a, HALVES[l], 1) for a in (q, e, dst))
                    pool.tensor_tensor(dst, q, e, ALU.mult).then_inc(qt_ready, 1)
            pool.dma_start(normw, norm_w[0:1, :].to_broadcast([P, P])).then_inc(normw_loaded, 16)
            pool.wait_ge(normw_loaded, 16)
            pool.wait_ge(hg_silu, 1)
            for t in range(TB):
                g3 = hg[:, t, :].rearrange("p (h e) -> p h e", h=HG_HEADS)
                pool.tensor_tensor(g3, g3, normw.unsqueeze(1).to_broadcast([P, HG_HEADS, P]), ALU.mult)\
                    .then_inc(gn_ready, 1)

            def load_ln(gains, biases, layer, gain, bias):
                pool.dma_start(gain, gains[layer:layer + 1, :].to_broadcast([P, D])).then_inc(gb_loaded, 16)
                pool.dma_start(bias, biases[layer:layer + 1, :].to_broadcast([P, D])).then_inc(gb_loaded, 16)

            pool.wait_ge(tp_done, 8)
            load_ln(ln_mix_g, ln_mix_b, 0, gb[:, 0, :], gb[:, 1, :])
            pool.dma_start(negsel, c_negsel).then_inc(fox_loaded, 16)
            pool.dma_start(causal, c_causal).then_inc(fox_loaded, 16)
            pool.dma_start(iota, c_route[:, 0:P]).then_inc(route_loaded, 16)
            pool.dma_start(before, c_route[:, P:2 * P]).then_inc(route_loaded, 16)
            pool.dma_start(w8, c_route[:, 2 * P:2 * P + E]).then_inc(route_loaded, 16)
            pool.dma_start(router_part(w_small), router_w[0].rearrange("(k p) n -> p k n", p=P))\
                .then_inc(route_loaded, 16)
            pool.dma_start(fgate_part(w_small), kv_v[:, :, 2 * D:2 * D + FOX_HEADS]).then_inc(route_loaded, 16)
            pool.wait_ge(x_ready, 4)
            load_ln(ln_ffn_g, ln_ffn_b, 0, gb[:, 0, :], gb[:, 1, :])
            pool.wait_ge(x_ready, 8)
            load_ln(ln_mix_g, ln_mix_b, 1, gb[:, 0, :], gb[:, 1, :])
            pool.wait_ge(rk_done, 1)
            load_ln(ln_ffn_g, ln_ffn_b, 1, last_gain, last_bias)


_INS = ["x", "hg_w_in", "hg_lb_logits", "hg_norm_w", "hg_w_out", "kv_w", "kv_fgate_b", "fox_w_qg", "fox_w_out",
        "ln_mix_g", "ln_mix_b", "ln_ffn_g", "ln_ffn_b", "ffn_w_gu", "ffn_w_down", "moe_w_router", "moe_w_gu",
        "moe_w_down"]


def _constants():
    import numpy as np

    r = np.arange(P)
    square = np.concatenate([np.eye(P), np.ones((P, P))], axis=1).astype(np.float32)
    levels = []
    for half in HALVES:
        same = (r[:, None] // (2 * half)) == (r[None, :] // (2 * half))
        levels.append(same & ((r[:, None] // half) % 2 == 0) & ((r[None, :] // half) % 2 == 1))
    levels.append(r[:, None] == r[None, :])
    levels = np.concatenate(levels, axis=1).astype(np.float32)
    negsel = -np.eye(FOX_HEADS).astype(np.float32)
    causal = np.concatenate([np.where(r[None, :] <= r[:, None], 0.0, MASKED), np.zeros((P, P)),
                             np.where(r[None, :] <= r[:, None], 0.0, MASKED)], axis=1).astype(np.float32)
    route = np.concatenate([np.broadcast_to(r, (P, P)), r[:, None] < r[None, :],
                            np.broadcast_to(E - np.arange(E), (P, E))], axis=1).astype(np.float32)
    return {"c_square": square, "c_levels": levels, "c_negsel": negsel, "c_causal": causal, "c_route": route}


def kernel(**inputs):
    import numpy as _np
    import concourse.bacc as _bacc
    from concourse import mybir as _mybir
    from concourse.bass_utils import run_bass_kernel_spmd as _run

    nc = _bacc.Bacc("TRN2", target_bir_lowering=False, num_devices=1)
    arrays, args = {}, []
    given = {name: _np.ascontiguousarray(inputs[name]) for name in _INS}
    for name, a in {**given, **_constants()}.items():
        arrays[f"in_{name}_dram"] = a
        args.append(nc.dram_tensor(f"in_{name}_dram", a.shape, _mybir.dt.from_np(a.dtype), kind="ExternalInput").ap())
    args.append(nc.dram_tensor("out_dram", (1, T, D), F32, kind="ExternalOutput").ap())
    build(nc, *args)
    r = _run(nc, [arrays], core_ids=[0])
    return r.results[0]["out_dram"]
```
